# Optimizing a Trainium2 kernel written in Bass

```python
import math
import jax, jax.numpy as jnp
from jax import lax
import numpy as np

D_MODEL = 1024
BATCH = 1
SEQ = 512
DEPTH = 2

N_META = 16
BLOCK = 128
A_HEADS = 8
A_HEAD_DIM = 64
IDX_HEADS = 8
IDX_DIM = 64
TOPK_MAX = 256
N_BUCKETS = 32
MAX_DISTANCE = 128
B_HEADS = 4
B_QK_DIM = 128
B_V_DIM = 256
ROPE_BASE = 10000.0
C_HEADS = 16
C_HEAD_DIM = 64
D_FF = 2816
CONV_WIDTH = 3
EPS = 1e-6

A_Q = A_HEADS * A_HEAD_DIM
A_IQ = IDX_HEADS * IDX_DIM
B_QK = B_HEADS * B_QK_DIM
B_V = B_HEADS * B_V_DIM
EVEN_SPLITS = [A_Q, A_Q, A_Q, A_IQ, IDX_DIM, IDX_HEADS, B_QK, B_QK, B_V, B_V]
EVEN_IN = sum(EVEN_SPLITS)
EVEN_OUT = A_Q + B_V
C_W = C_HEADS * C_HEAD_DIM
ODD_IN = 3 * C_W


def rmsnorm(x, g):
    xf = x.astype(jnp.float32)
    y = xf * lax.rsqrt(jnp.mean(jnp.square(xf), axis=-1, keepdims=True) + EPS)
    return (y * g.astype(jnp.float32)).astype(x.dtype)

def t5_bucket(rel):
    n = jnp.maximum(rel, 0)
    max_exact = N_BUCKETS // 2
    large = max_exact + (jnp.log(jnp.maximum(n, 1).astype(jnp.float32) / max_exact)
                         / math.log(MAX_DISTANCE / max_exact)
                         * (N_BUCKETS - max_exact)).astype(jnp.int32)
    large = jnp.minimum(large, N_BUCKETS - 1)
    return jnp.where(n < max_exact, n, large)

def rotary(x, pos):
    half = x.shape[-1] // 2
    inv = 1.0 / (ROPE_BASE ** (jnp.arange(half, dtype=jnp.float32) / half))
    ang = pos.astype(jnp.float32)[:, None] * inv[None, :]
    cos = jnp.cos(ang)[:, None, :]
    sin = jnp.sin(ang)[:, None, :]
    xf = x.astype(jnp.float32)
    x1, x2 = xf[..., :half], xf[..., half:]
    return jnp.concatenate([x1 * cos - x2 * sin, x2 * cos + x1 * sin], axis=-1).astype(x.dtype)

def dsa_attention(q, k, v, qi, ki, wi, rel_bias, n_keep):
    Bsz, L = q.shape[:2]
    nblk = L // BLOCK
    kpos = jnp.arange(L)
    is_meta = kpos < N_META

    def block(args):
        qb, qib, wib, qpos = args
        s = jnp.einsum('bqhd,bkd->bqhk', qib, ki).astype(jnp.float32) * (IDX_DIM ** -0.5)
        score = jnp.einsum('bqhk,bqh->bqk', jax.nn.relu(s), wib.astype(jnp.float32))
        causal = kpos[None, :] <= qpos[:, None]
        score = jnp.where(causal[None], jnp.where(is_meta[None, None, :], jnp.inf, score), -jnp.inf)
        _, idx = lax.top_k(score, n_keep)
        gather = jax.vmap(lambda a, i: a[i])
        ksel = gather(k, idx)
        vsel = gather(v, idx)
        rel = qpos[None, :, None] - idx
        bias = jnp.moveaxis(rel_bias[t5_bucket(rel)], -1, 2)
        logits = jnp.einsum('bqhd,bqkhd->bqhk', qb, ksel).astype(jnp.float32) * (A_HEAD_DIM ** -0.5)
        logits = logits + bias.astype(jnp.float32)
        logits = jnp.where((rel >= 0)[:, :, None, :], logits, -jnp.inf)
        p = jax.nn.softmax(logits, axis=-1).astype(v.dtype)
        return jnp.einsum('bqhk,bqkhd->bqhd', p, vsel)

    to_blocks = lambda a: jnp.moveaxis(a.reshape(Bsz, nblk, BLOCK, *a.shape[2:]), 1, 0)
    out = lax.map(block, (to_blocks(q), to_blocks(qi), to_blocks(wi), kpos.reshape(nblk, BLOCK)))
    return jnp.moveaxis(out, 0, 1).reshape(Bsz, L, *q.shape[2:])

def retention(q, k, v):
    Bsz, L, H, dk = q.shape
    dv = v.shape[-1]
    C = BLOCK
    N = L // C
    lg = jnp.log(1.0 - 2.0 ** (-5.0 - jnp.arange(H, dtype=jnp.float32)))
    n = jnp.arange(C, dtype=jnp.float32)
    diff = n[:, None] - n[None, :]
    dmat = jnp.where(diff[None] >= 0, jnp.exp(jnp.maximum(diff, 0.0)[None] * lg[:, None, None]), 0.0)
    xi = jnp.exp((n[None, :] + 1.0) * lg[:, None])[..., None]
    zeta = jnp.exp((C - 1.0 - n[None, :]) * lg[:, None])[..., None]
    g_chunk = jnp.exp(C * lg)[:, None, None]
    chunks = lambda a: a.astype(jnp.float32).reshape(Bsz, N, C, H, a.shape[-1]).transpose(1, 0, 3, 2, 4)
    qc, kc, vc = chunks(q), chunks(k * (dk ** -0.5)), chunks(v)

    def step(R, inp):
        qi, ki, vi = inp
        inner = jnp.einsum('bhcd,bhed->bhce', qi, ki) * dmat
        o = jnp.einsum('bhce,bhef->bhcf', inner, vi) + jnp.einsum('bhcd,bhdf->bhcf', qi, R) * xi
        R = R * g_chunk + jnp.einsum('bhcd,bhcf->bhdf', ki * zeta, vi)
        return R, o

    R0 = jnp.zeros((Bsz, H, dk, dv), jnp.float32)
    _, o = lax.scan(step, R0, (qc, kc, vc))
    return o.transpose(1, 0, 3, 2, 4).reshape(Bsz, L, H, dv)

def stick_breaking(q, k, v):
    L = q.shape[1]
    scale = q.shape[-1] ** -0.5
    outs = []
    for i in range(L // BLOCK):
        s, e = i * BLOCK, (i + 1) * BLOCK
        z = jnp.einsum('bqhd,bkhd->bhqk', q[:, s:e], k[:, :e]).astype(jnp.float32) * scale
        mask = (jnp.arange(e)[None, :] < jnp.arange(s, e)[:, None])[None, None]
        log_1m = jnp.where(mask, jax.nn.log_sigmoid(-z), 0.0)
        rest = lax.cumsum(log_1m, axis=3, reverse=True) - log_1m
        a = jnp.where(mask, jnp.exp(jax.nn.log_sigmoid(z) + rest), 0.0)
        outs.append(jnp.einsum('bhqk,bkhd->bqhd', a.astype(v.dtype), v[:, :e]))
    return jnp.concatenate(outs, axis=1)

def even_mixer(h, w_in, gn_gain, w_out, rel_bias, n_keep):
    Bsz, L, _ = h.shape
    p = h @ w_in
    splits = [int(s) for s in np.cumsum(EVEN_SPLITS)[:-1]]
    aq, ak, av, iq, ik, iw, bq, bk, bv, bg = jnp.split(p, splits, axis=-1)
    heads = lambda t, nh: t.reshape(Bsz, L, nh, -1)
    a_out = dsa_attention(heads(aq, A_HEADS), heads(ak, A_HEADS), heads(av, A_HEADS),
                          heads(iq, IDX_HEADS), ik, iw * (IDX_HEADS ** -0.5), rel_bias, n_keep)
    a_out = a_out.reshape(Bsz, L, A_Q)
    pos = jnp.arange(L)
    bq = rotary(heads(bq, B_HEADS), pos)
    bk = rotary(heads(bk, B_HEADS), pos)
    lead = (-N_META) % BLOCK
    frame = lambda t: jnp.pad(t[:, :L - lead], ((0, 0), (lead, 0), (0, 0), (0, 0)))
    r = retention(frame(bq), frame(bk), frame(heads(bv, B_HEADS)))
    r = jnp.pad(r[:, lead:], ((0, 0), (0, lead), (0, 0), (0, 0)))
    mu = jnp.mean(r, axis=-1, keepdims=True)
    var = jnp.mean(jnp.square(r - mu), axis=-1, keepdims=True)
    r = ((r - mu) * lax.rsqrt(var + EPS)).reshape(Bsz, L, B_V) * gn_gain.astype(jnp.float32)
    r_out = (r * jax.nn.silu(bg.astype(jnp.float32))).astype(h.dtype)
    return jnp.concatenate([a_out, r_out], axis=-1) @ w_out

def odd_mixer(h, w_in, w_out):
    Bsz, L, _ = h.shape
    q, k, v = jnp.split(h @ w_in, 3, axis=-1)
    heads = lambda t: t.reshape(Bsz, L, C_HEADS, C_HEAD_DIM)
    return stick_breaking(heads(q), heads(k), heads(v)).reshape(Bsz, L, C_W) @ w_out

def conv_ffn(h, w_up, w_gate, conv_w, conv_b, w_down):
    u = h @ w_up
    g = h @ w_gate
    g = lax.conv_general_dilated(g, conv_w[:, None, :].astype(g.dtype), window_strides=(1,),
                                 padding=[(CONV_WIDTH - 1, 0)],
                                 dimension_numbers=('NWC', 'WIO', 'NWC'),
                                 feature_group_count=D_FF) + conv_b
    return (jax.nn.silu(g) * u) @ w_down

def first_inputs(seed: int = 0) -> dict:
    key = jax.random.key(seed)
    ks = jax.random.split(key, 20)
    f32 = jnp.float32
    ne, no = (DEPTH + 1) // 2, DEPTH // 2
    nrm = lambda k, shape, fan_in: jax.random.normal(k, shape, f32) * (fan_in ** -0.5)
    gain = lambda k, shape: 1.0 + 0.05 * jax.random.normal(k, shape, f32)
    return {
        "x": jax.random.normal(ks[0], (BATCH, SEQ, D_MODEL), f32),
        "meta_tokens": jax.random.normal(ks[1], (N_META, D_MODEL), f32),
        "rel_bias": 0.5 * jax.random.normal(ks[2], (N_BUCKETS, A_HEADS), f32),
        "norm_mix": gain(ks[3], (DEPTH, D_MODEL)),
        "norm_ffn": gain(ks[4], (DEPTH, D_MODEL)),
        "norm_final": gain(ks[5], (D_MODEL,)),
        "even_w_in": nrm(ks[6], (ne, D_MODEL, EVEN_IN), D_MODEL),
        "even_gn_gain": gain(ks[7], (ne, B_V)),
        "even_w_out": nrm(ks[8], (ne, EVEN_OUT, D_MODEL), EVEN_OUT),
        "odd_w_in": nrm(ks[9], (no, D_MODEL, ODD_IN), D_MODEL),
        "odd_w_out": nrm(ks[10], (no, C_W, D_MODEL), C_W),
        "ffn_w_up": nrm(ks[11], (DEPTH, D_MODEL, D_FF), D_MODEL),
        "ffn_w_gate": nrm(ks[12], (DEPTH, D_MODEL, D_FF), D_MODEL),
        "ffn_conv_w": nrm(ks[13], (DEPTH, CONV_WIDTH, D_FF), CONV_WIDTH),
        "ffn_conv_b": 0.01 * jax.random.normal(ks[14], (DEPTH, D_FF), f32),
        "ffn_w_down": nrm(ks[15], (DEPTH, D_FF, D_MODEL), D_FF),
    }

def first_block(x, meta_tokens, rel_bias, norm_mix, norm_ffn, norm_final,
              even_w_in, even_gn_gain, even_w_out, odd_w_in, odd_w_out,
              ffn_w_up, ffn_w_gate, ffn_conv_w, ffn_conv_b, ffn_w_down):
    Bsz, S, D = x.shape
    lead = (-N_META) % BLOCK
    n_keep = min(TOPK_MAX, S // 4)
    meta = jnp.broadcast_to(meta_tokens[None].astype(x.dtype), (Bsz, N_META, D))
    h = jnp.concatenate([meta, x, jnp.zeros((Bsz, lead, D), x.dtype)], axis=1)
    for l in range(DEPTH):
        hn = rmsnorm(h, norm_mix[l])
        if l % 2 == 0:
            j = l // 2
            h = h + even_mixer(hn, even_w_in[j], even_gn_gain[j], even_w_out[j], rel_bias, n_keep)
        else:
            j = l // 2
            h = h + odd_mixer(hn, odd_w_in[j], odd_w_out[j])
        h = h + conv_ffn(rmsnorm(h, norm_ffn[l]), ffn_w_up[l], ffn_w_gate[l],
                         ffn_conv_w[l], ffn_conv_b[l], ffn_w_down[l])
    return rmsnorm(h, norm_final)[:, N_META:N_META + S]


DEPTH_2 = 1

HEAD_DIM = 64
FOX_HEADS = 4
FOX_W = FOX_HEADS * HEAD_DIM
CONV_W = 256
CONV_K = 3
MLSTM_HEADS = 4
MLSTM_W = MLSTM_HEADS * HEAD_DIM
MLSTM_CHUNK = 64
SWA_Q_HEADS = 8
SWA_KV_HEADS = 2
SWA_W = SWA_Q_HEADS * HEAD_DIM
SWA_KV_W = SWA_KV_HEADS * HEAD_DIM
WINDOW = 128
Q_BLOCK = 128
REL_BUCKETS = 32
REL_MAX_DIST = 128
N_BRANCH = 4
D_FF_2 = -(-8 * D_MODEL // (3 * 256)) * 256

SPLIT_SIZES = (FOX_W, FOX_W, FOX_W, FOX_HEADS,
               CONV_W, CONV_W, CONV_W,
               MLSTM_W, MLSTM_W, MLSTM_W, MLSTM_HEADS, MLSTM_HEADS, MLSTM_W,
               SWA_W, SWA_KV_W, SWA_KV_W,
               N_BRANCH * D_MODEL)
IN_COLS = sum(SPLIT_SIZES)


def rms_norm(x, gain):
    xf = x.astype(jnp.float32)
    y = xf * lax.rsqrt(jnp.mean(xf * xf, axis=-1, keepdims=True) + EPS)
    return (y * gain.astype(jnp.float32)).astype(x.dtype)

def t5_bucket_2(n):
    max_exact = REL_BUCKETS // 2
    nf = jnp.maximum(n, 1).astype(jnp.float32)
    large = max_exact + (jnp.log(nf / max_exact) / math.log(REL_MAX_DIST / max_exact)
                         * (REL_BUCKETS - max_exact)).astype(jnp.int32)
    large = jnp.minimum(large, REL_BUCKETS - 1)
    return jnp.where(n < max_exact, n, large)

def fox_attention(q, k, v, f_logit):
    B, S, H, d = q.shape
    nblk = S // Q_BLOCK
    c = jnp.cumsum(jax.nn.log_sigmoid(f_logit.astype(jnp.float32)), axis=1)
    c_t = c.transpose(0, 2, 1)
    qb = q.reshape(B, nblk, Q_BLOCK, H, d).transpose(1, 0, 2, 3, 4)
    cb = c.reshape(B, nblk, Q_BLOCK, H).transpose(1, 0, 3, 2)
    key_pos = jnp.arange(S)
    scale = d ** -0.5

    def block(args):
        qi, ci, bi = args
        s = jnp.einsum('bqhd,bkhd->bhqk', qi, k).astype(jnp.float32) * scale
        s = s + (ci[..., :, None] - c_t[..., None, :])
        q_pos = bi * Q_BLOCK + jnp.arange(Q_BLOCK)
        s = jnp.where(key_pos[None, :] <= q_pos[:, None], s, -jnp.inf)
        p = jax.nn.softmax(s, axis=-1).astype(v.dtype)
        return jnp.einsum('bhqk,bkhd->bqhd', p, v)

    out = lax.map(block, (qb, cb, jnp.arange(nblk)))
    return out.transpose(1, 0, 2, 3, 4).reshape(B, S, H * d)

def short_conv_mixer(u, b_gate, c_gate, w):
    z = c_gate * u
    y = lax.conv_general_dilated(z, w[:, None, :], window_strides=(1,),
                                 padding=[(CONV_K - 1, 0)],
                                 dimension_numbers=('NWC', 'WIO', 'NWC'),
                                 feature_group_count=z.shape[-1])
    return b_gate * y

def mlstm_chunkwise(q, k, v, i_pre, f_pre):
    out_dtype = q.dtype
    f32 = jnp.float32
    B, S, H, d = q.shape
    L = MLSTM_CHUNK
    nc = S // L
    q = q.astype(f32).reshape(B, nc, L, H, d) * d ** -0.5
    k = k.astype(f32).reshape(B, nc, L, H, d)
    v = v.astype(f32).reshape(B, nc, L, H, d)
    log_i = i_pre.astype(f32).reshape(B, nc, L, H)
    log_f = jax.nn.log_sigmoid(f_pre.astype(f32)).reshape(B, nc, L, H)
    b = jnp.cumsum(log_f, axis=2)
    b_last = b[:, :, -1]

    a = b_last[:, :, None] - b + log_i
    m_loc = a.max(axis=2)
    w_state = jnp.exp(a - m_loc[:, :, None])
    c_loc = jnp.einsum('bclh,bclhd,bclhe->bchde', w_state, k, v)
    n_loc = jnp.einsum('bclh,bclhd->bchd', w_state, k)

    def step(carry, xs):
        c_st, n_st, m_st = carry
        bl, ml, cl, nl = xs
        m_new = jnp.maximum(bl + m_st, ml)
        decay = jnp.exp(bl + m_st - m_new)
        wl = jnp.exp(ml - m_new)
        c_new = decay[..., None, None] * c_st + wl[..., None, None] * cl
        n_new = decay[..., None] * n_st + wl[..., None] * nl
        return (c_new, n_new, m_new), (c_st, n_st, m_st)

    init = (jnp.zeros((B, H, d, d), f32), jnp.zeros((B, H, d), f32), jnp.zeros((B, H), f32))
    xs = (jnp.moveaxis(b_last, 1, 0), jnp.moveaxis(m_loc, 1, 0),
          jnp.moveaxis(c_loc, 1, 0), jnp.moveaxis(n_loc, 1, 0))
    _, (c_prev, n_prev, m_prev) = lax.scan(step, init, xs)
    c_prev = jnp.moveaxis(c_prev, 0, 1)
    n_prev = jnp.moveaxis(n_prev, 0, 1)
    m_prev = jnp.moveaxis(m_prev, 0, 1)

    g = b + m_prev[:, :, None, :]
    dmat = b[:, :, :, None, :] - b[:, :, None, :, :] + log_i[:, :, None, :, :]
    causal = jnp.tril(jnp.ones((L, L), dtype=bool))
    dmat = jnp.where(causal[None, None, :, :, None], dmat, -jnp.inf)
    m_t = jnp.maximum(g, dmat.max(axis=3))
    s_w = jnp.einsum('bcthd,bcshd->bctsh', q, k) * jnp.exp(dmat - m_t[:, :, :, None, :])
    inter = jnp.exp(g - m_t)
    num = (jnp.einsum('bctsh,bcshe->bcthe', s_w, v)
           + inter[..., None] * jnp.einsum('bcthd,bchde->bcthe', q, c_prev))
    den = s_w.sum(axis=3) + inter * jnp.einsum('bcthd,bchd->bcth', q, n_prev)
    h = num / jnp.maximum(jnp.abs(den), jnp.exp(-m_t))[..., None]
    return h.reshape(B, S, H, d).astype(out_dtype)

def swa_attention(q, k, v, sinks, bias):
    B, S, Hq, d = q.shape
    Hkv = k.shape[2]
    G = Hq // Hkv
    W = WINDOW
    nb = S // W
    qb = q.reshape(B, nb, W, Hkv, G, d)

    def band(t):
        tp = jnp.pad(t, ((0, 0), (W, 0), (0, 0), (0, 0))).reshape(B, nb + 1, W, Hkv, d)
        return jnp.concatenate([tp[:, :-1], tp[:, 1:]], axis=2)

    kb, vb = band(k), band(v)
    s = jnp.einsum('bnqhgd,bnjhd->bnhgqj', qb, kb).astype(jnp.float32) * d ** -0.5
    s = s + bias.astype(jnp.float32).reshape(Hkv, G, W, 2 * W)
    qi = jnp.arange(W)[:, None]
    kj = jnp.arange(2 * W)[None, :]
    dist = qi + W - kj
    in_window = (dist >= 0) & (dist < WINDOW)
    key_pos = jnp.arange(nb)[:, None, None] * W - W + kj[None]
    valid = in_window[None] & (key_pos >= 0)
    s = jnp.where(valid[None, :, None, None], s, -jnp.inf)
    sink = jnp.broadcast_to(sinks.astype(jnp.float32).reshape(1, 1, Hkv, G, 1, 1),
                            s.shape[:-1] + (1,))
    p = jax.nn.softmax(jnp.concatenate([s, sink], axis=-1), axis=-1)[..., :-1]
    out = jnp.einsum('bnhgqj,bnjhd->bnqhgd', p.astype(v.dtype), vb)
    return out.reshape(B, S, Hq * d)

def second_inputs(seed: int = 0) -> dict:
    key = jax.random.key(seed)
    ks = jax.random.split(key, 24)

    def nrm(k, shape, scale):
        return jax.random.normal(k, shape, jnp.float32) * scale

    return {
        'x': nrm(ks[0], (BATCH, SEQ, D_MODEL), 1.0),
        'rel_bias': nrm(ks[1], (REL_BUCKETS, SWA_Q_HEADS), 0.5),
        'attn_norm': 1.0 + nrm(ks[2], (DEPTH_2, D_MODEL), 0.05),
        'w_in': nrm(ks[3], (DEPTH_2, D_MODEL, IN_COLS), D_MODEL ** -0.5),
        'fox_f_bias': 3.0 + nrm(ks[4], (DEPTH_2, FOX_HEADS), 1.0),
        'fox_q_gain': 1.0 + nrm(ks[5], (DEPTH_2, HEAD_DIM), 0.05),
        'fox_k_gain': 1.0 + nrm(ks[6], (DEPTH_2, HEAD_DIM), 0.05),
        'conv_w': nrm(ks[7], (DEPTH_2, CONV_K, CONV_W), CONV_K ** -0.5),
        'mlstm_i_bias': nrm(ks[8], (DEPTH_2, MLSTM_HEADS), 0.1),
        'mlstm_f_bias': 4.0 + nrm(ks[9], (DEPTH_2, MLSTM_HEADS), 1.0),
        'mlstm_h_gain': 1.0 + nrm(ks[10], (DEPTH_2, MLSTM_W), 0.05),
        'swa_q_gain': 1.0 + nrm(ks[11], (DEPTH_2, HEAD_DIM), 0.05),
        'swa_k_gain': 1.0 + nrm(ks[12], (DEPTH_2, HEAD_DIM), 0.05),
        'swa_sinks': nrm(ks[13], (DEPTH_2, SWA_Q_HEADS), 1.0),
        'w_fox_out': nrm(ks[14], (DEPTH_2, FOX_W, D_MODEL), FOX_W ** -0.5),
        'w_conv_out': nrm(ks[15], (DEPTH_2, CONV_W, D_MODEL), CONV_W ** -0.5),
        'w_mlstm_out': nrm(ks[16], (DEPTH_2, MLSTM_W, D_MODEL), MLSTM_W ** -0.5),
        'w_swa_out': nrm(ks[17], (DEPTH_2, SWA_W, D_MODEL), SWA_W ** -0.5),
        'w_merge_out': nrm(ks[18], (DEPTH_2, D_MODEL, D_MODEL), D_MODEL ** -0.5),
        'ffn_norm': 1.0 + nrm(ks[19], (DEPTH_2, D_MODEL), 0.05),
        'w_gate': nrm(ks[20], (DEPTH_2, D_MODEL, D_FF_2), D_MODEL ** -0.5),
        'w_up': nrm(ks[21], (DEPTH_2, D_MODEL, D_FF_2), D_MODEL ** -0.5),
        'w_down': nrm(ks[22], (DEPTH_2, D_FF_2, D_MODEL), D_FF_2 ** -0.5),
    }

def second_block(x, rel_bias, attn_norm, w_in, fox_f_bias, fox_q_gain, fox_k_gain, conv_w,
              mlstm_i_bias, mlstm_f_bias, mlstm_h_gain, swa_q_gain, swa_k_gain, swa_sinks,
              w_fox_out, w_conv_out, w_mlstm_out, w_swa_out, w_merge_out, ffn_norm,
              w_gate, w_up, w_down):
    B, S, _ = x.shape
    split_points = np.cumsum(SPLIT_SIZES)[:-1].tolist()

    dist = jnp.arange(WINDOW)[:, None] + WINDOW - jnp.arange(2 * WINDOW)[None, :]
    swa_bias = rel_bias[t5_bucket_2(jnp.maximum(dist, 0))].transpose(2, 0, 1)

    for l in range(DEPTH_2):
        h = rms_norm(x, attn_norm[l])
        proj = jnp.einsum('bsd,dc->bsc', h, w_in[l])
        (fq, fk, fv, ff, cu, cb, cc, mq, mk, mv, mi, mf, mo, sq, sk, sv,
         gates) = jnp.split(proj, split_points, axis=-1)

        fq = rms_norm(fq.reshape(B, S, FOX_HEADS, HEAD_DIM), fox_q_gain[l])
        fk = rms_norm(fk.reshape(B, S, FOX_HEADS, HEAD_DIM), fox_k_gain[l])
        fv = fv.reshape(B, S, FOX_HEADS, HEAD_DIM)
        y_fox = fox_attention(fq, fk, fv, ff + fox_f_bias[l])

        y_conv = short_conv_mixer(cu, cb, cc, conv_w[l])

        hm = mlstm_chunkwise(mq.reshape(B, S, MLSTM_HEADS, HEAD_DIM),
                             mk.reshape(B, S, MLSTM_HEADS, HEAD_DIM),
                             mv.reshape(B, S, MLSTM_HEADS, HEAD_DIM),
                             mi + mlstm_i_bias[l], mf + mlstm_f_bias[l])
        hm = rms_norm(hm, mlstm_h_gain[l].reshape(MLSTM_HEADS, HEAD_DIM))
        y_mlstm = jax.nn.sigmoid(mo) * hm.reshape(B, S, MLSTM_W)

        sq = rms_norm(sq.reshape(B, S, SWA_Q_HEADS, HEAD_DIM), swa_q_gain[l])
        sk = rms_norm(sk.reshape(B, S, SWA_KV_HEADS, HEAD_DIM), swa_k_gain[l])
        sv = sv.reshape(B, S, SWA_KV_HEADS, HEAD_DIM)
        y_swa = swa_attention(sq, sk, sv, swa_sinks[l], swa_bias)

        g = jax.nn.sigmoid(gates.reshape(B, S, N_BRANCH, D_MODEL))
        merged = (g[:, :, 0] * jnp.einsum('bsw,wd->bsd', y_fox, w_fox_out[l])
                  + g[:, :, 1] * jnp.einsum('bsw,wd->bsd', y_conv, w_conv_out[l])
                  + g[:, :, 2] * jnp.einsum('bsw,wd->bsd', y_mlstm, w_mlstm_out[l])
                  + g[:, :, 3] * jnp.einsum('bsw,wd->bsd', y_swa, w_swa_out[l]))
        x = x + jnp.einsum('bsd,de->bse', merged, w_merge_out[l])

        h = rms_norm(x, ffn_norm[l])
        act = jax.nn.silu(jnp.einsum('bsd,df->bsf', h, w_gate[l])) * jnp.einsum('bsd,df->bsf', h, w_up[l])
        x = x + jnp.einsum('bsf,fd->bsd', act, w_down[l])
    return x


def setup_inputs(seed=0):
    out = dict(first_inputs(seed))
    for name, value in second_inputs(seed + 1).items():
        if name != "x":
            out[name + "_2"] = value
    return out


def reference(
    x, meta_tokens, rel_bias, norm_mix, norm_ffn, norm_final, even_w_in, even_gn_gain,
    even_w_out, odd_w_in, odd_w_out, ffn_w_up, ffn_w_gate, ffn_conv_w, ffn_conv_b, ffn_w_down,
    rel_bias_2, attn_norm_2, w_in_2, fox_f_bias_2, fox_q_gain_2, fox_k_gain_2, conv_w_2,
    mlstm_i_bias_2, mlstm_f_bias_2, mlstm_h_gain_2, swa_q_gain_2, swa_k_gain_2, swa_sinks_2,
    w_fox_out_2, w_conv_out_2, w_mlstm_out_2, w_swa_out_2, w_merge_out_2, ffn_norm_2, w_gate_2,
    w_up_2, w_down_2,
):
    x = first_block(
        x, meta_tokens, rel_bias, norm_mix, norm_ffn, norm_final, even_w_in, even_gn_gain,
        even_w_out, odd_w_in, odd_w_out, ffn_w_up, ffn_w_gate, ffn_conv_w, ffn_conv_b,
        ffn_w_down,
    )
    return second_block(
        x, rel_bias_2, attn_norm_2, w_in_2, fox_f_bias_2, fox_q_gain_2, fox_k_gain_2, conv_w_2,
        mlstm_i_bias_2, mlstm_f_bias_2, mlstm_h_gain_2, swa_q_gain_2, swa_k_gain_2, swa_sinks_2,
        w_fox_out_2, w_conv_out_2, w_mlstm_out_2, w_swa_out_2, w_merge_out_2, ffn_norm_2,
        w_gate_2, w_up_2, w_down_2,
    )


_drawn_inputs = setup_inputs


def setup_inputs(seed=0):
    import zlib

    import numpy as np

    out = dict(_drawn_inputs(seed))
    spreads = {}
    factors = {'ffn_conv_b': 5.952,
     'fox_q_gain_2': 6.751,
     'fox_k_gain_2': 8.0,
     'mlstm_i_bias_2': 200.0,
     'mlstm_h_gain_2': 3.963,
     'swa_q_gain_2': 8.0,
     'swa_k_gain_2': 8.0,
     'swa_sinks_2': 171.665,
     'rel_bias_2': 2.968}
    for name, (base, spread) in spreads.items():
        noise = np.random.default_rng([zlib.crc32(name.encode()), seed]).standard_normal(out[name].shape)
        drawn = base * np.exp(spread * noise) if base else spread * noise
        out[name] = __import__('jax').numpy.asarray(drawn.astype(out[name].dtype))
    for name, factor in factors.items():
        out[name] = (out[name] * factor).astype(out[name].dtype)
    return out
```

```python
from contextlib import ExitStack, contextmanager

import numpy as np
import concourse.bass as bass
from concourse import mybir

F32 = mybir.dt.float32
F32R = mybir.dt.float32r
ALU = mybir.AluOpType
ACT = mybir.ActivationFunctionType
AX_X = mybir.AxisListType.X

P = 128
D = 1024
KB = D // P
META = 16
SEQ = 512
T1 = META + SEQ
T2 = SEQ
DFF = 2816
FB = DFF // P
CHUNKS = [(0, 8), (8, 8), (16, 6)]
EPS = 1e-6
KEEP = 128
NEG = -1e30
CAP = 3.0e38
TAKEN = -3.4e38
TAKEN_LIMIT = -3.2e38
START = 3 * 16
LOADS_UNITS = 2


class Count:

    def __init__(self):
        self.n, self.i, self.per, self.start = 0, None, 0, 0

    def enter(self, i, per):
        self.i, self.per, self.start = i, per, self.n

    def leave(self, trips):
        assert self.n - self.start == self.per, (self.n, self.start, self.per)
        self.n, self.i = self.start + self.per * trips, None

    def value(self):
        return self.n if self.i is None else self.i * self.per + self.n

    def step(self, k=1):
        self.n += k
        return self.value()


class Signal:

    def __init__(self, sem):
        self.sem, self.made, self.read = sem, Count(), {}

    def by(self, ins, k=1):
        ins.then_inc(self.sem, k)
        self.made.step(k)

    def reader(self, who):
        return self.read.setdefault(who, Count())

    def take(self, eng, who, k=1):
        eng.wait_ge(self.sem, self.reader(who).step(k))

    def last(self, eng):
        eng.wait_ge(self.sem, self.made.value())


class Stage:
    def __init__(self, name, first, units, trips=1):
        self.name, self.first, self.units, self.trips = name, first, units, trips
        self.advance = units // 4 if trips > 1 else 0
        assert trips == 1 or units % 4 == 0
        self.end = first + units * trips


def make_plan():
    plan, at = {}, 0

    def add(name, units, trips=1):
        nonlocal at
        plan[name] = Stage(name, at, units, trips)
        at += units * trips

    add("a_v", 4)
    add("a_q", 4), add("a_k", 4), add("a_iq", 4)
    add("a_small", 2)
    add("a_out", 4, 2)
    for g in range(2):
        add(f"b_q{g}", 2), add(f"b_k{g}", 2), add(f"b_v{g}", 4), add(f"b_g{g}", 4)
    add("b_out", 4, 2)
    for l in range(3):
        if l == 1:
            for g in range(2):
                add(f"c_v{g}", 4), add(f"c_q{g}", 4), add(f"c_k{g}", 4)
            add("c_out", 4, 2)
        if l == 2:
            add("f_v", 2), add("f_q", 2), add("f_k", 2), add("f_small", 3), add("m_o", 3)
            add("v_u", 2), add("v_b", 2), add("v_c", 2)
            add("m_v", 2), add("m_q", 2), add("m_k", 2)
            add("s_q", 4), add("s_k", 2)
            add("merge", 12, 4)
            add("merge_out", 4, 2)
        for c, (_, n) in enumerate(CHUNKS):
            add(f"ffn{l}_up{c}", 4, n // 2)
            add(f"ffn{l}_down{c}", 4, 2)
    plan["total"] = at
    return plan


PLAN = make_plan()
UNITS = PLAN["total"]
LOADS = UNITS // LOADS_UNITS

PARAMS = {}


def lay_params():
    at = 0
    for name, cols in (("g_mix0", 8), ("g_ffn0", 8), ("g_mix1", 8), ("g_ffn1", 8), ("g_final", 8), ("g_attn", 8),
                       ("g_ffn2", 8), ("gn", 8), ("conv0", 4 * FB), ("conv1", 4 * FB), ("conv2", 6), ("fq", 1),
                       ("fk", 1), ("sq", 1), ("sk", 1), ("mh", 2), ("fbias", 1), ("ibias", 1), ("mfbias", 1)):
        PARAMS[name] = (at, cols)
        at += cols
    return at


NPARAM = lay_params()
CONSTS = {"ident": (0, 128), "ones": (128, 128), "causal": (256, 512), "causalT": (768, 128)}
NCONST = 896
EXTRA = {"flip": (0, 128), "cap": (128, 128), "blockones": (256, 128), "strictT": (384, 128), "strictmul": (512, 128),
         "ntri": (640, 128), "nones": (768, 128), "rot": (896, 128), "cos": (1024, 528), "sin": (1552, 528),
         "decay": (2080, 4 * 528), "selneg": (4192, 512), "onehot1": (4704, 384), "onehot2": (5088, 384)}
NEXTRA = 5472

KEYTILE = [(s, min(P, T1 - P * s)) for s in range(5)]
PIECES = [(4, 512, 528), (3, 384, 528), (2, 256, 528), (1, 128, 528), (0, 264, 528), (0, 0, 264)]
TILE_AT = [0, 528, 928, 1200, 1344]
TRI = 1360


def program(nc, xT, w_all, params, consts, extra, sinks, relb1, relb2, scratch, out):
    ctx = ExitStack()
    with ctx:
        def sb(name, shape, dt=F32):
            return ctx.enter_context(nc.sbuf_tensor(name, shape, dt))

        def sem(name):
            return ctx.enter_context(nc.semaphore(name))

        def signal(name):
            return Signal(sem(name))

        ps = ctx.enter_context(nc.psum_tensor("ps", [P, 8, 512], F32))
        X = sb("X", [P, KB, T1])
        Hh, Hl = sb("Hh", [P, KB, T1], F32R), sb("Hl", [P, KB, T1], F32R)
        Yh, Yl = sb("Yh", [P, 10 * 512], F32R), sb("Yl", [P, 10 * 512], F32R)
        raw = sb("raw", [P, 2, KB, 256])
        wh, wl = sb("wh", [P, 4, KB, P], F32R), sb("wl", [P, 4, KB, P], F32R)
        par = sb("par", [P, NPARAM])
        cst = sb("cst", [P, NCONST])
        zero = sb("zero", [P, 1])
        eps = sb("eps", [P, 2])
        ARENA = 16700
        arena = sb("arena", [P, ARENA])

        def Y(part, T, b, n, c0, c1):
            return part[:, b * T:(b + n) * T].rearrange("p (b t) -> p b t", b=n)[:, :, c0:c1]

        def param(name, c=0, rows=P):
            a = PARAMS[name][0] + c
            return par[0:rows, a:a + 1]

        def const(name):
            a, n = CONSTS[name]
            return cst[:, a:a + n]

        ident, ones, causal, causalT = (const(n) for n in ("ident", "ones", "causal", "causalT"))

        class Cut:
            def __init__(self, at=0):
                self.at = at

            def __call__(self, words, rows=P, **dims):
                v = arena[0:rows, self.at:self.at + words]
                self.at += words
                assert self.at <= ARENA, self.at
                if dims:
                    k = list(dims)
                    v = v.rearrange(f"p ({' '.join(k)} z) -> p {' '.join(k)} z", **dims)
                return v

        raw_landed = [sem(f"raw_landed{s}") for s in range(2)]
        hi_split = sem("hi_split")
        split_ready = [sem(f"split_ready{j}") for j in range(4)]
        unit_done = [sem(f"unit_done{j}") for j in range(4)]
        acc_free = [sem(f"acc_free{j}") for j in range(4)]
        start_landed = sem("start_landed")
        dve = signal("dve_chain")
        acts = signal("act_chain")
        pool_zero = sem("pool_zero")
        h_ready = signal("h_ready")
        y_ready = signal("y_ready")
        sq_made, sq_used, rms_in, rms_sum, rms_std = (signal(n) for n in ("sq_made", "sq_used", "rms_in", "rms_sum", "rms_std"))
        n_tmp, n_hi = signal("n_tmp"), signal("n_hi")
        act_stage, dve_stage, pe_stage = signal("act_stage"), signal("dve_stage"), signal("pe_stage")
        tables_landed = signal("tables_landed")
        out_stored = sem("out_stored")
        b_landed, v_written = sem("b_landed"), sem("v_written")

        sig = {n: signal(n) for n in (
            "g_conv", "g_silu", "prod_hi", "scores", "scores_read", "logits", "probs", "turned", "turn_copied", "pv",
            "pv_read", "yt", "yt_tmp", "yt_hi", "yt_lo", "cv_tmp", "cv_hi", "cv_lo", "idx", "idx_relu", "idx_added", "z_made",             "z_log", "l_made", "cum", "a_diag", "a_exp", "oT_hi", "oT_lo", "rot_made", "rot_done",
            "ret_s", "ret_a", "ret_o", "ret_copied", "ret_var", "ret_std", "hn_sq", "hn_sum", "hn_std", "hn_done",
            "v_made", "tb_made", "tb_copied", "row_made", "row_log", "row_scan", "bc_made",
            "bc_copied", "m_w", "m_wd", "m_s", "m_a", "m_o", "m_read", "m_ss", "m_std", "mg_sum", "mg_hi",
            "memset_done", "stage_dve", "o_used", "ret_norm", "row_done")}
        turn_done = [signal(f"turn_done{q}") for q in range(2)]
        turn_out = [signal(f"turn_out{q}") for q in range(2)]
        turn_count = {}
        block = ctx.enter_context(nc.Block())

        @contextmanager
        def loop(eng, trips, counts):
            with eng.Fori(0, trips) as i:
                for c, per in counts:
                    c.enter(i, per)
                yield i
            for c, _ in counts:
                c.leave(trips)

        def halves(T):
            return [(0, 264), (264, 528)] if T == T1 else [(0, 512)]

        def unit(stage, b, i=0):
            u = stage.first + b
            return u % 4, i * stage.advance + (u // 4 + 1)

        def acc(j, T):
            return ps[:, 2 * j:2 * j + 2, 0:264] if T == T1 else ps[:, 2 * j, :]

        def cols(ap, T):
            return ap.rearrange("p (h n) -> p h n", h=2) if T == T1 else ap

        def wait_evacuated(eng, stage):
            for j in range(4):
                eng.wait_ge(acc_free[j], (stage.end - j + 3) // 4)

        def pe_first(pe, units, T):
            for k in range(KB):
                h_ready.take(pe, "pe")
                for stage, b in units:
                    j, n = unit(stage, b)
                    if k == 0:
                        pe.wait_ge(split_ready[j], n)
                        if stage.first + b >= 4:
                            pe.wait_ge(acc_free[j], n - 1)
                    for part, (w, x) in enumerate(((wh, Hh), (wh, Hl), (wl, Hh))):
                        for h, (c0, c1) in enumerate(halves(T)):
                            mm = pe.matmul(ps[:, 2 * j + h, 0:c1 - c0], w[:, j, k, :], x[:, k, c0:c1],
                                           start=(k == 0 and part == 0), stop=(k == KB - 1 and part == 2))
                    if k == KB - 1:
                        mm.then_inc(unit_done[j], 1)

        def pe_units(pe, stage, T, src=None, blocks=tuple(range(KB)), groups=None, only=None, start=0):
            sh, sl = src if src else (Hh, Hl)

            def body(i):
                for b in (range(stage.units) if only is None else only):
                    j, n = unit(stage, b, i)
                    pe.wait_ge(split_ready[j], n)
                    if stage.first + b >= 4:
                        pe.wait_ge(acc_free[j], n - 1)
                    gs = groups(b) if groups else [(0, (sh, sl), list(enumerate(blocks)))]
                    for bank, (sh_, sl_), ks in gs:
                        for at, (k, blk) in enumerate(ks):
                            for part, (w, x) in enumerate(((wh, sh_), (wh, sl_), (wl, sh_))):
                                for h, (c0, c1) in enumerate(halves(T)):
                                    mm = pe.matmul(ps[:, 2 * j + h + bank, 0:c1 - c0], w[:, j, k, :],
                                                   x[:, blk, c0:c1], start=(at == 0 and part == 0),
                                                   stop=(at == len(ks) - 1 and part == 2))
                    mm.then_inc(unit_done[j], 1)

            if stage.trips == 1:
                body(0)
            else:
                with pe.Fori(start, stage.trips) as i:
                    body(i)

        def evac_units(act, dve_, stage, T, dst, scale=1.0, func=ACT.Copy, base=0, only=None):
            for b in (range(stage.units) if only is None else only):
                j, n = unit(stage, b)
                mine = act is not None if (func != ACT.Copy or b % 2 == 0) else dve_ is not None
                if not mine:
                    continue
                eng = act or dve_
                eng.wait_ge(unit_done[j], n)
                o = cols(dst[:, b - base, :], T)
                if act is not None:
                    ins = act.activation(o, acc(j, T), func, scale=scale)
                else:
                    ins = dve_.tensor_scalar(o, acc(j, T), scale, None, ALU.mult)
                ins.then_inc(acc_free[j], 1)

        def residual_units(v, stage, T, off):
            with v.Fori(0, stage.trips) as i:
                for b in range(stage.units):
                    residual_unit(v, stage, T, off, i, b)

        def residual_unit(v, stage, T, off, i, b):
            j, n = unit(stage, b, i)
            v.wait_ge(unit_done[j], n)
            x = X[:, bass.ds(i * 4 + b, 1), off:off + T]
            x = x.rearrange("p a (h n) -> p (a h) n", h=2) if T == T1 else x.rearrange("p a n -> p (a n)")
            v.tensor_tensor(x, acc(j, T), x, ALU.add).then_inc(acc_free[j], 1)

        YBLK = {T: (lambda part, T=T: part[:, 0:(KB if T == T1 else 10) * T].rearrange("p (b t) -> p b t", t=T))
                for T in (T1, T2)}

        def norm_views(T):
            cut = Cut()
            return cut(4 * T, a=4), cut(T), cut(T), cut(2 * T, a=2)

        def squares_act(act, T, off, stage=None):
            sq = norm_views(T)[0]

            def four(i, blocks):
                for b in range(4):
                    if stage is None:
                        x = X[:, blocks + b, off:off + T]
                        if off == META:
                            sig["stage_dve"].take(act, "act")
                    else:
                        j, n = unit(stage, b, i)
                        act.wait_ge(acc_free[j], n)
                        x = X[:, bass.ds(i * 4 + b, 1), off:off + T].rearrange("p a n -> p (a n)")
                    sq_made.by(act.activation(sq[:, b], x, ACT.Square))
                sq_used.take(act, "act", 4)

            if stage is None:
                four(0, 0)
                four(0, 4)
            else:
                with loop(act, 2, [(sq_made.made, 4), (sq_used.reader("act"), 4)]) as i:
                    four(i, None)
            act.preload_act_table(ACT.Sqrt)

        def squares_dve(v, T, b):
            sq, total, _, _ = norm_views(T)
            sq_made.take(v, "dve")
            sq_used.by(v.tensor_tensor(total, total, sq[:, b], ALU.add))
            sq_used.last(v)

        def residual_squares(v, stage, T, off):
            j, n = unit(stage, 0)
            v.wait_ge(unit_done[j], n)
            dve.by(v.memset(norm_views(T)[1], 0.0))
            dve.last(v)
            with loop(v, stage.trips, [(sq_made.reader("dve"), 4), (sq_used.made, 4)]) as i:
                for b in range(5):
                    if b < 4:
                        residual_unit(v, stage, T, off, i, b)
                    if b:
                        squares_dve(v, T, b - 1)
            rms_in.by(v.tensor_scalar(norm_views(T)[1], norm_views(T)[1], 1.0, None, ALU.mult))

        def norm_act(act, T, split, then=None):
            _, _, rs, tmp = norm_views(T)
            rms_sum.take(act, "act")
            rms_std.by(act.activation(cols(rs, T), acc(0, T), ACT.Sqrt, bias=eps[:, 0:1], scale=1.0 / D))
            if then is not None:
                act.preload_act_table(then)
            if split:
                for k in range(KB):
                    n_tmp.take(act, "act")
                    n_hi.by(act.activation(Hh[:, k, 0:T], tmp[:, k % 2], ACT.Copy))

        def norm_pe(pe, prev, T):
            if prev is not None:
                wait_evacuated(pe, prev)
            rms_in.take(pe, "pe")
            for h, (c0, c1) in enumerate(halves(T)):
                mm = pe.matmul(ps[:, h, 0:c1 - c0], ones, norm_views(T)[1][:, c0:c1], start=True, stop=True)
            rms_sum.by(mm)

        def norm_dve(v, T, off, gain, split):
            _, _, rs, tmp = norm_views(T)
            rms_std.take(v, "dve")
            dve.by(v.reciprocal(rs, rs))
            dve.last(v)
            for k in range(KB + 1):
                if k < KB:
                    x = X[:, k, off:off + T]
                    if split and k >= 2:
                        h_ready.last(v)
                    ins = v.scalar_tensor_tensor(out=tmp[:, k % 2] if split else x, in0=x, scalar=param(gain, k),
                                                 in1=rs, op0=ALU.mult, op1=ALU.mult)
                    (n_tmp if split else sig["stage_dve"]).by(ins)
                if k >= 1 and split:
                    n_hi.take(v, "dve")
                    h_ready.by(v.tensor_tensor(Hl[:, k - 1, 0:T], tmp[:, (k - 1) % 2],
                                               Hh[:, k - 1, 0:T].bitcast(F32), ALU.subtract))

        def squares_alone(v, T):
            total = norm_views(T)[1]
            dve.by(v.memset(total, 0.0))
            dve.last(v)
            for b in range(KB):
                squares_dve(v, T, b % 4)
            rms_in.by(v.tensor_scalar(total, total, 1.0, None, ALU.mult))

        def ffn_views(T):
            cut = Cut()
            return cut(2 * (T + 2), a=2), cut(2 * T, a=2), cut(2 * T, a=2), cut(2 * T, a=2)

        def ffn_act(act, l, T):
            gs, c1, sg, t = ffn_views(T)
            conv = l < 2
            for c, (m0, n) in enumerate(CHUNKS):
                st = PLAN[f"ffn{l}_up{c}"]
                counts = [(sig["prod_hi"].made, 2)]
                if conv:
                    counts += [(sig["g_conv"].reader("act"), 2), (sig["g_silu"].made, 2)]
                with loop(act, n // 2, counts) as i:
                    for mm in range(2):
                        j, k = unit(st, mm, i)
                        act.wait_ge(unit_done[j], k)
                        if conv:
                            act.activation(cols(gs[:, mm, 2:], T), acc(j, T), ACT.Copy).then_inc(acc_free[j], 1)
                        else:
                            act.activation(cols(sg[:, mm], T), acc(j, T), ACT.Silu).then_inc(acc_free[j], 1)
                    if conv:
                        for mm in range(2):
                            sig["g_conv"].take(act, "act")
                            sig["g_silu"].by(act.activation(sg[:, mm], c1[:, mm], ACT.Silu))
                    for mm in range(2):
                        j, k = unit(st, 2 + mm, i)
                        act.wait_ge(acc_free[j], k)
                        sig["prod_hi"].by(act.activation(
                            YBLK[T](Yh)[:, bass.ds(i * 2 + mm, 1), :].rearrange("p a n -> p (a n)"), t[:, mm], ACT.Copy))

        def ffn_dve(v, l, T, off):
            gs, c1, sg, t = ffn_views(T)
            conv = l < 2
            for c, (m0, n) in enumerate(CHUNKS):
                st = PLAN[f"ffn{l}_up{c}"]
                counts = [(sig["prod_hi"].reader("dve"), 2), (y_ready.made, 2)]
                if conv:
                    counts += [(sig["g_silu"].reader("dve"), 2), (sig["g_conv"].made, 2), (dve.made, 4)]
                if conv and c == 0:
                    dve.by(v.memset(gs[:, :, 0:2], 0.0))
                    dve.last(v)
                with loop(v, n // 2, counts) as i:
                    if conv:
                        pa = PARAMS[f"conv{l}"][0]
                        w = [[par[:, bass.ds(i * 8 + (pa + 4 * (m0 + mm) + q), 1)] for q in range(4)]
                             for mm in range(2)]
                        for mm in range(2):
                            j, k = unit(st, mm, i)
                            v.wait_ge(acc_free[j], k)
                            dve.by(v.tensor_scalar(c1[:, mm], gs[:, mm, 2:], w[mm][2], w[mm][3], ALU.mult, ALU.add))
                            dve.last(v)
                            dve.by(v.scalar_tensor_tensor(out=c1[:, mm], in0=gs[:, mm, 1:T + 1], scalar=w[mm][1],
                                                          in1=c1[:, mm], op0=ALU.mult, op1=ALU.add))
                            dve.last(v)
                            sig["g_conv"].by(v.scalar_tensor_tensor(out=c1[:, mm], in0=gs[:, mm, 0:T],
                                                                    scalar=w[mm][0], in1=c1[:, mm], op0=ALU.mult,
                                                                    op1=ALU.add))
                    for mm in range(2):
                        if not conv:
                            j, k = unit(st, mm, i)
                            v.wait_ge(acc_free[j], k)
                        else:
                            sig["g_silu"].take(v, "dve")
                        j, k = unit(st, 2 + mm, i)
                        v.wait_ge(unit_done[j], k)
                        v.tensor_tensor(cols(t[:, mm], T), acc(j, T), cols(sg[:, mm], T), ALU.mult)\
                         .then_inc(acc_free[j], 1)
                    for mm in range(2):
                        j, k = unit(st, 2 + mm, i)
                        v.wait_ge(acc_free[j], k)
                        sig["prod_hi"].take(v, "dve")
                        yb = bass.ds(i * 2 + mm, 1)
                        y_ready.by(v.tensor_tensor(YBLK[T](Yl)[:, yb, :].rearrange("p a n -> p (a n)"), t[:, mm],
                                                   YBLK[T](Yh)[:, yb, :].rearrange("p a n -> p (a n)").bitcast(F32),
                                                   ALU.subtract))
                    y_ready.last(v)
                last = c == len(CHUNKS) - 1 and l < 2
                (residual_squares if last else residual_units)(v, PLAN[f"ffn{l}_down{c}"], T, off)

        def ffn_pe(pe, l, T):
            pe_first(pe, [(PLAN[f"ffn{l}_up0"], b) for b in range(4)], T)
            for c, (m0, n) in enumerate(CHUNKS):
                pe_units(pe, PLAN[f"ffn{l}_up{c}"], T, start=(c == 0))
                y_ready.take(pe, "pe", n)
                pe_units(pe, PLAN[f"ffn{l}_down{c}"], T, (YBLK[T](Yh), YBLK[T](Yl)), tuple(range(n)))

        def turn_pe(pe, jobs):
            for n, (parts, _) in enumerate(jobs):
                q = n % 2
                if turn_done[q].made.value():
                    turn_out[q].take(pe, "pe")
                for src, col in parts:
                    p, f = src.shape
                    mm = flip_over(pe, ps[0:f, 6 + q, col:col + p], src)
                turn_done[q].by(mm)

        def flip_over(pe, dst, src):
            p, f = src.shape
            if f == P and p == P:
                return pe.transpose(dst, src, ident)
            return pe.matmul(dst, src, ident[0:p, 0:p], start=True, stop=True)

        def turned_all(eng, who):
            for q in range(2):
                n = turn_done[q].made.value() if who == "pe" else turn_count[who][q]
                if n:
                    eng.wait_ge(turn_out[q].sem, n)

        def turn_copy(eng, who, jobs, scale=1.0):
            c = turn_count.setdefault(who, [0, 0])
            for n, (_, copies) in enumerate(jobs):
                q = n % 2
                c[q] += 1
                if (who == "act") != (q == 0):
                    continue
                eng.wait_ge(turn_done[q].sem, c[q])
                for a, (rows, bank_cols, dst) in enumerate(copies):
                    src = ps[0:rows, 6 + q, bank_cols[0]:bank_cols[1]]
                    if len(dst.shape) == 3:
                        src = src.rearrange("p (a b) -> p a b", a=dst.shape[1])
                    if who == "act":
                        ins = eng.activation(dst, src, ACT.Copy, scale=scale)
                    else:
                        ins = eng.tensor_scalar(dst, src, scale, None, ALU.mult)
                    if a == len(copies) - 1:
                        turn_out[q].by(ins)

        def v_jobs(vT, V, T, nb):
            jobs = []
            for s in range(-(-T // P)):
                R = min(P, T - P * s)
                jobs.append(([(vT[:, b, P * s:P * s + R], P * b) for b in range(nb)],
                             [(R, (0, P * nb), V[0:R, s, 0:P * nb])]))
            return jobs

        def yturn_pe(pe, jobs):
            for n, job in enumerate(jobs):
                if n >= 2:
                    sig["yt_lo"].take(pe, "pe")
                srcs = job["srcs"]
                for b, src in enumerate(srcs):
                    mm = flip_over(pe, ps[:, 4 + n % 2, b * src.shape[0]:(b + 1) * src.shape[0]], src)
                sig["yt"].by(mm)
            sig["yt_lo"].take(pe, "pe", min(2, len(jobs)))

        def yturn_views(n, job, T):
            nb, R = len(job["srcs"]), job["srcs"][0].shape[0]
            src = ps[:, 4 + n % 2, 0:nb * R].rearrange("p (a b) -> p a b", a=nb)
            hi, lo = (YBLK[T](y)[:, job["y0"]:job["y0"] + nb, job["c0"]:job["c0"] + R] for y in (Yh, Yl))
            return nb, R, src, hi, lo

        def yturn_act(act, jobs, T):
            for n, job in enumerate(jobs):
                nb, R, src, hi, lo = yturn_views(n, job, T)
                sig["yt"].take(act, "act")
                if "mult" in job:
                    sig["yt_tmp"].take(act, "act")
                    src = job["tmp"][:, n % 2, 0:nb * R].rearrange("p (a b) -> p a b", a=nb)
                sig["yt_hi"].by(act.activation(hi, src, ACT.Copy))

        def yturn_dve(v, jobs, T):
            for n, job in enumerate(jobs):
                nb, R, src, hi, lo = yturn_views(n, job, T)
                sig["yt"].take(v, "dve")
                if "mult" in job:
                    for b, (gain, other) in enumerate(job["mult"]):
                        ins = v.scalar_tensor_tensor(out=job["tmp"][:, n % 2, b * R:(b + 1) * R],
                                                     in0=src[:, b], scalar=gain, in1=other, op0=ALU.mult,
                                                     op1=ALU.mult)
                    sig["yt_tmp"].by(ins)
                    src = job["tmp"][:, n % 2, 0:nb * R].rearrange("p (a b) -> p a b", a=nb)
                    sig["yt_tmp"].last(v)
                sig["yt_hi"].take(v, "dve")
                sig["yt_lo"].by(v.tensor_tensor(lo, src, hi.bitcast(F32), ALU.subtract))

        def attn_views(L, PT, small):
            return L, PT, [small[:, 4 * a:4 * a + 4] for a in range(7)]

        def attn_pe(pe, cases, L, PT):
            N = len(cases)
            for n in range(N + 2):
                if n < N:
                    c = cases[n]
                    if n >= 2:
                        sig["scores_read"].take(pe, "pe")
                    for q, k, bank, col in c["qk"]:
                        mm = pe.matmul(ps[0:c["R"], 2 * (n % 2) + bank, col:col + k.shape[1]], q, k, start=True,
                                       stop=True)
                    sig["scores"].by(mm)
                if 1 <= n <= N:
                    m, c = n - 1, cases[n - 1]
                    sig["probs"].take(pe, "pe")
                    for a, (c0, nk, _) in enumerate(c["tiles"]):
                        mm = flip_over(pe, ps[0:nk, 4 + m % 2, a * c["R"]:(a + 1) * c["R"]],
                                       L[0:c["R"], m % 2, c0:c0 + nk])
                    sig["turned"].by(mm)
                if n >= 2:
                    m, c = n - 2, cases[n - 2]
                    sig["turn_copied"].take(pe, "pe")
                    if m >= 2:
                        sig["pv_read"].take(pe, "pe")
                    for a, (c0, nk, val) in enumerate(c["tiles"]):
                        mm = pe.matmul(ps[0:c["R"], 6 + m % 2, 0:64], PT[0:nk, m % 2, a * c["R"]:(a + 1) * c["R"]],
                                       val, start=(a == 0), stop=(a == len(c["tiles"]) - 1))
                    sig["pv"].by(mm)
            sig["scores_read"].take(pe, "pe", 2)
            sig["pv_read"].take(pe, "pe", 2)

        def attn_act(act, cases, L, PT, small):
            N = len(cases)
            _, _, (mx, nm, sm, es, den, rc, _) = attn_views(L, PT, small)
            for n in range(N + 1):
                if n < N:
                    c, a = cases[n], n % 4
                    R, K = c["R"], c["K"]
                    sig["logits"].take(act, "act")
                    if c.get("sink") is not None:
                        act.activation(es[0:R, a:a + 1], c["sink"], ACT.Exp, bias=nm[0:R, a:a + 1])
                    lg = L[0:R, n % 2, 0:K]
                    sig["probs"].by(act.activation(lg, lg, ACT.Exp, bias=nm[0:R, a:a + 1],
                                                   accum_out=sm[0:R, a:a + 1]))
                if n >= 1:
                    m, c = n - 1, cases[n - 1]
                    R = c["R"]
                    sig["turned"].take(act, "act")
                    if m >= 2:
                        sig["pv"].take(act, "act")
                    full = sum(1 for _, nk, _ in c["tiles"] if nk == P)
                    pieces = [(P, 0, full * R)] if full else []
                    if full < len(c["tiles"]):
                        pieces.append((c["tiles"][-1][1], full * R, (full + 1) * R))
                    for rows, c0, c1 in pieces:
                        ins = act.activation(PT[0:rows, m % 2, c0:c1], ps[0:rows, 4 + m % 2, c0:c1], ACT.Copy)
                    sig["turn_copied"].by(ins)
            sig["pv"].take(act, "act", 2)

        def attn_dve(v, cases, L, PT, small):
            N = len(cases)
            _, _, (mx, nm, sm, es, den, rc, _) = attn_views(L, PT, small)
            for n in range(N + 2):
                if n < N:
                    c, a = cases[n], n % 4
                    R, K = c["R"], c["K"]
                    sig["scores"].take(v, "dve")
                    if n >= 2:
                        sig["turned"].take(v, "dve")
                    lg = L[0:R, n % 2, 0:K]
                    if c["mask"] is None:
                        (bank, c0, c1, at, bias), = c["adds"]
                        sig["scores_read"].by(v.tensor_tensor_reduce(
                            out=lg, in0=ps[0:R, 2 * (n % 2) + bank, c0:c1], in1=bias, scale=1.0, scalar=-3.4e38,
                            op0=ALU.add, op1=ALU.max, accum_out=mx[0:R, a:a + 1]))
                        sig["scores_read"].last(v)
                    else:
                        for x, (bank, c0, c1, at, bias) in enumerate(c["adds"]):
                            src, dst = ps[0:R, 2 * (n % 2) + bank, c0:c1], L[0:R, n % 2, at:at + c1 - c0]
                            if bias.shape[1] == 1:
                                ins = v.tensor_scalar(dst, src, bias, None, ALU.add)
                            else:
                                ins = v.tensor_tensor(dst, src, bias, ALU.add)
                        sig["scores_read"].by(ins)
                        sig["scores_read"].last(v)
                        dve.by(v.tensor_tensor_reduce(out=lg, in0=lg, in1=c["mask"], scale=1.0, scalar=-3.4e38,
                                                      op0=ALU.add, op1=ALU.max, accum_out=mx[0:R, a:a + 1]))
                        dve.last(v)
                    if c.get("sink") is not None:
                        ins = v.tensor_scalar(nm[0:R, a:a + 1], mx[0:R, a:a + 1], c["sink"], -1.0, ALU.max, ALU.mult)
                    else:
                        ins = v.tensor_scalar(nm[0:R, a:a + 1], mx[0:R, a:a + 1], -1.0, None, ALU.mult)
                    sig["logits"].by(ins)
                if n >= 2:
                    m, c, a = n - 2, cases[n - 2], (n - 2) % 4
                    R = c["R"]
                    sig["pv"].take(v, "dve")
                    total = sm
                    if c.get("sink") is not None:
                        dve.by(v.tensor_tensor(den[0:R, a:a + 1], sm[0:R, a:a + 1], es[0:R, a:a + 1], ALU.add))
                        dve.last(v)
                        total = den
                    dve.by(v.reciprocal(rc[0:R, a:a + 1], total[0:R, a:a + 1]))
                    dve.last(v)
                    sig["pv_read"].by(v.tensor_scalar(c["out"], ps[0:R, 6 + m % 2, 0:64], rc[0:R, a:a + 1], None,
                                                      ALU.mult))
            sig["turned"].take(v, "dve", 2)

        def tables_act(act, which, cut_views):
            rel, onehot, vec, hank, flip, TB = cut_views
            a, n = EXTRA["onehot1" if which == 0 else "onehot2"]
            act.dma_start(onehot, extra[0:33, a:a + n]).then_inc(b_landed, 16)
            act.dma_start(flip, extra[:, EXTRA["flip"][0]:EXTRA["flip"][0] + P]).then_inc(b_landed, 16)
            act.dma_start(rel[0:32], relb1 if which == 0 else relb2).then_inc(b_landed, 16)
            sig["v_made"].take(act, "act")
            acts.by(act.activation(vec, ps[0:8, 0, 0:384], ACT.Copy))
            acts.last(act)
            act.dma_start(scratch[which], vec).then_inc(v_written, 16)
            act.wait_ge(v_written, 16 * (which + 1))
            act.dma_start(hank.rearrange("p (h c) -> p h c", h=8),
                          bass.AP(tensor=scratch.tensor, offset=which * 8 * 384, ap=[[1, P], [384, 8], [1, 256]]))\
               .then_inc(b_landed, 16)
            sig["tb_made"].take(act, "act")
            sig["tb_copied"].by(act.activation(TB, ps[:, 0:4, :].rearrange("p a b -> p (a b)"), ACT.Copy))

        def tables_dve(v, cut_views):
            sig["memset_done"].by(v.memset(cut_views[0][32:33], NEG))

        def tables_pe(pe, which, cut_views):
            rel, onehot, vec, hank, flip, TB = cut_views
            pe.wait_ge(b_landed, 64 * which + 48)
            sig["memset_done"].take(pe, "pe")
            sig["v_made"].by(pe.matmul(ps[0:8, 0, 0:384], rel, onehot, start=True, stop=True))
            pe.wait_ge(b_landed, 64 * which + 64)
            for a in range(4):
                mm = pe.matmul(ps[:, a, :], flip, hank[:, 512 * a:512 * a + 512], start=True, stop=True)
            sig["tb_made"].by(mm)
            sig["tb_copied"].take(pe, "pe")

        def dsa_views():
            cut = Cut()
            q, k = cut(4 * T1, b=4), cut(4 * T1, b=4)
            at = cut.at
            iq, ikk = cut(4 * T1, b=4), cut(T1)
            O = Cut(at)(5 * 512, t=5)
            at = cut.at
            cut(2400)
            w = Cut(at)
            vT = w(4 * T1, b=4)
            w = Cut(at)
            L, PT = w(2 * T1, a=2), w(2 * 640, a=2)
            V, TB = cut(5 * 512, t=5), cut(2048)
            at = cut.at
            A = cut(4 * T1, a=4)
            iwT = Cut(at)(T1, rows=8)
            hank = Cut(at)(2048)
            cap, iwt, small, far, m8 = cut(128), cut(40, t=5), cut(28), cut(8), cut(8)
            rel = cut(8, rows=33)
            w = Cut()
            onehot, vec, flip = w(384, rows=33), w(384, rows=8), w(128)
            return dict(q=q, k=k, iq=iq, ikk=ikk, O=O, vT=vT, L=L, PT=PT, V=V, TB=TB.rearrange("p (h c) -> p h c", h=8),
                        A=A, iwT=iwT, cap=cap, iwt=iwt, small=small, far=far, m8=m8,
                        tables=(rel, onehot, vec, hank, flip, TB))

        def head(a, h, c0, c1):
            return a[64 * (h % 2):64 * (h % 2) + 64, h // 2, c0:c1]

        def index_cases():
            return [(t, h, min(P, T1 - P * t), min(T1, P * (t + 1))) for t in range(1, 5) for h in range(8)]

        def bank_parts(K):
            return [(0, 0, K)] if K <= 512 else [(0, 0, 384), (1, 384, K)]

        def dsa_cases(d):
            cases = []
            for t in range(5):
                R, K = min(P, T1 - P * t), min(T1, P * (t + 1))
                for h in range(8):
                    adds = []
                    if t >= 2:
                        adds.append((0, 0, P * (t - 1), 0, d["far"][0:R, h:h + 1]))
                    if t == 0:
                        adds.append((0, 0, P, 0, d["TB"][:, h, P:2 * P]))
                    elif t < 4:
                        adds.append((0, K - 256, K, K - 256, d["TB"][:, h, :]))
                    else:
                        adds.append((1, 0, K - 384, 384, d["TB"][0:R, h, 0:K - 384]))
                    cases.append(dict(
                        R=R, K=K, adds=adds, mask=causal[:, 384:512] if t == 0 else d["A"][0:R, t - 1, 0:K],
                        qk=[(head(d["q"], h, P * t, P * t + R), head(d["k"], h, c0, c1), bank, 0)
                            for bank, c0, c1 in bank_parts(K)],
                        tiles=[(P * s, n, d["V"][0:n, s, 64 * h:64 * h + 64]) for s, n in KEYTILE[0:t + 1]],
                        out=d["O"][0:R, t, 64 * h:64 * h + 64]))
            return cases

        def dsa_turns(d):
            iw = [(d["iwT"][:, P * t:P * t + min(P, T1 - P * t)], 8 * t) for t in range(5)]
            return [(iw, [(P, (0, 32), d["iwt"][:, 0:4, :]), (16, (32, 40), d["iwt"][0:16, 4, :])])]

        def dsa_ys(d):
            return [dict(srcs=[d["O"][0:min(P, T1 - P * t), t, P * b:P * b + P] for b in range(4)], y0=0, c0=P * t)
                    for t in range(5)]

        def dsa_pe(pe):
            d = dsa_views()
            pe_first(pe, [(PLAN["a_v"], b) for b in range(4)], T1)
            for n in ("a_q", "a_k", "a_iq", "a_small"):
                pe_units(pe, PLAN[n], T1)
            wait_evacuated(pe, PLAN["a_small"])
            turn_pe(pe, dsa_turns(d))
            turn_pe(pe, v_jobs(d["vT"], d["V"], T1, 4))
            for n, (t, h, R, K) in enumerate(index_cases()):
                if n >= 2:
                    sig["idx_relu"].take(pe, "pe")
                for bank, c0, c1 in bank_parts(K):
                    mm = pe.matmul(ps[0:R, 2 * (n % 2) + bank, 0:c1 - c0], head(d["iq"], h, P * t, P * t + R),
                                   d["ikk"][64 * (h % 2):64 * (h % 2) + 64, c0:c1], start=True, stop=True)
                sig["idx"].by(mm)
            sig["idx_relu"].take(pe, "pe", 2)
            turned_all(pe, "pe")
            attn_pe(pe, dsa_cases(d), d["L"], d["PT"])
            yturn_pe(pe, dsa_ys(d))
            pe_units(pe, PLAN["a_out"], T1, (YBLK[T1](Yh), YBLK[T1](Yl)), tuple(range(4)))

        def dsa_act(act):
            d = dsa_views()
            evac_units(act, None, PLAN["a_v"], T1, d["vT"])
            a = EXTRA["cap"][0]
            act.dma_start(d["cap"], extra[:, a:a + P]).then_inc(tables_landed.sem, 16)
            act.dma_start(d["far"], bass.AP(tensor=relb1.tensor, offset=31 * 8, ap=[[0, P], [1, 8]]))\
               .then_inc(tables_landed.sem, 16)
            evac_units(act, None, PLAN["a_q"], T1, d["q"], 64 ** -0.5)
            evac_units(act, None, PLAN["a_k"], T1, d["k"])
            evac_units(act, None, PLAN["a_iq"], T1, d["iq"])
            j, n = unit(PLAN["a_small"], 0)
            act.wait_ge(unit_done[j], n)
            act.activation(cols(d["ikk"], T1), acc(j, T1), ACT.Copy).then_inc(acc_free[j], 1)
            turn_copy(act, "act", dsa_turns(d), 8 ** -0.5 * 64 ** -0.5)
            turn_copy(act, "act", v_jobs(d["vT"], d["V"], T1, 4))
            turned_all(act, "act")
            for n, (t, h, R, K) in enumerate(index_cases()):
                sig["idx"].take(act, "act")
                if n >= 2:
                    sig["idx_added"].take(act, "act")
                for bank, c0, c1 in bank_parts(K):
                    ins = act.activation(d["L"][0:R, n % 2, c0:c1], ps[0:R, 2 * (n % 2) + bank, 0:c1 - c0], ACT.Relu)
                sig["idx_relu"].by(ins)
            sig["idx_added"].take(act, "act", 2)
            attn_act(act, dsa_cases(d), d["L"], d["PT"], d["small"])
            yturn_act(act, dsa_ys(d), T1)

        def dsa_dve(v):
            d = dsa_views()
            evac_units(None, v, PLAN["a_v"], T1, d["vT"])
            evac_units(None, v, PLAN["a_q"], T1, d["q"], 64 ** -0.5)
            evac_units(None, v, PLAN["a_k"], T1, d["k"])
            evac_units(None, v, PLAN["a_iq"], T1, d["iq"])
            j, n = unit(PLAN["a_small"], 1)
            v.wait_ge(unit_done[j], n)
            v.tensor_copy(cols(d["iwT"], T1), ps[0:8, 2 * j:2 * j + 2, 0:264]).then_inc(acc_free[j], 1)
            turn_copy(v, "dve", dsa_turns(d))
            turn_copy(v, "dve", v_jobs(d["vT"], d["V"], T1, 4))
            turned_all(v, "dve")
            v.wait_ge(tables_landed.sem, 32)
            for t, h, R, K in index_cases():
                A, r = d["A"][0:R, t - 1, 0:K], d["L"][0:R, h % 2, 0:K]
                sig["idx_relu"].take(v, "dve")
                if h == 0:
                    ins = v.tensor_scalar(A, r, d["iwt"][0:R, t, 0:1], None, ALU.mult)
                else:
                    ins = v.scalar_tensor_tensor(out=A, in0=r, scalar=d["iwt"][0:R, t, h:h + 1], in1=A,
                                                 op0=ALU.mult, op1=ALU.add)
                sig["idx_added"].by(ins)
                sig["idx_added"].last(v)
                if h < 7:
                    continue
                diag = A[:, P * t:P * t + R]
                dve.by(v.tensor_tensor(diag, diag, d["cap"][0:R, 0:R], ALU.min))
                dve.last(v)
                rest = A[:, META:K]
                for _ in range((KEEP - META) // 8):
                    dve.by(v.max(d["m8"][0:R], rest))
                    dve.last(v)
                    dve.by(v.match_replace(rest, d["m8"][0:R], rest, TAKEN))
                    dve.last(v)
                dve.by(v.tensor_scalar(rest, rest, TAKEN_LIMIT, NEG, ALU.is_gt, ALU.mult))
                dve.by(v.memset(A[:, 0:META], 0.0))
                dve.last(v)
            attn_dve(v, dsa_cases(d), d["L"], d["PT"], d["small"])
            yturn_dve(v, dsa_ys(d), T1)
            residual_units(v, PLAN["a_out"], T1, 0)

        def ret_views():
            cut = Cut()
            q, k = cut(2 * T1, b=2), cut(2 * T1, b=2)
            at = cut.at
            AT = cut(2 * TRI, b=2)
            vT = Cut(at)(4 * T1, b=4)
            V, G = cut(5 * 512, t=5), cut(4 * T1, b=4)
            at = cut.at
            O = cut(5 * 512, t=5)
            rt = Cut(at)(2 * T1, a=2)
            decay, cos, sin, rot = cut(2 * T1, b=2), cut(T1), cut(T1), cut(P)
            tmp, st, mv, sd = cut(1024, a=2), cut(6), cut(20, a=10), cut(10)
            return dict(q=q, k=k, qk=(q, k), AT=AT, vT=vT, V=V, G=G, O=O, rt=rt, decay=decay, cos=cos, sin=sin, rot=rot, tmp=tmp,
                        st=st, mv=mv, sd=sd)

        RET_PIECES = [(hh, *p) for hh in range(2) for p in PIECES]
        RET_OUTS = [(hh, t, min(P, T1 - P * t)) for hh in range(2) for t in range(5)]

        def ret_ys(d, g):
            return [dict(srcs=[d["O"][0:min(P, T1 - P * t), t, P * b:P * b + P] for b in range(4)], y0=4 * g, c0=P * t,
                         tmp=d["tmp"], mult=[(param("gn", 4 * g + b), d["G"][:, b, P * t:min(T1, P * t + P)])
                                             for b in range(4)]) for t in range(5)]

        def ret_pe(pe, g):
            d = ret_views()
            for n in ("b_q", "b_k", "b_v", "b_g"):
                pe_units(pe, PLAN[f"{n}{g}"], T1)
            wait_evacuated(pe, PLAN[f"b_g{g}"])
            pe.wait_ge(tables_landed.sem, 32 + 64 * (g + 1))
            turn_pe(pe, v_jobs(d["vT"], d["V"], T1, 4))
            for n in range(4):
                if n >= 2:
                    sig["rot_done"].take(pe, "pe")
                x = d["qk"[n // 2]][:, n % 2, :]
                for h, (c0, c1) in enumerate(halves(T1)):
                    mm = pe.matmul(ps[:, 2 * (n % 2) + h, 0:c1 - c0], d["rot"], x[:, c0:c1], start=True, stop=True)
                sig["rot_made"].by(mm)
            sig["rot_done"].take(pe, "pe", 2)
            turned_all(pe, "pe")
            for n, (hh, s, c0, c1) in enumerate(RET_PIECES):
                if n >= 4:
                    sig["ret_a"].take(pe, "pe")
                R = KEYTILE[s][1]
                sig["ret_s"].by(pe.matmul(ps[0:R, n % 4, 0:c1 - c0], d["k"][:, hh, P * s:P * s + R],
                                          d["q"][:, hh, c0:c1], start=True, stop=True))
            sig["ret_a"].take(pe, "pe", 4)
            for n, (hh, t, R) in enumerate(RET_OUTS):
                if n >= 2:
                    sig["ret_copied"].take(pe, "pe")
                for s in range(t + 1):
                    a = TILE_AT[s] + P * (t - s)
                    mm = pe.matmul(ps[0:R, 4 + n % 2, 0:256], d["AT"][0:KEYTILE[s][1], hh, a:a + R],
                                   d["V"][0:KEYTILE[s][1], s, 256 * hh:256 * hh + 256], start=(s == 0), stop=(s == t))
                sig["ret_o"].by(mm)
            sig["ret_copied"].take(pe, "pe", 2)
            sig["ret_norm"].take(pe, "pe")
            yturn_pe(pe, ret_ys(d, g))

        def ret_act(act, g):
            d = ret_views()
            evac_units(act, None, PLAN[f"b_q{g}"], T1, d["q"])
            for name, dst, c, n in (("cos", d["cos"], 0, T1), ("sin", d["sin"], 0, T1), ("rot", d["rot"], 0, P),
                                    ("decay", d["decay"].rearrange("p b t -> p (b t)"), 2 * T1 * g, 2 * T1)):
                a = EXTRA[name][0] + c
                act.dma_start(dst, extra[:, a:a + n]).then_inc(tables_landed.sem, 16)
            evac_units(act, None, PLAN[f"b_k{g}"], T1, d["k"])
            evac_units(act, None, PLAN[f"b_v{g}"], T1, d["vT"])
            evac_units(act, None, PLAN[f"b_g{g}"], T1, d["G"], func=ACT.Silu)
            turn_copy(act, "act", v_jobs(d["vT"], d["V"], T1, 4))
            for n, (hh, t, R) in enumerate(RET_OUTS):
                sig["ret_o"].take(act, "act")
                sig["ret_copied"].by(act.activation(d["O"][0:R, t, 256 * hh:256 * hh + 256],
                                                    ps[0:R, 4 + n % 2, 0:256], ACT.Copy))
            sig["ret_var"].take(act, "act")
            sig["ret_std"].by(act.activation(d["sd"], d["mv"][:, :, 1], ACT.Sqrt, bias=eps[:, 0:1]))
            yturn_act(act, ret_ys(d, g), T1)

        def ret_dve(v, g):
            d = ret_views()
            evac_units(None, v, PLAN[f"b_q{g}"], T1, d["q"])
            evac_units(None, v, PLAN[f"b_k{g}"], T1, d["k"])
            evac_units(None, v, PLAN[f"b_v{g}"], T1, d["vT"])
            turn_copy(v, "dve", v_jobs(d["vT"], d["V"], T1, 4))
            v.wait_ge(tables_landed.sem, 32 + 64 * (g + 1))
            for n in range(4):
                sig["rot_made"].take(v, "dve")
                if n:
                    sig["rot_done"].last(v)
                x = d["qk"[n // 2]][:, n % 2, :]
                dve.by(v.tensor_tensor(d["rt"][:, 0], x, d["cos"], ALU.mult))
                dve.by(v.tensor_tensor(cols(d["rt"][:, 1], T1), acc(n % 2, T1), cols(d["sin"], T1), ALU.mult))
                dve.last(v)
                sig["rot_done"].by(v.tensor_tensor(x, d["rt"][:, 0], d["rt"][:, 1], ALU.add))
            for n, (hh, s, c0, c1) in enumerate(RET_PIECES):
                sig["ret_s"].take(v, "dve")
                if n == 0:
                    turned_all(v, "dve")
                R, a = KEYTILE[s][1], TILE_AT[s] + c0 - P * s
                sig["ret_a"].by(v.tensor_tensor(d["AT"][0:R, hh, a:a + c1 - c0], ps[0:R, n % 4, 0:c1 - c0],
                                                d["decay"][0:R, hh, c0 - P * s:c1 - P * s], ALU.mult))
            dve.by(v.memset(d["mv"], 1.0))
            dve.last(v)
            for n, (hh, t, R) in enumerate(RET_OUTS):
                sig["ret_copied"].take(v, "dve")
                dve.by(v.bn_stats(d["st"][0:R], d["O"][0:R, t, 256 * hh:256 * hh + 256]))
                dve.last(v)
                dve.by(v.bn_aggr(d["mv"][0:R, n], d["st"][0:R]))
                dve.last(v)
            sig["ret_var"].by(v.memset(d["st"], 0.0))
            sig["ret_std"].take(v, "dve")
            dve.by(v.reciprocal(d["sd"], d["sd"]))
            dve.last(v)
            for n, (hh, t, R) in enumerate(RET_OUTS):
                o = d["O"][0:R, t, 256 * hh:256 * hh + 256]
                ins = v.tensor_scalar(o, o, d["mv"][0:R, n, 0:1], d["sd"][0:R, n:n + 1], ALU.subtract, ALU.mult)
            sig["ret_norm"].by(ins)
            yturn_dve(v, ret_ys(d, g), T1)

        def stick_views():
            cut = Cut()
            q, k = cut(4 * T1, b=4), cut(4 * T1, b=4)
            at = cut.at
            L1 = cut(2 * TRI, b=2)
            vT = Cut(at)(4 * T1, b=4)
            V, A, E, Dg = cut(5 * 512, t=5), cut(3 * 400, a=3), cut(3 * 400, a=3), cut(2 * P, a=2)
            strictT, strictmul, ntri, nones = cut(P), cut(P), cut(P), cut(P)
            return dict(q=q, k=k, L1=L1, vT=vT, V=V, A=A, E=E, D=Dg, strictT=strictT, strictmul=strictmul, ntri=ntri,
                        nones=nones)

        STICK = [(hh, x, *p) for hh in range(8) for x, p in enumerate(PIECES)]
        NS = len(STICK)

        def has_diag(s, c0):
            return c0 == P * s

        def l_cols(d, hh, s, c0, c1):
            a = TILE_AT[s] - P * s
            return d["L1"][0:KEYTILE[s][1], hh % 2, a + c0:a + c1]

        def stick_pe(pe, g):
            d = stick_views()
            if g == 0:
                pe_first(pe, [(PLAN["c_v0"], b) for b in range(4)], T1)
            for n in ("c_v", "c_q", "c_k")[g == 0:]:
                pe_units(pe, PLAN[f"{n}{g}"], T1)
            wait_evacuated(pe, PLAN[f"c_k{g}"])
            pe.wait_ge(tables_landed.sem, 32 + 128 + 64 * (g + 1))
            turn_pe(pe, v_jobs(d["vT"], d["V"], T1, 4))
            turned_all(pe, "pe")
            for n in range(NS + 4):
                if n < NS:
                    hh, x, s, c0, c1 = STICK[n]
                    R = KEYTILE[s][1]
                    sig["z_made"].by(pe.matmul(ps[0:R, n % 6, 0:c1 - c0], head(d["k"], hh, P * s, P * s + R),
                                               head(d["q"], hh, c0, c1), start=True, stop=True))
                if 0 <= n - 2 < NS:
                    m = n - 2
                    hh, x, s, c0, c1 = STICK[m]
                    R = KEYTILE[s][1]
                    sig["l_made"].take(pe, "pe")
                    mm = pe.matmul(ps[0:R, m % 6, 0:c1 - c0], d["ntri"][0:R, 0:R], l_cols(d, hh, s, c0, c1),
                                   start=False, stop=True, skip_group_check=True)
                    for s2 in range(s + 1, 5):
                        lo = max(c0, P * s2)
                        if lo < c1:
                            mm = pe.matmul(ps[0:R, m % 6, lo - c0:c1 - c0], d["nones"][0:KEYTILE[s2][1], 0:R],
                                           l_cols(d, hh, s2, lo, c1), start=False, stop=True, skip_group_check=True)
                    sig["cum"].by(mm)
                if 0 <= n - 4:
                    m = n - 4
                    hh, x, s, c0, c1 = STICK[m]
                    R = KEYTILE[s][1]
                    sig["a_exp"].take(pe, "pe")
                    if x == 0 and hh % 2 == 0 and hh >= 2:
                        sig["oT_lo"].take(pe, "pe")
                    for h, (h0, h1) in enumerate(halves(T1)):
                        lo, hi = max(c0, h0), min(c1, h1)
                        if lo < hi:
                            mm = pe.matmul(ps[64 * (hh % 2):64 * (hh % 2) + 64, 6 + h, lo - h0:hi - h0],
                                           d["V"][0:R, s, 64 * hh:64 * hh + 64], d["A"][0:R, m % 3, lo - c0:hi - c0],
                                           start=(x == (2, 0)[h]), stop=(x == (5, 4)[h]), skip_group_check=True)
                    sig["o_used"].by(mm)
            sig["oT_lo"].take(pe, "pe")

        def stick_act(act, g):
            d = stick_views()
            evac_units(act, None, PLAN[f"c_v{g}"], T1, d["vT"])
            for name in ("strictT", "strictmul", "ntri", "nones"):
                a = EXTRA[name][0]
                act.dma_start(d[name], extra[:, a:a + P]).then_inc(tables_landed.sem, 16)
            evac_units(act, None, PLAN[f"c_q{g}"], T1, d["q"], 64 ** -0.5)
            evac_units(act, None, PLAN[f"c_k{g}"], T1, d["k"])
            turn_copy(act, "act", v_jobs(d["vT"], d["V"], T1, 4))
            act.preload_act_table_set("natural_log_exp_and_others")
            for n in range(NS + 5):
                if n < NS:
                    hh, x, s, c0, c1 = STICK[n]
                    R = KEYTILE[s][1]
                    e = d["E"][0:R, n % 3, 0:c1 - c0]
                    sig["z_made"].take(act, "act")
                    if n >= 3:
                        sig["l_made"].take(act, "act")
                    acts.by(act.activation(e, ps[0:R, n % 6, 0:c1 - c0], ACT.Abs))
                    acts.last(act)
                    acts.by(act.activation(e, e, ACT.Exp, scale=-1.0))
                    acts.last(act)
                    sig["z_log"].by(act.activation(e, e, ACT.Ln, bias=1.0))
                if 0 <= n - 3 < NS:
                    m = n - 3
                    hh, x, s, c0, c1 = STICK[m]
                    R = KEYTILE[s][1]
                    sig["cum"].take(act, "act")
                    if m >= 3:
                        sig["o_used"].take(act, "act")
                    at = 0
                    if has_diag(s, c0):
                        sig["a_diag"].take(act, "act")
                        ins = act.activation(d["A"][0:R, m % 3, 0:R], d["D"][0:R, m % 2, 0:R], ACT.Exp)
                        at = R
                    if at < c1 - c0:
                        ins = act.activation(d["A"][0:R, m % 3, at:c1 - c0], ps[0:R, m % 6, at:c1 - c0], ACT.Exp)
                    sig["a_exp"].by(ins)
                if 0 <= n - 5 < NS:
                    hh, x = STICK[n - 5][0:2]
                    if x == 5 and hh % 2:
                        act.wait_ge(sig["o_used"].sem, NS * g + n - 4)
                        sig["oT_hi"].by(act.activation(cols(YBLK[T1](Yh)[:, 4 * g + hh // 2, :], T1),
                                                       acc(3, T1), ACT.Copy))
            sig["o_used"].take(act, "act", 3)
            sig["l_made"].take(act, "act", 3)

        def stick_dve(v, g):
            d = stick_views()
            evac_units(None, v, PLAN[f"c_v{g}"], T1, d["vT"])
            evac_units(None, v, PLAN[f"c_q{g}"], T1, d["q"], 64 ** -0.5)
            evac_units(None, v, PLAN[f"c_k{g}"], T1, d["k"])
            turn_copy(v, "dve", v_jobs(d["vT"], d["V"], T1, 4))
            turned_all(v, "dve")
            v.wait_ge(tables_landed.sem, 32 + 128 + 64 * (g + 1))
            for n in range(NS + 5):
                if 0 <= n - 1 < NS:
                    m = n - 1
                    hh, x, s, c0, c1 = STICK[m]
                    R = KEYTILE[s][1]
                    if x == 0 and hh >= 2:
                        sig["cum"].take(v, "dve", 6)
                    sig["z_log"].take(v, "dve")
                    l1 = l_cols(d, hh, s, c0, c1)
                    ins = v.scalar_tensor_tensor(out=l1, in0=ps[0:R, m % 6, 0:c1 - c0], scalar=0.0,
                                                 in1=d["E"][0:R, m % 3, 0:c1 - c0], op0=ALU.max, op1=ALU.add)
                    if has_diag(s, c0):
                        dve.by(ins)
                        dve.last(v)
                        ins = v.tensor_tensor(l1[:, 0:R], l1[:, 0:R], d["strictmul"][0:R, 0:R], ALU.mult)
                    sig["l_made"].by(ins)
                if 0 <= n - 3 < NS:
                    m = n - 3
                    hh, x, s, c0, c1 = STICK[m]
                    R = KEYTILE[s][1]
                    if m >= 2:
                        sig["a_exp"].take(v, "dve")
                    if has_diag(s, c0):
                        v.wait_ge(sig["cum"].sem, NS * g + m + 1)
                        sig["a_diag"].by(v.tensor_tensor(d["D"][0:R, m % 2, 0:R], ps[0:R, m % 6, 0:R],
                                                         d["strictT"][0:R, 0:R], ALU.add))
                if 0 <= n - 5 < NS:
                    hh, x = STICK[n - 5][0:2]
                    if x == 5 and hh % 2:
                        sig["oT_hi"].take(v, "dve")
                        yh, yl = (YBLK[T1](y)[:, 4 * g + hh // 2, :] for y in (Yh, Yl))
                        sig["oT_lo"].by(v.tensor_tensor(cols(yl, T1), acc(3, T1), cols(yh, T1).bitcast(F32),
                                                        ALU.subtract))
            sig["cum"].take(v, "dve", 12)
            sig["a_exp"].take(v, "dve", 2)

        def keep_views():
            cut = Cut(ARENA - 4096)
            sv, mo = cut(T2), cut(2 * T2, b=2)
            rows = [cut(T2, rows=4) for _ in range(5)]
            return dict(sv=sv, mo=mo, c=rows[0], B=rows[1], u=rows[2], M=rows[3], e=rows[4])

        def headnorm_act(act, items, sq, rs):
            N = len(items)
            for n in range(N + 1):
                if n < N:
                    sig["hn_sq"].by(act.activation(sq[:, n % 2], items[n][0], ACT.Square))
                if n >= 1:
                    m = n - 1
                    sig["hn_sum"].take(act, "act")
                    if m >= 2:
                        sig["hn_done"].take(act, "act")
                    e = 64 if items[m][2] else 1
                    sig["hn_std"].by(act.activation(rs[:, m % 2], ps[:, m % 2, :], ACT.Sqrt,
                                                    bias=eps[:, 1:2] if items[m][2] else eps[:, 0:1], scale=e / 64))
            sig["hn_done"].take(act, "act", 2)

        def headnorm_pe(pe, N, sq, blockones):
            for n in range(N):
                sig["hn_sq"].take(pe, "pe")
                if n >= 2:
                    sig["hn_std"].take(pe, "pe")
                sig["hn_sum"].by(pe.matmul(ps[:, n % 2, :], blockones, sq[:, n % 2], start=True, stop=True))
            sig["hn_std"].take(pe, "pe", 2)
            pe.wait_ge(sig["hn_done"].sem, headnorm_pe_total(N))

        hn_total = [0]

        def headnorm_pe_total(N):
            hn_total[0] += N
            return hn_total[0]

        def headnorm_dve(v, items, rs):
            for n, (x, gain, _) in enumerate(items):
                sig["hn_std"].take(v, "dve")
                dve.by(v.reciprocal(rs[:, n % 2], rs[:, n % 2]))
                dve.last(v)
                sig["hn_done"].by(v.scalar_tensor_tensor(out=x, in0=x, scalar=gain, in1=rs[:, n % 2], op0=ALU.mult,
                                                         op1=ALU.mult))

        TABLES1 = 32 + 128 + 128
        TB1 = TABLES1

        def spread_act(act, dst):
            sig["bc_made"].take(act, "act")
            sig["bc_copied"].by(act.activation(dst, ps[:, 0:4, :], ACT.Copy))

        def spread_pe(pe, selneg, row):
            for h in range(4):
                mm = pe.matmul(ps[:, h, :], selneg[:, h, :], row, start=True, stop=True)
            sig["bc_made"].by(mm)
            sig["bc_copied"].take(pe, "pe")

        def fox_views():
            cut = Cut()
            vT, V = cut(2 * T2, b=2), cut(4 * 256, t=4)
            q, k = cut(2 * T2, b=2), cut(2 * T2, b=2)
            at = cut.at
            NC = cut(4 * T2, h=4)
            tmp = Cut(at)
            z1, l1, z2, l2 = (tmp(T2, rows=4) for _ in range(4))
            L = cut(2 * T2, a=2)
            at = cut.at
            PT = cut(2 * 512, a=2)
            one = Cut(at)(T2, rows=4)
            O, sq, rs = cut(4 * 256, t=4), cut(2 * T2, a=2), cut(2 * T2, a=2)
            blockones, selneg, small = cut(P), cut(4 * P, rows=4, h=4), cut(28)
            return dict(vT=vT, V=V, q=q, k=k, NC=NC, z=(z1, z2), l=(l1, l2), L=L, PT=PT, one=one, O=O, sq=sq, rs=rs,
                        blockones=blockones, selneg=selneg, small=small, **{"keep": keep_views()})

        def fox_norms(d):
            return [(d["q"][:, b], param("fq"), True) for b in range(2)] + \
                   [(d["k"][:, b], param("fk"), False) for b in range(2)]

        def fox_cases(d):
            return [dict(R=P, K=P * (t + 1), adds=[(0, 0, P * (t + 1), 0, d["NC"][:, h, 0:P * (t + 1)])],
                         mask=causal[:, 512 - P * (t + 1):512],
                         qk=[(head(d["q"], h, P * t, P * t + P), head(d["k"], h, 0, P * (t + 1)), 0, 0)],
                         tiles=[(P * s, P, d["V"][:, s, 64 * h:64 * h + 64]) for s in range(t + 1)],
                         out=d["O"][:, t, 64 * h:64 * h + 64]) for t in range(4) for h in range(4)]

        def token_ys(O, nb, y0, **more):
            return [dict(srcs=[O[:, t, P * b:P * b + P] for b in range(nb)], y0=y0, c0=P * t, **more)
                    for t in range(4)]

        def fox_pe(pe):
            d = fox_views()
            pe_first(pe, [(PLAN[n], b) for n in ("f_v", "f_q") for b in range(2)], T2)
            for n in ("f_k", "f_small", "m_o"):
                pe_units(pe, PLAN[n], T2)
            wait_evacuated(pe, PLAN["m_o"])
            pe.wait_ge(tables_landed.sem, TB1 + 32)
            turn_pe(pe, v_jobs(d["vT"], d["V"], T2, 2))
            headnorm_pe(pe, 4, d["sq"], d["blockones"])
            sig["row_scan"].take(pe, "pe")
            spread_pe(pe, d["selneg"], d["keep"]["c"])
            turned_all(pe, "pe")
            attn_pe(pe, fox_cases(d), d["L"], d["PT"])
            yturn_pe(pe, token_ys(d["O"], 2, 0))

        def fox_act(act):
            d = fox_views()
            kp = d["keep"]
            evac_units(act, None, PLAN["f_v"], T2, d["vT"])
            for name, dst, n in (("blockones", d["blockones"], P), ("selneg", d["selneg"].rearrange("p h c -> p (h c)"),
                                                                    4 * P)):
                a = EXTRA[name][0]
                act.dma_start(dst, extra[0:dst.shape[0], a:a + n]).then_inc(tables_landed.sem, 16)
            evac_units(act, None, PLAN["f_q"], T2, d["q"])
            evac_units(act, None, PLAN["f_k"], T2, d["k"])
            for b, (dst, bias) in enumerate(((d["z"][0], "fbias"), (d["z"][1], "mfbias"), (kp["u"], "ibias"))):
                j, n = unit(PLAN["f_small"], b)
                act.wait_ge(unit_done[j], n)
                act.activation(dst, ps[0:4, 2 * j, :], ACT.Identity, bias=param(bias, 0, 4)).then_inc(acc_free[j], 1)
            for b in range(2):
                j, n = unit(PLAN["f_small"], b)
                act.wait_ge(acc_free[j], n)
                acts.by(act.activation(d["l"][b], d["z"][b], ACT.Abs))
                acts.last(act)
                acts.by(act.activation(d["l"][b], d["l"][b], ACT.Exp, scale=-1.0))
                acts.last(act)
                sig["row_log"].by(act.activation(d["l"][b], d["l"][b], ACT.Ln, bias=1.0))
            for b in range(2):
                j, n = unit(PLAN["m_o"], b)
                act.wait_ge(unit_done[j], n)
                act.activation(kp["mo"][:, b], acc(j, T2), ACT.Sigmoid).then_inc(acc_free[j], 1)
            turn_copy(act, "act", v_jobs(d["vT"], d["V"], T2, 2))
            wait_evacuated(act, PLAN["f_k"])
            headnorm_act(act, fox_norms(d), d["sq"], d["rs"])
            sig["row_done"].take(act, "act")
            acts.by(act.activation(kp["e"], kp["e"], ACT.Exp, scale=-1.0))
            acts.last(act)
            spread_act(act, d["NC"])
            attn_act(act, fox_cases(d), d["L"], d["PT"], d["small"])
            yturn_act(act, token_ys(d["O"], 2, 0), T2)

        def fox_dve(v):
            d = fox_views()
            kp = d["keep"]
            evac_units(None, v, PLAN["f_v"], T2, d["vT"])
            evac_units(None, v, PLAN["f_q"], T2, d["q"])
            evac_units(None, v, PLAN["f_k"], T2, d["k"])
            j, n = unit(PLAN["m_o"], 2)
            v.wait_ge(unit_done[j], n)
            v.tensor_copy(kp["sv"], acc(j, T2)).then_inc(acc_free[j], 1)
            dve.by(v.memset(d["one"], 1.0))
            for b, dst in enumerate((kp["c"], kp["B"])):
                sig["row_log"].take(v, "dve")
                dve.by(v.scalar_tensor_tensor(out=d["l"][b], in0=d["z"][b], scalar=0.0, in1=d["l"][b], op0=ALU.min,
                                              op1=ALU.subtract))
                dve.last(v)
                ins = v.tensor_tensor_scan(dst, d["one"], d["l"][b], 0.0, ALU.mult, ALU.add)
                (dve if b else sig["row_scan"]).by(ins)
            dve.last(v)
            j, n = unit(PLAN["f_small"], 2)
            v.wait_ge(acc_free[j], n)
            dve.by(v.tensor_tensor(kp["u"], kp["u"], kp["B"], ALU.subtract))
            dve.last(v)
            dve.by(v.tensor_tensor_scan(kp["M"], d["one"], kp["u"], 0.0, ALU.mult, ALU.max))
            dve.last(v)
            sig["row_done"].by(v.tensor_tensor(kp["e"], kp["B"], kp["M"], ALU.add))
            turn_copy(v, "dve", v_jobs(d["vT"], d["V"], T2, 2))
            headnorm_dve(v, fox_norms(d), d["rs"])
            sig["bc_copied"].take(v, "dve")
            attn_dve(v, fox_cases(d), d["L"], d["PT"], d["small"])
            yturn_dve(v, token_ys(d["O"], 2, 0), T2)

        def conv_views():
            cut = Cut()
            return dict(u=cut(2 * T2, b=2), b=cut(2 * T2, b=2), c=cut(2 * T2, b=2), z=cut(2 * (T2 + 2), b=2),
                        y=cut(2 * T2, b=2))

        def conv_pe(pe):
            for n in ("v_u", "v_b", "v_c"):
                pe_units(pe, PLAN[n], T2)

        def conv_act(act):
            d = conv_views()
            for n in "ubc":
                evac_units(act, None, PLAN["v_" + n], T2, d[n])
            for b in range(2):
                sig["cv_tmp"].take(act, "act")
                sig["cv_hi"].by(act.activation(YBLK[T2](Yh)[:, 2 + b], d["y"][:, b], ACT.Copy))

        def conv_dve(v):
            d = conv_views()
            for n in "ubc":
                evac_units(None, v, PLAN["v_" + n], T2, d[n])
            wait_evacuated(v, PLAN["v_c"])
            dve.by(v.memset(d["z"][:, :, 0:2], 0.0))
            for b in range(2):
                w = [param("conv2", 3 * b + a) for a in range(3)]
                dve.by(v.tensor_tensor(d["z"][:, b, 2:], d["c"][:, b], d["u"][:, b], ALU.mult))
                dve.last(v)
                dve.by(v.tensor_scalar(d["y"][:, b], d["z"][:, b, 2:], w[2], None, ALU.mult))
                dve.last(v)
                for a in (1, 0):
                    dve.by(v.scalar_tensor_tensor(out=d["y"][:, b], in0=d["z"][:, b, a:a + T2], scalar=w[a],
                                                  in1=d["y"][:, b], op0=ALU.mult, op1=ALU.add))
                    dve.last(v)
                sig["cv_tmp"].by(v.tensor_tensor(d["y"][:, b], d["y"][:, b], d["b"][:, b], ALU.mult))
            for b in range(2):
                sig["cv_tmp"].last(v)
                sig["cv_hi"].take(v, "dve")
                sig["cv_lo"].by(v.tensor_tensor(YBLK[T2](Yl)[:, 2 + b], d["y"][:, b],
                                                YBLK[T2](Yh)[:, 2 + b].bitcast(F32), ALU.subtract))

        M_AT = [0, 512, 896, 1152]

        def mlstm_views():
            cut = Cut()
            at = cut.at
            sq = cut(4 * 256, t=4)
            vT = Cut(at)(2 * T2, b=2)
            V = cut(4 * 4 * 65, t=4, h=4)
            q, k, NM = cut(2 * T2, b=2), cut(2 * T2, b=2), cut(4 * T2, h=4)
            AT, W, D = cut(2 * 1280, a=2), cut(2 * T2, a=2), cut(2 * P, a=2)
            H, tmp = cut(4 * 256, t=4), cut(2 * 256, a=2)
            selneg, ue, dn, rc, ss = cut(4 * P, rows=4, h=4), cut(32), cut(2), cut(2), cut(16)
            return dict(sq=sq, vT=vT, V=V, q=q, k=k, NM=NM, AT=AT, W=W, D=D, H=H, tmp=tmp, selneg=selneg, ue=ue,
                        dn=dn, rc=rc, ss=ss, keep=keep_views())

        def mlstm_turns(d):
            kp, jobs = d["keep"], []
            parts = [(kp[r][:, P * t:P * t + P], 16 * a + 4 * t) for a, r in enumerate(("u", "e")) for t in range(4)]
            jobs.append((parts, [(P, (0, 32), d["ue"])]))
            for s in range(4):
                jobs.append(([(d["vT"][:, b, P * s:P * s + P], P * b) for b in range(2)],
                             [(P, (0, 256), d["V"][:, s, :, 0:64])]))
            return jobs

        MP = [(h, s) for h in range(4) for s in range(4)]

        def mlstm_ys(d):
            return [dict(srcs=[d["H"][:, t, P * b:P * b + P] for b in range(2)], y0=4, c0=P * t, tmp=d["tmp"],
                         mult=[(param("mh", b), d["keep"]["mo"][:, b, P * t:P * t + P]) for b in range(2)])
                    for t in range(4)]

        def mlstm_pe(pe):
            d = mlstm_views()
            for n in ("m_v", "m_q", "m_k"):
                pe_units(pe, PLAN[n], T2)
            wait_evacuated(pe, PLAN["m_k"])
            pe.wait_ge(tables_landed.sem, TB1 + 48)
            spread_pe(pe, d["selneg"], d["keep"]["M"])
            turn_pe(pe, mlstm_turns(d))
            turned_all(pe, "pe")
            for h in range(5):
                for s in range(4 if h < 4 else 0):
                    n = 4 * h + s
                    if n >= 4:
                        sig["m_a"].take(pe, "pe")
                    sig["m_s"].by(pe.matmul(ps[:, n % 4, 0:512 - P * s], head(d["k"], h, P * s, P * s + P),
                                            head(d["q"], h, P * s, T2), start=True, stop=True))
                if h == 4:
                    sig["m_a"].take(pe, "pe", 4)
                for t in range(4 if h else 0):
                    n = 4 * (h - 1) + t
                    if n >= 2:
                        sig["m_read"].take(pe, "pe")
                    for s in range(t + 1):
                        a = M_AT[s] + P * (t - s)
                        mm = pe.matmul(ps[:, 4 + n % 2, 0:65], d["AT"][:, (h - 1) % 2, a:a + P], d["V"][:, s, h - 1],
                                       start=(s == 0), stop=(s == t))
                    sig["m_o"].by(mm)
            sig["m_read"].take(pe, "pe", 2)
            sig["ret_norm"].take(pe, "pe")
            yturn_pe(pe, mlstm_ys(d))

        def mlstm_act(act):
            d = mlstm_views()
            evac_units(act, None, PLAN["m_v"], T2, d["vT"])
            a = EXTRA["selneg"][0]
            act.dma_start(d["selneg"].rearrange("p h c -> p (h c)"), extra[0:4, a:a + 4 * P])\
               .then_inc(tables_landed.sem, 16)
            evac_units(act, None, PLAN["m_q"], T2, d["q"], 64 ** -0.5)
            evac_units(act, None, PLAN["m_k"], T2, d["k"])
            spread_act(act, d["NM"])
            turn_copy(act, "act", mlstm_turns(d))
            turned_all(act, "act")
            for n, (h, s) in enumerate(MP):
                sig["m_wd"].take(act, "act")
                if n >= 2:
                    sig["m_a"].take(act, "act")
                u = d["ue"][:, 4 * s + h:4 * s + h + 1]
                ins = act.activation(d["W"][:, n % 2, 0:P], d["D"][:, n % 2], ACT.Exp, bias=u)
                if s < 3:
                    ins = act.activation(d["W"][:, n % 2, P:512 - P * s], d["NM"][:, h, P * s + P:512], ACT.Exp, bias=u)
                sig["m_w"].by(ins)
            sig["m_a"].take(act, "act", 2)
            sig["m_ss"].take(act, "act")
            sig["m_std"].by(act.activation(d["ss"], d["ss"], ACT.Sqrt, bias=eps[:, 0:1], scale=1 / 64))
            yturn_act(act, mlstm_ys(d), T2)

        def mlstm_dve(v):
            d = mlstm_views()
            evac_units(None, v, PLAN["m_v"], T2, d["vT"])
            evac_units(None, v, PLAN["m_q"], T2, d["q"], 64 ** -0.5)
            evac_units(None, v, PLAN["m_k"], T2, d["k"])
            dve.by(v.memset(d["V"][:, :, :, 64:65], 1.0))
            dve.last(v)
            sig["bc_copied"].take(v, "dve")
            turn_copy(v, "dve", mlstm_turns(d))
            turned_all(v, "dve")
            for h in range(5):
                for s in range(5 if h < 4 else 0):
                    if s < 4:
                        n = 4 * h + s
                        sig["m_wd"].by(v.tensor_tensor(d["D"][:, n % 2], d["NM"][:, h, P * s:P * s + P], causalT,
                                                       ALU.add))
                    if s >= 1:
                        n, s1 = 4 * h + s - 1, s - 1
                        sig["m_w"].take(v, "dve")
                        sig["m_s"].take(v, "dve")
                        w = 512 - P * s1
                        sig["m_a"].by(v.tensor_tensor(d["AT"][:, h % 2, M_AT[s1]:M_AT[s1] + w], ps[:, n % 4, 0:w],
                                                      d["W"][:, n % 2, 0:w], ALU.mult))
                for t in range(4 if h else 0):
                    n = 4 * (h - 1) + t
                    o = ps[:, 4 + n % 2, :]
                    sig["m_o"].take(v, "dve")
                    dn, rc = d["dn"][:, n % 2:n % 2 + 1], d["rc"][:, n % 2:n % 2 + 1]
                    e = d["ue"][:, 16 + 4 * t + h - 1:17 + 4 * t + h - 1]
                    dve.by(v.tensor_scalar(dn, o[:, 64:65], -1.0, e, ALU.mult, ALU.max))
                    dve.last(v)
                    dve.by(v.tensor_tensor(dn, dn, o[:, 64:65], ALU.max))
                    dve.last(v)
                    dve.by(v.reciprocal(rc, dn))
                    dve.last(v)
                    sig["m_read"].by(v.tensor_scalar(d["H"][:, t, 64 * (h - 1):64 * h], o[:, 0:64], rc, None,
                                                     ALU.mult))
            sig["m_read"].last(v)
            Hf = d["H"].rearrange("p t (h e) -> p (t h) e", h=4)
            sqf = d["sq"].rearrange("p t (h e) -> p (t h) e", h=4)
            dve.by(v.tensor_tensor(sqf, Hf, Hf, ALU.mult))
            dve.last(v)
            sig["m_ss"].by(v.tensor_reduce(d["ss"], sqf, AX_X, ALU.add))
            sig["m_std"].take(v, "dve")
            dve.by(v.reciprocal(d["ss"], d["ss"]))
            dve.last(v)
            for n in range(16):
                ins = v.tensor_scalar(Hf[:, n], Hf[:, n], d["ss"][:, n:n + 1], None, ALU.mult)
            sig["ret_norm"].by(ins)
            yturn_dve(v, mlstm_ys(d), T2)

        def swa_views():
            cut = Cut()
            q, k = cut(4 * T2, b=4), cut(2 * T2, b=2)
            V, TB = cut(4 * P, t=4), cut(2048)
            at = cut.at
            O = cut(4 * 512, t=4)
            hank = Cut(at)(2048)
            rel, sink = cut(8, rows=33), cut(8)
            L, PT, small = cut(2 * 256, a=2), cut(2 * 256, a=2), cut(28)
            sq, rs, blockones = cut(2 * T2, a=2), cut(2 * T2, a=2), cut(P)
            w = Cut(2048)
            w = cut
            onehot, vec, flip = w(384, rows=33), w(384, rows=8), w(P)
            return dict(q=q, k=k, V=V, TB=TB.rearrange("p (h c) -> p h c", h=8), O=O, sink=sink, L=L, PT=PT,
                        small=small, sq=sq, rs=rs, blockones=blockones, keep=keep_views(),
                        tables=(rel, onehot, vec, hank, flip, TB))

        def swa_norms(d):
            return [(d["q"][:, b], param("sq"), True) for b in range(4)] + \
                   [(d["k"][:, b], param("sk"), False) for b in range(2)]

        def swa_turns(d):
            return [([(d["keep"]["sv"][:, P * s:P * s + P], 0)], [(P, (0, P), d["V"][:, s, :])]) for s in range(4)]

        def swa_cases(d):
            cases = []
            for t in range(4):
                for h in range(8):
                    k0 = max(t - 1, 0) * P
                    K = P * (t + 1) - k0
                    po = 64 * (h % 2)
                    cases.append(dict(
                        R=P, K=K, adds=[(0, 0, K, 0, d["TB"][:, h, 256 - K:256])], mask=None,
                        sink=d["sink"][:, h:h + 1],
                        qk=[(head(d["q"], h, P * t, P * t + P), d["k"][po:po + 64, h // 4, k0:k0 + K], 0, 0)],
                        tiles=[(P * a, P, d["V"][:, k0 // P + a, 64 * (h // 4):64 * (h // 4) + 64])
                               for a in range(K // P)],
                        out=d["O"][:, t, 64 * h:64 * h + 64]))
            return cases

        def swa_pe(pe):
            d = swa_views()
            for n in ("s_q", "s_k"):
                pe_units(pe, PLAN[n], T2)
            wait_evacuated(pe, PLAN["s_k"])
            tables_pe(pe, 1, d["tables"])
            pe.wait_ge(tables_landed.sem, TB1 + 80)
            turn_pe(pe, swa_turns(d))
            headnorm_pe(pe, 6, d["sq"], d["blockones"])
            turned_all(pe, "pe")
            attn_pe(pe, swa_cases(d), d["L"], d["PT"])
            yturn_pe(pe, token_ys(d["O"], 4, 6))

        def swa_act(act):
            d = swa_views()
            evac_units(act, None, PLAN["s_q"], T2, d["q"])
            a = EXTRA["blockones"][0]
            act.dma_start(d["blockones"], extra[:, a:a + P]).then_inc(tables_landed.sem, 16)
            act.dma_start(d["sink"], bass.AP(tensor=sinks.tensor, offset=0, ap=[[0, P], [1, 8]]))\
               .then_inc(tables_landed.sem, 16)
            evac_units(act, None, PLAN["s_k"], T2, d["k"])
            tables_act(act, 1, d["tables"])
            turn_copy(act, "act", swa_turns(d))
            wait_evacuated(act, PLAN["s_k"])
            headnorm_act(act, swa_norms(d), d["sq"], d["rs"])
            act.wait_ge(tables_landed.sem, TB1 + 80)
            attn_act(act, swa_cases(d), d["L"], d["PT"], d["small"])
            yturn_act(act, token_ys(d["O"], 4, 6), T2)

        def swa_dve(v):
            d = swa_views()
            evac_units(None, v, PLAN["s_q"], T2, d["q"])
            evac_units(None, v, PLAN["s_k"], T2, d["k"])
            tables_dve(v, d["tables"])
            sig["tb_copied"].take(v, "dve")
            turn_copy(v, "dve", swa_turns(d))
            headnorm_dve(v, swa_norms(d), d["rs"])
            v.wait_ge(tables_landed.sem, TB1 + 80)
            attn_dve(v, swa_cases(d), d["L"], d["PT"], d["small"])
            yturn_dve(v, token_ys(d["O"], 4, 6), T2)

        def merge_views():
            cut = Cut()
            return cut(8 * T2, b=8), cut(8 * T2, b=8), cut(3 * T2, a=3)

        def merge_groups(b):
            y, hsrc = (YBLK[T2](Yh), YBLK[T2](Yl)), (Hh, Hl)
            if b < 8:
                return [(0, hsrc, list(enumerate(range(KB))))]
            if b < 10:
                return [(0, y, [(0, 0), (1, 1)]), (1, y, [(2, 2), (3, 3)])]
            return [(0, y, [(0, 4), (1, 5)]), (1, y, [(2, 6), (3, 7), (4, 8), (5, 9)])]

        def merge_pe(pe):
            pe_units(pe, PLAN["merge"], T2, groups=merge_groups)
            y_ready.take(pe, "pe", 8)
            pe_units(pe, PLAN["merge_out"], T2, (YBLK[T2](Yh), YBLK[T2](Yl)))

        def merge_act(act):
            G, MG, _ = merge_views()
            st = PLAN["merge"]
            with loop(act, st.trips, [(sig["mg_sum"].reader("act"), 2)]) as i:
                for b in range(8):
                    j, n = unit(st, b, i)
                    act.wait_ge(unit_done[j], n)
                    act.activation(G[:, b], acc(j, T2), ACT.Sigmoid).then_inc(acc_free[j], 1)
                sig["mg_sum"].take(act, "act", 2)
            for m in range(KB):
                sig["mg_hi"].by(act.activation(YBLK[T2](Yh)[:, m], MG[:, m], ACT.Copy))

        def merge_dve(v):
            G, MG, t = merge_views()
            st = PLAN["merge"]
            with loop(v, st.trips, [(dve.made, 8), (sig["mg_sum"].made, 2)]) as i:
                for mm in range(2):
                    for a, (b, bank) in enumerate(((8 + mm, 0), (8 + mm, 1), (10 + mm, 0), (10 + mm, 1))):
                        j, n = unit(st, b, i)
                        jg, ng = unit(st, 2 * a + mm, i)
                        v.wait_ge(acc_free[jg], ng)
                        v.wait_ge(unit_done[j], n)
                        last = MG[:, bass.ds(i * 2 + mm, 1), :].rearrange("p a n -> p (a n)")
                        ins = v.tensor_tensor(t[:, min(a, 1)], ps[:, 2 * j + bank, :], G[:, 2 * a + mm], ALU.mult)
                        if bank:
                            ins.then_inc(acc_free[j], 1)
                            v.wait_ge(acc_free[j], n)
                        else:
                            dve.by(ins)
                            dve.last(v)
                        if a:
                            ins = v.tensor_tensor(t[:, 0] if a < 3 else last, t[:, 0], t[:, 1], ALU.add)
                            if a < 3:
                                dve.by(ins)
                                dve.last(v)
                            else:
                                sig["mg_sum"].by(ins)
                                sig["mg_sum"].last(v)
            sig["mg_sum"].last(v)
            for m in range(KB):
                sig["mg_hi"].take(v, "dve")
                y_ready.by(v.tensor_tensor(YBLK[T2](Yl)[:, m], MG[:, m], YBLK[T2](Yh)[:, m].bitcast(F32),
                                           ALU.subtract))
            residual_squares(v, PLAN["merge_out"], T2, META)

        @block.sync
        def _(sp):
            sp.dma_start(X[:, :, :], xT.rearrange("(b p) t -> p b t", p=P)).then_inc(start_landed, 16)
            sp.dma_start(par[:, :], params).then_inc(start_landed, 16)
            sp.dma_start(cst[:, :], consts).then_inc(start_landed, 16)

            def load(n, s):
                sp.dma_start(raw[:, s].rearrange("p k c -> p (k c)"),
                             w_all[bass.ds(n, 1)].rearrange("a p c -> (a p) c")).then_inc(raw_landed[s], 16)

            load(0, 0)
            load(1, 1)
            with sp.Fori(1, LOADS // 2) as i:
                for s in range(2):
                    sp.wait_ge(split_ready[2 * s + 1], i * 1)
                    load(i * 2 + s, s)
            wait_evacuated(sp, PLAN["ffn2_down2"])
            sp.dma_start(out.rearrange("(b p) t -> p b t", p=P), X[:, :, META:META + T2]).then_inc(out_stored, 16)
            sp.wait_ge(out_stored, 16)

        @block.gpsimd
        def _(pool):
            pool.memset(zero[:, :], 0.0).then_inc(pool_zero, 1)
            pool.memset(eps[:, 0:1], EPS).then_inc(pool_zero, 1)
            pool.memset(eps[:, 1:2], 64 * EPS).then_inc(pool_zero, 1)
            pool.wait_ge(pool_zero, 3)

            def split(i, s):
                pool.wait_ge(raw_landed[s], i * 16 + 16)
                for e in range(2):
                    j = 2 * s + e
                    src = raw[:, s, :, P * e:P * e + P]
                    if not (isinstance(i, int) and i == 0):
                        pool.wait_ge(unit_done[j], i * 1)
                    pool.tensor_tensor(wh[:, j], src, zero[:, 0:1].to_broadcast([P, KB, P]), ALU.add)\
                        .then_inc(hi_split, 1)
                    pool.wait_ge(hi_split, i * 4 + (j + 1))
                    pool.tensor_tensor(wl[:, j], src, wh[:, j].bitcast(F32), ALU.subtract).then_inc(split_ready[j], 1)

            split(0, 0)
            split(0, 1)
            with pool.Fori(1, UNITS // 4) as i:
                split(i, 0)
                split(i, 1)

        @block.tensor
        def _(pe):
            pe.wait_ge(start_landed, START)
            tables_pe(pe, 0, dsa_views()["tables"])
            norm_pe(pe, None, T1)
            dsa_pe(pe)
            for g in range(2):
                ret_pe(pe, g)
            pe_units(pe, PLAN["b_out"], T1, (YBLK[T1](Yh), YBLK[T1](Yl)))
            norm_pe(pe, PLAN["b_out"], T1)
            ffn_pe(pe, 0, T1)
            norm_pe(pe, PLAN["ffn0_down2"], T1)
            for g in range(2):
                stick_pe(pe, g)
            pe_units(pe, PLAN["c_out"], T1, (YBLK[T1](Yh), YBLK[T1](Yl)))
            norm_pe(pe, PLAN["c_out"], T1)
            ffn_pe(pe, 1, T1)
            norm_pe(pe, PLAN["ffn1_down2"], T1)
            norm_pe(pe, None, T2)
            fox_pe(pe)
            conv_pe(pe)
            mlstm_pe(pe)
            swa_pe(pe)
            sig["cv_lo"].take(pe, "pe", 2)
            merge_pe(pe)
            norm_pe(pe, PLAN["merge_out"], T2)
            ffn_pe(pe, 2, T2)

        @block.scalar
        def _(act):
            act.wait_ge(pool_zero, 3)
            act.wait_ge(start_landed, START)
            tables_act(act, 0, dsa_views()["tables"])
            squares_act(act, T1, 0)
            norm_act(act, T1, True)
            dsa_act(act)
            for g in range(2):
                ret_act(act, g)
            squares_act(act, T1, 0, PLAN["b_out"])
            norm_act(act, T1, True, ACT.Silu)
            ffn_act(act, 0, T1)
            squares_act(act, T1, 0, PLAN["ffn0_down2"])
            norm_act(act, T1, True)
            for g in range(2):
                stick_act(act, g)
            squares_act(act, T1, 0, PLAN["c_out"])
            norm_act(act, T1, True, ACT.Silu)
            ffn_act(act, 1, T1)
            squares_act(act, T1, 0, PLAN["ffn1_down2"])
            norm_act(act, T1, False)
            squares_act(act, T2, META)
            norm_act(act, T2, True)
            fox_act(act)
            conv_act(act)
            mlstm_act(act)
            swa_act(act)
            merge_act(act)
            squares_act(act, T2, META, PLAN["merge_out"])
            norm_act(act, T2, True, ACT.Silu)
            ffn_act(act, 2, T2)

        @block.vector
        def _(v):
            v.wait_ge(start_landed, START)
            tables_dve(v, dsa_views()["tables"])
            sig["tb_copied"].take(v, "dve")
            squares_alone(v, T1)
            norm_dve(v, T1, 0, "g_mix0", True)
            dsa_dve(v)
            for g in range(2):
                ret_dve(v, g)
            residual_squares(v, PLAN["b_out"], T1, 0)
            norm_dve(v, T1, 0, "g_ffn0", True)
            ffn_dve(v, 0, T1, 0)
            norm_dve(v, T1, 0, "g_mix1", True)
            for g in range(2):
                stick_dve(v, g)
            residual_squares(v, PLAN["c_out"], T1, 0)
            norm_dve(v, T1, 0, "g_ffn1", True)
            ffn_dve(v, 1, T1, 0)
            norm_dve(v, T1, 0, "g_final", False)
            sig["stage_dve"].last(v)
            squares_alone(v, T2)
            norm_dve(v, T2, META, "g_attn", True)
            fox_dve(v)
            conv_dve(v)
            mlstm_dve(v)
            swa_dve(v)
            merge_dve(v)
            norm_dve(v, T2, META, "g_ffn2", True)
            ffn_dve(v, 2, T2, META)


def bucket(n):
    n = np.maximum(n, 0)
    large = 16 + (np.log(np.maximum(n, 1).astype(np.float32) / np.float32(16)) / np.float32(np.log(8.0))
                  * np.float32(16)).astype(np.int32)
    return np.where(n < 16, n, np.minimum(large, 31))


def const_arrays():
    c = np.zeros((P, NCONST), np.float32)
    e = np.zeros((P, NEXTRA), np.float32)
    p, f = np.arange(P)[:, None], np.arange(P)[None, :]

    def put(a, table, name, v):
        at = table[name][0]
        a[:v.shape[0], at:at + v.shape[1]] = v

    put(c, CONSTS, "ident", (p == f).astype(np.float32))
    put(c, CONSTS, "ones", np.ones((P, P), np.float32))
    put(c, CONSTS, "causal", np.concatenate([np.zeros((P, 384)), np.where(f > p, NEG, 0.0)], 1))
    put(c, CONSTS, "causalT", np.where(p > f, NEG, 0.0))
    put(e, EXTRA, "flip", (p + f == P - 1).astype(np.float32))
    put(e, EXTRA, "cap", np.where(f <= p, CAP, -CAP))
    put(e, EXTRA, "blockones", (p // 64 == f // 64).astype(np.float32))
    put(e, EXTRA, "strictT", np.where(p >= f, NEG, 0.0))
    put(e, EXTRA, "strictmul", (p < f).astype(np.float32))
    put(e, EXTRA, "ntri", np.where(p >= f, -1.0, 0.0))
    put(e, EXTRA, "nones", -np.ones((P, P)))
    put(e, EXTRA, "rot", np.where(p == f + 64, -1.0, 0.0) + np.where(p + 64 == f, 1.0, 0.0))
    half = 64
    inv = (1.0 / (np.float32(10000.0) ** (np.arange(half, dtype=np.float32) / half))).astype(np.float32)
    ang = (np.arange(T1, dtype=np.float32)[:, None] * inv[None, :]).astype(np.float64).T
    put(e, EXTRA, "cos", np.concatenate([np.cos(ang)] * 2, 0))
    put(e, EXTRA, "sin", np.concatenate([np.sin(ang)] * 2, 0))
    diff = np.arange(T1)[None, :] - p
    decay = [np.where(diff >= 0, np.exp(np.maximum(diff, 0) * np.log(1.0 - 2.0 ** (-5.0 - h))), 0.0) * P ** -0.5
             for h in range(4)]
    put(e, EXTRA, "decay", np.concatenate(decay, 1))
    put(e, EXTRA, "selneg", np.concatenate([np.where(np.arange(4)[:, None] == h, -1.0, 0.0) * np.ones((4, P))
                                            for h in range(4)], 1))
    dist = 255 - np.arange(384)
    b = np.arange(32)[:, None]
    hot = (bucket(dist)[None, :] == b) & (np.arange(384) < 383)[None, :]
    put(e, EXTRA, "onehot1", hot.astype(np.float32))
    valid = ((dist >= 0) & (dist < 128))[None, :]
    put(e, EXTRA, "onehot2", np.concatenate([hot & valid, ~valid], 0).astype(np.float32))
    return c, e


def lay_weights(a):
    wide = np.zeros((UNITS, P, KB, P), np.float32)
    at = [0]

    def put(cols_):
        k = -(-cols_.shape[0] // P)
        wide[at[0], :, 0:k, 0:cols_.shape[1]] = cols_.reshape(k, P, cols_.shape[1]).transpose(1, 0, 2)
        at[0] += 1

    def many(w, c0, n):
        for m in range(n):
            put(w[:, c0 + P * m:c0 + P * m + P])

    def ffn(up, gate, down):
        for m0, n in CHUNKS:
            for i in range(n // 2):
                c = P * (m0 + 2 * i)
                many(gate, c, 2)
                many(up, c, 2)
            many(down[P * m0:P * (m0 + n)], 0, 8)

    w = a["even_w_in"][0]
    many(w, 1024, 4), many(w, 0, 4), many(w, 512, 4), many(w, 1536, 4)
    put(np.concatenate([w[:, 2048:2112]] * 2, 1)), put(w[:, 2112:2120])
    many(a["even_w_out"][0][0:512], 0, 8)
    for g in range(2):
        many(w, 2120 + 256 * g, 2), many(w, 2632 + 256 * g, 2), many(w, 3144 + 512 * g, 4), many(w, 4168 + 512 * g, 4)
    many(a["even_w_out"][0][512:], 0, 8)
    ffn(a["ffn_w_up"][0], a["ffn_w_gate"][0], a["ffn_w_down"][0])
    w = a["odd_w_in"][0]
    for g in range(2):
        many(w, 2048 + 512 * g, 4), many(w, 512 * g, 4), many(w, 1024 + 512 * g, 4)
    many(a["odd_w_out"][0], 0, 8)
    ffn(a["ffn_w_up"][1], a["ffn_w_gate"][1], a["ffn_w_down"][1])
    w = a["w_in_2"][0]
    many(w, 512, 2), many(w, 0, 2), many(w, 256, 2)
    put(w[:, 768:772]), put(w[:, 2312:2316]), put(w[:, 2308:2312])
    many(w, 2316, 2), many(w, 3212, 1)
    many(w, 772, 2), many(w, 1028, 2), many(w, 1284, 2)
    many(w, 2052, 2), many(w, 1540, 2), many(w, 1796, 2)
    many(w, 2572, 4)
    for g in range(2):
        put(np.concatenate([w[:, 3084 + 64 * g:3148 + 64 * g]] * 2, 1))
    first = np.concatenate([a["w_fox_out_2"][0], a["w_conv_out_2"][0]], 0)
    second = np.concatenate([a["w_mlstm_out_2"][0], a["w_swa_out_2"][0]], 0)
    for i in range(4):
        for b in range(4):
            many(w, 3340 + 1024 * b + 256 * i, 2)
        many(first, 256 * i, 2), many(second, 256 * i, 2)
    many(a["w_merge_out_2"][0], 0, 8)
    ffn(a["w_up_2"][0], a["w_gate_2"][0], a["w_down_2"][0])
    assert at[0] == UNITS
    wide = wide.reshape(LOADS, 2, P, KB, P).transpose(0, 2, 3, 1, 4)
    return np.ascontiguousarray(wide).reshape(LOADS, P, KB * 2 * P)


def lay_small(a):
    par = np.zeros((P, NPARAM), np.float32)

    def put(name, v):
        at = PARAMS[name][0]
        par[:v.shape[0], at:at + v.shape[1]] = v

    blocks = lambda v: v.reshape(-1, P).T
    put("g_mix0", blocks(a["norm_mix"][0])), put("g_mix1", blocks(a["norm_mix"][1]))
    put("g_ffn0", blocks(a["norm_ffn"][0])), put("g_ffn1", blocks(a["norm_ffn"][1]))
    put("g_final", blocks(a["norm_final"])), put("g_attn", blocks(a["attn_norm_2"][0]))
    put("g_ffn2", blocks(a["ffn_norm_2"][0])), put("gn", blocks(a["even_gn_gain"][0]))
    for l in range(2):
        w = np.concatenate([a["ffn_conv_w"][l], a["ffn_conv_b"][l][None]], 0)
        put(f"conv{l}", w.reshape(4, FB, P).transpose(2, 1, 0).reshape(P, 4 * FB))
    put("conv2", a["conv_w_2"][0].reshape(3, 2, P).transpose(2, 1, 0).reshape(P, 6))
    for name, src in (("fq", "fox_q_gain_2"), ("fk", "fox_k_gain_2"), ("sq", "swa_q_gain_2"), ("sk", "swa_k_gain_2")):
        put(name, np.concatenate([a[src][0]] * 2)[:, None])
    put("mh", blocks(a["mlstm_h_gain_2"][0]))
    put("fbias", a["fox_f_bias_2"][0][:, None]), put("ibias", a["mlstm_i_bias_2"][0][:, None])
    put("mfbias", a["mlstm_f_bias_2"][0][:, None])
    return par


def kernel(**inputs):
    import concourse.bacc as bacc
    from concourse.bass_utils import run_bass_kernel_spmd as run

    a = {k: np.asarray(v) for k, v in inputs.items()}
    consts, extra = const_arrays()
    arrays = {
        "xT": np.ascontiguousarray(np.concatenate([a["meta_tokens"], a["x"][0]], 0).T),
        "w_all": lay_weights(a), "params": lay_small(a), "consts": consts, "extra": extra,
        "sinks": np.ascontiguousarray(a["swa_sinks_2"]), "relb1": np.ascontiguousarray(a["rel_bias"]),
        "relb2": np.ascontiguousarray(a["rel_bias_2"]),
    }
    nc = bacc.Bacc("TRN2", target_bir_lowering=False, num_devices=1)
    h = {k: nc.dram_tensor("in_" + k, v.shape, F32, kind="ExternalInput").ap() for k, v in arrays.items()}
    scratch = nc.dram_tensor("scratch", [2, 8, 384], F32, kind="Internal").ap()
    out = nc.dram_tensor("out", [D, T2], F32, kind="ExternalOutput").ap()
    program(nc, h["xT"], h["w_all"], h["params"], h["consts"], h["extra"], h["sinks"], h["relb1"], h["relb2"], scratch,
            out)
    r = run(nc, [{"in_" + k: v for k, v in arrays.items()}], core_ids=[0]).results[0]["out"]
    return np.ascontiguousarray(r.T)[None]
```

```python
from contextlib import ExitStack, contextmanager

import numpy as np
import concourse.bass as bass
from concourse import mybir

F32 = mybir.dt.float32
F32R = mybir.dt.float32r
ALU = mybir.AluOpType
ACT = mybir.ActivationFunctionType
AX_X = mybir.AxisListType.X

P = 128
D = 1024
KB = D // P
META = 16
SEQ = 512
T1 = META + SEQ
T2 = SEQ
DFF = 2816
FB = DFF // P
CHUNKS = [(0, 8), (8, 8), (16, 6)]
EPS = 1e-6
KEEP = 128
NEG = -1e30
CAP = 3.0e38
TAKEN = -3.4e38
TAKEN_LIMIT = -3.2e38
START = 3 * 16
LOADS_UNITS = 2


class Count:

    def __init__(self):
        self.n, self.i, self.per, self.start = 0, None, 0, 0

    def enter(self, i, per):
        self.i, self.per, self.start = i, per, self.n

    def leave(self, trips):
        assert self.n - self.start == self.per, (self.n, self.start, self.per)
        self.n, self.i = self.start + self.per * trips, None

    def value(self):
        return self.n if self.i is None else self.i * self.per + self.n

    def step(self, k=1):
        self.n += k
        return self.value()


class Signal:

    def __init__(self, sem):
        self.sem, self.made, self.read = sem, Count(), {}

    def by(self, ins, k=1):
        ins.then_inc(self.sem, k)
        self.made.step(k)

    def reader(self, who):
        return self.read.setdefault(who, Count())

    def take(self, eng, who, k=1):
        eng.wait_ge(self.sem, self.reader(who).step(k))

    def last(self, eng):
        eng.wait_ge(self.sem, self.made.value())


class Stage:
    def __init__(self, name, first, units, trips=1):
        self.name, self.first, self.units, self.trips = name, first, units, trips
        self.advance = units // 4 if trips > 1 else 0
        assert trips == 1 or units % 4 == 0
        self.end = first + units * trips


def make_plan():
    plan, at = {}, 0

    def add(name, units, trips=1):
        nonlocal at
        plan[name] = Stage(name, at, units, trips)
        at += units * trips

    add("a_v", 4)
    add("a_q", 4), add("a_k", 4), add("a_iq", 4)
    add("a_small", 2)
    add("a_out", 4, 2)
    for g in range(2):
        add(f"b_q{g}", 2), add(f"b_k{g}", 2), add(f"b_v{g}", 4), add(f"b_g{g}", 4)
    add("b_out", 4, 2)
    for l in range(3):
        if l == 1:
            for g in range(2):
                add(f"c_v{g}", 4), add(f"c_q{g}", 4), add(f"c_k{g}", 4)
            add("c_out", 4, 2)
        if l == 2:
            add("f_v", 2), add("f_q", 2), add("f_k", 2), add("f_small", 3), add("m_o", 3)
            add("v_u", 2), add("v_b", 2), add("v_c", 2)
            add("m_v", 2), add("m_q", 2), add("m_k", 2)
            add("s_q", 4), add("s_k", 2)
            add("merge", 12, 4)
            add("merge_out", 4, 2)
        for c, (_, n) in enumerate(CHUNKS):
            add(f"ffn{l}_up{c}", 4, n // 2)
            add(f"ffn{l}_down{c}", 4, 2)
    plan["total"] = at
    return plan


PLAN = make_plan()
UNITS = PLAN["total"]
LOADS = UNITS // LOADS_UNITS

PARAMS = {}


def lay_params():
    at = 0
    for name, cols in (("g_mix0", 8), ("g_ffn0", 8), ("g_mix1", 8), ("g_ffn1", 8), ("g_final", 8), ("g_attn", 8),
                       ("g_ffn2", 8), ("gn", 8), ("conv0", 4 * FB), ("conv1", 4 * FB), ("conv2", 6), ("fq", 1),
                       ("fk", 1), ("sq", 1), ("sk", 1), ("mh", 2), ("fbias", 1), ("ibias", 1), ("mfbias", 1)):
        PARAMS[name] = (at, cols)
        at += cols
    return at


NPARAM = lay_params()
CONSTS = {"ident": (0, 128), "ones": (128, 128), "causal": (256, 512), "causalT": (768, 128)}
NCONST = 896
EXTRA = {"flip": (0, 128), "cap": (128, 128), "blockones": (256, 128), "strictT": (384, 128), "strictmul": (512, 128),
         "ntri": (640, 128), "nones": (768, 128), "rot": (896, 128), "cos": (1024, 528), "sin": (1552, 528),
         "decay": (2080, 4 * 528), "selneg": (4192, 512), "onehot1": (4704, 384), "onehot2": (5088, 384)}
NEXTRA = 5472

KEYTILE = [(s, min(P, T1 - P * s)) for s in range(5)]
PIECES = [(4, 512, 528), (3, 384, 528), (2, 256, 528), (1, 128, 528), (0, 264, 528), (0, 0, 264)]
TILE_AT = [0, 528, 928, 1200, 1344]
TRI = 1360


def program(nc, xT, w_all, params, consts, extra, sinks, relb1, relb2, scratch, out):
    ctx = ExitStack()
    with ctx:
        def sb(name, shape, dt=F32):
            return ctx.enter_context(nc.sbuf_tensor(name, shape, dt))

        def sem(name):
            return ctx.enter_context(nc.semaphore(name))

        def signal(name):
            return Signal(sem(name))

        ps = ctx.enter_context(nc.psum_tensor("ps", [P, 8, 512], F32))
        X = sb("X", [P, KB, T1])
        Hh, Hl = sb("Hh", [P, KB, T1], F32R), sb("Hl", [P, KB, T1], F32R)
        Yh, Yl = sb("Yh", [P, 10 * 512], F32R), sb("Yl", [P, 10 * 512], F32R)
        raw = sb("raw", [P, 2, KB, 256])
        wh, wl = sb("wh", [P, 4, KB, P], F32R), sb("wl", [P, 4, KB, P], F32R)
        par = sb("par", [P, NPARAM])
        cst = sb("cst", [P, NCONST])
        zero = sb("zero", [P, 1])
        eps = sb("eps", [P, 2])
        ARENA = 16700
        with nc.sbuf_tensor("arena_r", [P, ARENA], F32R) as arena_r:
            pass
        arena = sb("arena", [P, ARENA])

        def param(name, c=0, rows=P):
            a = PARAMS[name][0] + c
            return par[0:rows, a:a + 1]

        def const(name):
            a, n = CONSTS[name]
            return cst[:, a:a + n]

        ident, ones, causal, causalT = (const(n) for n in ("ident", "ones", "causal", "causalT"))

        class Cut:
            def __init__(self, at=0, arena=arena):
                self.at, self.arena = at, arena

            def __call__(self, words, rows=P, **dims):
                v = self.arena[0:rows, self.at:self.at + words]
                self.at += words
                assert self.at <= ARENA, self.at
                if dims:
                    k = list(dims)
                    v = v.rearrange(f"p ({' '.join(k)} z) -> p {' '.join(k)} z", **dims)
                return v

        raw_landed = [sem(f"raw_landed{s}") for s in range(2)]
        hi_split = sem("hi_split")
        split_ready = [sem(f"split_ready{j}") for j in range(4)]
        unit_done = [sem(f"unit_done{j}") for j in range(4)]
        acc_free = [sem(f"acc_free{j}") for j in range(4)]
        start_landed = sem("start_landed")
        dve = signal("dve_chain")
        acts = signal("act_chain")
        pool_zero = sem("pool_zero")
        h_ready = signal("h_ready")
        y_ready = signal("y_ready")
        sq_made, sq_used, rms_sum, rms_std = (signal(n) for n in ("sq_made", "sq_used", "rms_sum", "rms_std"))
        n_tmp, n_hi = signal("n_tmp"), signal("n_hi")
        tables_landed = signal("tables_landed")
        out_stored = sem("out_stored")
        b_landed, v_written = sem("b_landed"), sem("v_written")

        sig = {n: signal(n) for n in (
            "g_conv", "g_silu", "prod_hi", "scores", "scores_read", "logits", "probs", "turned", "turn_copied",
            "pv", "pv_read", "recip", "yt", "yt_tmp", "yt_hi", "yt_lo", "cv_tmp", "cv_hi", "cv_lo", "idx",
            "idx_relu", "idx_added", "z_made", "z_log", "alone_made", "alone_summed", "z_exp", "l_made", "cum",
            "a_diag", "a_exp", "oT_copied", "oT_hi", "oT_lo", "rot_made", "rot_done", "ret_s", "ret_a", "ret_o",
            "ret_copied", "ret_var", "ret_std", "hn_sq", "hn_sum", "hn_std", "hn_done", "v_made", "v_copied",
            "tb_made", "tb_copied", "row_log", "row_scan", "bc_made", "bc_copied", "m_w", "m_wd", "m_s", "m_a",
            "m_o", "m_read", "m_ss", "m_std", "mg_sum", "mg_hi", "memset_done", "stage_dve", "o_used",
            "ret_norm", "row_done")}
        turn_done = [signal(f"turn_done{q}") for q in range(2)]
        turn_out = [signal(f"turn_out{q}") for q in range(2)]
        turn_count = {}
        block = ctx.enter_context(nc.Block())

        @contextmanager
        def loop(eng, trips, counts):
            with eng.Fori(0, trips) as i:
                for c, per in counts:
                    c.enter(i, per)
                yield i
            for c, _ in counts:
                c.leave(trips)

        def halves(T):
            return [(0, 264), (264, 528)] if T == T1 else [(0, 512)]

        def unit(stage, b, i=0):
            u = stage.first + b
            return u % 4, i * stage.advance + (u // 4 + 1)

        def acc(j, T):
            return ps[:, 2 * j:2 * j + 2, 0:264] if T == T1 else ps[:, 2 * j, :]

        def cols(ap, T):
            return ap.rearrange("p (h n) -> p h n", h=2) if T == T1 else ap

        def wait_evacuated(eng, stage):
            for j in range(4):
                eng.wait_ge(acc_free[j], (stage.end - j + 3) // 4)

        def pe_first(pe, units, T):
            for group in [(k, units[:3]) for k in range(KB)] + [(k, units[3:]) for k in range(KB)]:
                k = group[0]
                if len(group[1]) == 3:
                    h_ready.take(pe, "pe")
                for stage, b in group[1]:
                    j, n = unit(stage, b)
                    if k == 0:
                        pe.wait_ge(split_ready[j], n)
                        if stage.first + b >= 4:
                            pe.wait_ge(acc_free[j], n - 1)
                    for part, (w, x) in enumerate(((wh, Hh), (wh, Hl), (wl, Hh))):
                        for h, (c0, c1) in enumerate(halves(T)):
                            mm = pe.matmul(ps[:, 2 * j + h, 0:c1 - c0], w[:, j, k, :], x[:, k, c0:c1],
                                           start=(k == 0 and part == 0), stop=(k == KB - 1 and part == 2))
                    if k == KB - 1:
                        mm.then_inc(unit_done[j], 1)

        def pe_units(pe, stage, T, src=None, blocks=tuple(range(KB)), groups=None, only=None, start=0, ready=None):
            sh, sl = src if src else (Hh, Hl)

            def body(i):
                for b in (range(stage.units) if only is None else only):
                    j, n = unit(stage, b, i)
                    pe.wait_ge(split_ready[j], n)
                    if stage.first + b >= 4:
                        pe.wait_ge(acc_free[j], n - 1)
                    gs = groups(b) if groups else [(0, (sh, sl), list(enumerate(blocks)))]
                    for bank, (sh_, sl_), ks in gs:
                        for at, (k, blk) in enumerate(ks):
                            if ready is not None and b == 0:
                                pe.wait_ge(y_ready.sem, ready + k + 1)
                            for part, (w, x) in enumerate(((wh, sh_), (wh, sl_), (wl, sh_))):
                                for h, (c0, c1) in enumerate(halves(T)):
                                    mm = pe.matmul(ps[:, 2 * j + h + bank, 0:c1 - c0], w[:, j, k, :],
                                                   x[:, blk, c0:c1], start=(at == 0 and part == 0),
                                                   stop=(at == len(ks) - 1 and part == 2))
                    mm.then_inc(unit_done[j], 1)

            if stage.trips == 1:
                body(0)
            else:
                with pe.Fori(start, stage.trips) as i:
                    body(i)

        def evac_units(act, dve_, stage, T, dst, scale=1.0, func=ACT.Copy, base=0, only=None):
            for b in (range(stage.units) if only is None else only):
                j, n = unit(stage, b)
                mine = act is not None if (func != ACT.Copy or b % 2 == 0) else dve_ is not None
                if not mine:
                    continue
                eng = act or dve_
                eng.wait_ge(unit_done[j], n)
                o = cols(dst[:, b - base, :], T)
                if act is not None:
                    ins = act.activation(o, acc(j, T), func, scale=scale)
                else:
                    ins = dve_.tensor_scalar(o, acc(j, T), scale, None, ALU.mult)
                ins.then_inc(acc_free[j], 1)

        def residual_units(v, stage, T, off):
            with v.Fori(0, stage.trips) as i:
                for b in range(stage.units):
                    residual_unit(v, stage, T, off, i, b)

        def residual_unit(v, stage, T, off, i, b):
            j, n = unit(stage, b, i)
            v.wait_ge(unit_done[j], n)
            x = X[:, bass.ds(i * 4 + b, 1), off:off + T]
            x = x.rearrange("p a (h n) -> p (a h) n", h=2) if T == T1 else x.rearrange("p a n -> p (a n)")
            v.tensor_tensor(x, acc(j, T), x, ALU.add).then_inc(acc_free[j], 1)

        YBLK = {T: (lambda part, T=T: part[:, 0:(KB if T == T1 else 10) * T].rearrange("p (b t) -> p b t", t=T))
                for T in (T1, T2)}

        def norm_views(T):
            cut = Cut()
            return cut(4 * T, a=4), cut(T), cut(T), cut(2 * T, a=2)

        def squares_alone_act(act, T, off):
            sq = norm_views(T)[0]
            for b in range(KB):
                if off == META:
                    sig["stage_dve"].take(act, "act")
                if b >= 4:
                    sig["alone_summed"].take(act, "act")
                sig["alone_made"].by(act.activation(sq[:, b % 4], X[:, b, off:off + T], ACT.Square))
            act.preload_act_table_set("natural_log_exp_and_others")
            sig["alone_summed"].take(act, "act", 4)

        def squares_alone_pe(pe, T):
            sq = norm_views(T)[0]
            for b in range(KB):
                sig["alone_made"].take(pe, "pe")
                for h, (c0, c1) in enumerate(halves(T)):
                    mm = pe.matmul(ps[:, h, 0:c1 - c0], ones, sq[:, b % 4, c0:c1], start=(b == 0), stop=(b == KB - 1))
                sig["alone_summed"].by(mm)

        def squares_act(act, T, off, stage):
            sq = norm_views(T)[0]
            with loop(act, 2, [(sq_made.made, 4), (sq_used.reader("act"), 4)]) as i:
                for b in range(4):
                    j, n = unit(stage, b, i)
                    act.wait_ge(acc_free[j], n)
                    x = X[:, bass.ds(i * 4 + b, 1), off:off + T].rearrange("p a n -> p (a n)")
                    sq_made.by(act.activation(sq[:, b], x, ACT.Square))
                sq_used.take(act, "act", 4)
            act.preload_act_table_set("natural_log_exp_and_others")

        def rsqrt(act, done, dst, src, bias, scale):
            acts.by(act.activation(dst, src, ACT.Ln, bias=bias, scale=scale))
            acts.last(act)
            done.by(act.activation(dst, dst, ACT.Exp, scale=-0.5))

        def squares_dve(v, T, b):
            sq, total, _, _ = norm_views(T)
            sq_made.take(v, "dve")
            sq_used.by(v.tensor_tensor(total, total, sq[:, b], ALU.add))
            sq_used.last(v)

        def residual_squares(v, stage, T, off):
            j, n = unit(stage, 0)
            v.wait_ge(unit_done[j], n)
            dve.by(v.memset(norm_views(T)[1], 0.0))
            dve.last(v)
            with loop(v, stage.trips, [(sq_made.reader("dve"), 4), (sq_used.made, 4)]) as i:
                for b in range(5):
                    if b < 4:
                        residual_unit(v, stage, T, off, i, b)
                    if b:
                        squares_dve(v, T, b - 1)

        def norm_act(act, T, split, then=None, root=False, alone=False):
            _, _, rs, tmp = norm_views(T)
            if not alone:
                rms_sum.take(act, "act")
            if root:
                rms_std.by(act.activation(cols(rs, T), acc(0, T), ACT.Sqrt, bias=eps[:, 0:1], scale=1.0 / D))
            else:
                rsqrt(act, rms_std, cols(rs, T), acc(0, T), eps[:, 0:1], 1.0 / D)
            if then is not None:
                act.preload_act_table(then)
            if split:
                for k in range(KB):
                    n_tmp.take(act, "act")
                    n_hi.by(act.activation(Hh[:, k, 0:T], tmp[:, k % 2], ACT.Copy))

        def norm_pe(pe, prev, T):
            wait_evacuated(pe, prev)
            sq_used.take(pe, "pe", KB)
            for h, (c0, c1) in enumerate(halves(T)):
                mm = pe.matmul(ps[:, h, 0:c1 - c0], ones, norm_views(T)[1][:, c0:c1], start=True, stop=True)
            rms_sum.by(mm)

        def norm_dve(v, T, off, gain, split, root=False):
            _, _, rs, tmp = norm_views(T)
            rms_std.take(v, "dve")
            if root:
                dve.by(v.reciprocal(rs, rs))
                dve.last(v)
            for k in range(KB + 1):
                if k < KB:
                    x = X[:, k, off:off + T]
                    if split and k >= 2:
                        h_ready.last(v)
                    ins = v.scalar_tensor_tensor(out=tmp[:, k % 2] if split else x, in0=x, scalar=param(gain, k),
                                                 in1=rs, op0=ALU.mult, op1=ALU.mult)
                    (n_tmp if split else sig["stage_dve"]).by(ins)
                if k >= 1 and split:
                    n_hi.take(v, "dve")
                    h_ready.by(v.tensor_tensor(Hl[:, k - 1, 0:T], tmp[:, (k - 1) % 2],
                                               Hh[:, k - 1, 0:T].bitcast(F32), ALU.subtract))

        def ffn_views(T):
            cut = Cut()
            return cut(2 * (T + 2), a=2), cut(2 * T, a=2), cut(2 * T, a=2), cut(2 * T, a=2)

        def ffn_act(act, l, T):
            gs, c1, sg, t = ffn_views(T)
            conv = l < 2
            for c, (m0, n) in enumerate(CHUNKS):
                st = PLAN[f"ffn{l}_up{c}"]
                counts = [(sig["prod_hi"].made, 2)]
                if conv:
                    counts += [(sig["g_conv"].reader("act"), 2), (sig["g_silu"].made, 2)]
                with loop(act, n // 2, counts) as i:
                    for mm in range(2):
                        j, k = unit(st, mm, i)
                        act.wait_ge(unit_done[j], k)
                        if conv:
                            act.activation(cols(gs[:, mm, 2:], T), acc(j, T), ACT.Copy).then_inc(acc_free[j], 1)
                        else:
                            act.activation(cols(sg[:, mm], T), acc(j, T), ACT.Silu).then_inc(acc_free[j], 1)
                    if conv:
                        for mm in range(2):
                            sig["g_conv"].take(act, "act")
                            sig["g_silu"].by(act.activation(sg[:, mm], c1[:, mm], ACT.Silu))
                    for mm in range(2):
                        j, k = unit(st, 2 + mm, i)
                        act.wait_ge(acc_free[j], k)
                        sig["prod_hi"].by(act.activation(
                            YBLK[T](Yh)[:, bass.ds(i * 2 + mm, 1), :].rearrange("p a n -> p (a n)"), t[:, mm], ACT.Copy))

        def ffn_dve(v, l, T, off):
            gs, c1, sg, t = ffn_views(T)
            conv = l < 2
            for c, (m0, n) in enumerate(CHUNKS):
                st = PLAN[f"ffn{l}_up{c}"]
                counts = [(sig["prod_hi"].reader("dve"), 2), (y_ready.made, 2)]
                if conv:
                    counts += [(sig["g_silu"].reader("dve"), 2), (sig["g_conv"].made, 2), (dve.made, 4)]
                if conv and c == 0:
                    dve.by(v.memset(gs[:, :, 0:2], 0.0))
                    dve.last(v)
                with loop(v, n // 2, counts) as i:
                    if conv:
                        pa = PARAMS[f"conv{l}"][0]
                        w = [[par[:, bass.ds(i * 8 + (pa + 4 * (m0 + mm) + q), 1)] for q in range(4)]
                             for mm in range(2)]
                        for mm in range(2):
                            j, k = unit(st, mm, i)
                            v.wait_ge(acc_free[j], k)
                            dve.by(v.tensor_scalar(c1[:, mm], gs[:, mm, 2:], w[mm][2], w[mm][3], ALU.mult, ALU.add))
                            dve.last(v)
                            dve.by(v.scalar_tensor_tensor(out=c1[:, mm], in0=gs[:, mm, 1:T + 1], scalar=w[mm][1],
                                                          in1=c1[:, mm], op0=ALU.mult, op1=ALU.add))
                            dve.last(v)
                            sig["g_conv"].by(v.scalar_tensor_tensor(out=c1[:, mm], in0=gs[:, mm, 0:T],
                                                                    scalar=w[mm][0], in1=c1[:, mm], op0=ALU.mult,
                                                                    op1=ALU.add))
                    for mm in range(2):
                        if not conv:
                            j, k = unit(st, mm, i)
                            v.wait_ge(acc_free[j], k)
                        else:
                            sig["g_silu"].take(v, "dve")
                        j, k = unit(st, 2 + mm, i)
                        v.wait_ge(unit_done[j], k)
                        v.tensor_tensor(cols(t[:, mm], T), acc(j, T), cols(sg[:, mm], T), ALU.mult)\
                         .then_inc(acc_free[j], 1)
                    for mm in range(2):
                        j, k = unit(st, 2 + mm, i)
                        v.wait_ge(acc_free[j], k)
                        sig["prod_hi"].take(v, "dve")
                        yb = bass.ds(i * 2 + mm, 1)
                        y_ready.by(v.tensor_tensor(YBLK[T](Yl)[:, yb, :].rearrange("p a n -> p (a n)"), t[:, mm],
                                                   YBLK[T](Yh)[:, yb, :].rearrange("p a n -> p (a n)").bitcast(F32),
                                                   ALU.subtract))
                    y_ready.last(v)
                last = c == len(CHUNKS) - 1 and l < 2
                (residual_squares if last else residual_units)(v, PLAN[f"ffn{l}_down{c}"], T, off)

        def ffn_pe(pe, l, T):
            pe_first(pe, [(PLAN[f"ffn{l}_up0"], b) for b in range(4)], T)
            for c, (m0, n) in enumerate(CHUNKS):
                pe_units(pe, PLAN[f"ffn{l}_up{c}"], T, start=(c == 0))
                before = y_ready.reader("pe").value()
                pe_units(pe, PLAN[f"ffn{l}_down{c}"], T, (YBLK[T](Yh), YBLK[T](Yl)), tuple(range(n)), ready=before)
                y_ready.take(pe, "pe", n)

        def turn_pe(pe, jobs):
            for n, (parts, _) in enumerate(jobs):
                q = n % 2
                if turn_done[q].made.value():
                    turn_out[q].take(pe, "pe")
                for src, col in parts:
                    p, f = src.shape
                    mm = flip_over(pe, ps[0:f, 6 + q, col:col + p], src)
                turn_done[q].by(mm)

        def flip_over(pe, dst, src):
            p, f = src.shape
            if f == P and p == P:
                return pe.transpose(dst, src, ident)
            return pe.matmul(dst, src, ident[0:p, 0:p], start=True, stop=True)

        def turned_all(eng, who):
            for q in range(2):
                n = turn_done[q].made.value() if who == "pe" else turn_count[who][q]
                if n:
                    eng.wait_ge(turn_out[q].sem, n)

        def turn_copy(eng, who, jobs, scale=1.0):
            c = turn_count.setdefault(who, [0, 0])
            for n, (_, copies) in enumerate(jobs):
                q = n % 2
                c[q] += 1
                if (who == "act") != (q == 0):
                    continue
                eng.wait_ge(turn_done[q].sem, c[q])
                for a, (rows, bank_cols, dst) in enumerate(copies):
                    src = ps[0:rows, 6 + q, bank_cols[0]:bank_cols[1]]
                    if len(dst.shape) == 3:
                        src = src.rearrange("p (a b) -> p a b", a=dst.shape[1])
                    if who == "act":
                        ins = eng.activation(dst, src, ACT.Copy, scale=scale)
                    else:
                        ins = eng.tensor_scalar(dst, src, scale, None, ALU.mult)
                    if a == len(copies) - 1:
                        turn_out[q].by(ins)

        def v_jobs(vT, V, T, nb):
            jobs = []
            for s in range(-(-T // P)):
                R = min(P, T - P * s)
                jobs.append(([(vT[:, b, P * s:P * s + R], P * b) for b in range(nb)],
                             [(R, (0, P * nb), V[0:R, s, 0:P * nb])]))
            return jobs

        def yturn_pe(pe, jobs, normed=None):
            for n, job in enumerate(jobs):
                if normed is not None:
                    normed.take(pe, "pe")
                if n >= 2:
                    sig["yt_lo"].take(pe, "pe")
                srcs = job["srcs"]
                for b, src in enumerate(srcs):
                    mm = flip_over(pe, ps[:, 4 + n % 2, b * src.shape[0]:(b + 1) * src.shape[0]], src)
                sig["yt"].by(mm)
            sig["yt_lo"].take(pe, "pe", min(2, len(jobs)))

        def yturn_views(n, job, T):
            nb, R = len(job["srcs"]), job["srcs"][0].shape[0]
            src = ps[:, 4 + n % 2, 0:nb * R].rearrange("p (a b) -> p a b", a=nb)
            hi, lo = (YBLK[T](y)[:, job["y0"]:job["y0"] + nb, job["c0"]:job["c0"] + R] for y in (Yh, Yl))
            return nb, R, src, hi, lo

        def yturn_act(act, jobs, T):
            for n, job in enumerate(jobs):
                nb, R, src, hi, lo = yturn_views(n, job, T)
                sig["yt"].take(act, "act")
                if "mult" in job:
                    sig["yt_tmp"].take(act, "act")
                    src = job["tmp"][:, n % 2, 0:nb * R].rearrange("p (a b) -> p a b", a=nb)
                sig["yt_hi"].by(act.activation(hi, src, ACT.Copy))

        def yturn_dve(v, jobs, T):
            for n, job in enumerate(jobs):
                nb, R, src, hi, lo = yturn_views(n, job, T)
                sig["yt"].take(v, "dve")
                if "mult" in job:
                    for b, (gain, other) in enumerate(job["mult"]):
                        ins = v.scalar_tensor_tensor(out=job["tmp"][:, n % 2, b * R:(b + 1) * R],
                                                     in0=src[:, b], scalar=gain, in1=other, op0=ALU.mult,
                                                     op1=ALU.mult)
                    sig["yt_tmp"].by(ins)
                    src = job["tmp"][:, n % 2, 0:nb * R].rearrange("p (a b) -> p a b", a=nb)
                    sig["yt_tmp"].last(v)
                sig["yt_hi"].take(v, "dve")
                sig["yt_lo"].by(v.tensor_tensor(lo, src, hi.bitcast(F32), ALU.subtract))

        def attn_columns(small):
            return [small[:, 4 * a:4 * a + 4] for a in range(6)]

        def attn_pe(pe, cases, L, PT):
            N = len(cases)
            for n in range(N + 3):
                if n < N:
                    c = cases[n]
                    if n >= 2:
                        sig["scores_read"].take(pe, "pe")
                    for q, k, bank, col in c["qk"]:
                        mm = pe.matmul(ps[0:c["R"], 2 * (n % 2) + bank, col:col + k.shape[1]], q, k, start=True,
                                       stop=True)
                    sig["scores"].by(mm)
                if 0 <= n - 2 < N:
                    m, c = n - 2, cases[n - 2]
                    sig["probs"].take(pe, "pe")
                    for a, (c0, nk, _) in enumerate(c["tiles"]):
                        mm = flip_over(pe, ps[0:nk, 4 + m % 2, a * c["R"]:(a + 1) * c["R"]],
                                       L[0:c["R"], m % 3, c0:c0 + nk])
                    sig["turned"].by(mm)
                if n >= 3:
                    m, c = n - 3, cases[n - 3]
                    sig["turn_copied"].take(pe, "pe")
                    if m >= 2:
                        sig["pv_read"].take(pe, "pe")
                    for a, (c0, nk, val) in enumerate(c["tiles"]):
                        mm = pe.matmul(ps[0:c["R"], 6 + m % 2, 0:64], PT[0:nk, m % 2, a * c["R"]:(a + 1) * c["R"]],
                                       val, start=(a == 0), stop=(a == len(c["tiles"]) - 1))
                    sig["pv"].by(mm)
            sig["scores_read"].take(pe, "pe", 2)
            sig["pv_read"].take(pe, "pe", 2)

        def attn_act(act, cases, L, PT, small):
            N = len(cases)
            mx, nm, sm, es, den, rc = attn_columns(small)
            for n in range(N + 3):
                if n < N:
                    c, a = cases[n], n % 4
                    R, K = c["R"], c["K"]
                    sig["logits"].take(act, "act")
                    if c.get("sink") is not None:
                        act.activation(es[0:R, a:a + 1], c["sink"], ACT.Exp, bias=nm[0:R, a:a + 1])
                    lg = L[0:R, n % 3, 0:K]
                    sig["probs"].by(act.activation(lg, lg, ACT.Exp, bias=nm[0:R, a:a + 1],
                                                   accum_out=sm[0:R, a:a + 1]))
                if 0 <= n - 2 < N:
                    m, c = n - 2, cases[n - 2]
                    R = c["R"]
                    sig["turned"].take(act, "act")
                    full = sum(1 for _, nk, _ in c["tiles"] if nk == P)
                    pieces = [(P, 0, full * R)] if full else []
                    if full < len(c["tiles"]):
                        pieces.append((c["tiles"][-1][1], full * R, (full + 1) * R))
                    for rows, c0, c1 in pieces:
                        ins = act.activation(PT[0:rows, m % 2, c0:c1], ps[0:rows, 4 + m % 2, c0:c1], ACT.Copy)
                    sig["turn_copied"].by(ins)
                if n >= 3:
                    m, c, a = n - 3, cases[n - 3], (n - 3) % 4
                    R = c["R"]
                    sig["recip"].take(act, "act")
                    sig["pv"].take(act, "act")
                    sig["pv_read"].by(act.activation(c["out"], ps[0:R, 6 + m % 2, 0:64], ACT.Copy,
                                                     scale=rc[0:R, a:a + 1]))

        def attn_dve(v, cases, L, PT, small, between=None):
            N = len(cases)
            mx, nm, sm, es, den, rc = attn_columns(small)
            for n in range(N + 3):
                if n < N:
                    c, a = cases[n], n % 4
                    R, K = c["R"], c["K"]
                    sig["scores"].take(v, "dve")
                    if n >= 3:
                        sig["turned"].take(v, "dve")
                    lg = L[0:R, n % 3, 0:K]
                    if c["mask"] is None:
                        (bank, c0, c1, at, bias), = c["adds"]
                        sig["scores_read"].by(v.tensor_tensor_reduce(
                            out=lg, in0=ps[0:R, 2 * (n % 2) + bank, c0:c1], in1=bias, scale=1.0, scalar=-3.4e38,
                            op0=ALU.add, op1=ALU.max, accum_out=mx[0:R, a:a + 1]))
                        sig["scores_read"].last(v)
                    else:
                        for x, (bank, c0, c1, at, bias) in enumerate(c["adds"]):
                            src, dst = ps[0:R, 2 * (n % 2) + bank, c0:c1], L[0:R, n % 3, at:at + c1 - c0]
                            if bias.shape[1] == 1:
                                ins = v.tensor_scalar(dst, src, bias, None, ALU.add)
                            else:
                                ins = v.tensor_tensor(dst, src, bias, ALU.add)
                        sig["scores_read"].by(ins)
                        sig["scores_read"].last(v)
                        dve.by(v.tensor_tensor_reduce(out=lg, in0=lg, in1=c["mask"], scale=1.0, scalar=-3.4e38,
                                                      op0=ALU.add, op1=ALU.max, accum_out=mx[0:R, a:a + 1]))
                        dve.last(v)
                    if c.get("sink") is not None:
                        ins = v.tensor_scalar(nm[0:R, a:a + 1], mx[0:R, a:a + 1], c["sink"], -1.0, ALU.max, ALU.mult)
                    else:
                        ins = v.tensor_scalar(nm[0:R, a:a + 1], mx[0:R, a:a + 1], -1.0, None, ALU.mult)
                    sig["logits"].by(ins)
                    if between:
                        between(n)
                if n >= 3:
                    m, c, a = n - 3, cases[n - 3], (n - 3) % 4
                    R = c["R"]
                    sig["probs"].take(v, "dve")
                    if m >= 4:
                        sig["pv_read"].take(v, "dve")
                    total = sm
                    if c.get("sink") is not None:
                        dve.by(v.tensor_tensor(den[0:R, a:a + 1], sm[0:R, a:a + 1], es[0:R, a:a + 1], ALU.add))
                        dve.last(v)
                        total = den
                    sig["recip"].by(v.reciprocal(rc[0:R, a:a + 1], total[0:R, a:a + 1]))
            sig["pv_read"].take(v, "dve", 4)
            sig["turned"].take(v, "dve", 3)

        def tables_load(act, which, cut_views):
            rel, onehot, vec, hank, flip, TB = cut_views
            a, n = EXTRA["onehot1" if which == 0 else "onehot2"]
            act.dma_start(onehot, extra[0:33, a:a + n]).then_inc(b_landed, 16)
            act.dma_start(flip, extra[:, EXTRA["flip"][0]:EXTRA["flip"][0] + P]).then_inc(b_landed, 16)
            act.dma_start(rel[0:32], relb1 if which == 0 else relb2).then_inc(b_landed, 16)

        def tables_store(act, which, cut_views):
            vec = cut_views[2]
            sig["v_made"].take(act, "act")
            sig["v_copied"].by(act.activation(vec, ps[0:8, 1, 0:384], ACT.Copy))
            sig["v_copied"].last(act)
            act.dma_start(scratch[which], vec).then_inc(v_written, 16)

        def tables_reload(act, which, cut_views):
            hank = cut_views[3]
            act.wait_ge(v_written, 16 * (which + 1))
            act.dma_start(hank.rearrange("p (h c) -> p h c", h=8),
                          bass.AP(tensor=scratch.tensor, offset=which * 8 * 384, ap=[[1, P], [384, 8], [1, 256]]))\
               .then_inc(b_landed, 16)

        def tables_copy(act, cut_views):
            sig["tb_made"].take(act, "act")
            sig["tb_copied"].by(act.activation(cut_views[5], ps[:, 0:4, :].rearrange("p a b -> p (a b)"), ACT.Copy))

        def tables_dve(v, cut_views):
            sig["memset_done"].by(v.memset(cut_views[0][32:33], NEG))

        def tables_product(pe, which, cut_views):
            rel, onehot = cut_views[0:2]
            pe.wait_ge(b_landed, 64 * which + 48)
            sig["memset_done"].take(pe, "pe")
            sig["v_made"].by(pe.matmul(ps[0:8, 1, 0:384], rel, onehot, start=True, stop=True))

        def tables_flip(pe, which, cut_views):
            hank, flip = cut_views[3:5]
            pe.wait_ge(b_landed, 64 * which + 64)
            for a in range(4):
                mm = pe.matmul(ps[:, a, :], flip, hank[:, 512 * a:512 * a + 512], start=True, stop=True)
            sig["tb_made"].by(mm)

        def dsa_views():
            cut = Cut()
            q, k = cut(4 * T1, b=4), cut(4 * T1, b=4)
            at = cut.at
            iq, ikk = cut(4 * T1, b=4), cut(T1)
            O = Cut(at)(5 * 512, t=5)
            at = cut.at
            cut(3 * T1 + 2 * 640)
            w = Cut(at)
            vT = w(4 * T1, b=4)
            w2 = Cut(at)
            L, PT = w2(3 * T1, a=3), w2(2 * 640, a=2)
            iwT = w(T1, rows=8)
            w = Cut(cut.at)
            onehot, vec, flip = w(384, rows=33), w(384, rows=8), w(128)
            V, TB = cut(5 * 512, t=5), cut(2048)
            at = cut.at
            A = cut(4 * T1, a=4)
            hank = Cut(at)(2048)
            cap, iwt, small, far, m8 = cut(128), cut(40, t=5), cut(28), cut(8), cut(8)
            rel = cut(8, rows=33)
            return dict(q=q, k=k, iq=iq, ikk=ikk, O=O, vT=vT, L=L, PT=PT, V=V, TB=TB.rearrange("p (h c) -> p h c", h=8),
                        A=A, iwT=iwT, cap=cap, iwt=iwt, small=small, far=far, m8=m8,
                        tables=(rel, onehot, vec, hank, flip, TB))

        def head(a, h, c0, c1):
            return a[64 * (h % 2):64 * (h % 2) + 64, h // 2, c0:c1]

        def index_cases():
            return [(t, h, min(P, T1 - P * t), min(T1, P * (t + 1))) for t in range(1, 5) for h in range(8)]

        def bank_parts(K):
            return [(0, 0, K)] if K <= 512 else [(0, 0, 384), (1, 384, K)]

        def dsa_cases(d):
            cases = []
            for t in range(5):
                R, K = min(P, T1 - P * t), min(T1, P * (t + 1))
                for h in range(8):
                    adds = []
                    if t >= 2:
                        adds.append((0, 0, P * (t - 1), 0, d["far"][0:R, h:h + 1]))
                    if t == 0:
                        adds.append((0, 0, P, 0, d["TB"][:, h, P:2 * P]))
                    elif t < 4:
                        adds.append((0, K - 256, K, K - 256, d["TB"][:, h, :]))
                    else:
                        adds.append((1, 0, K - 384, 384, d["TB"][0:R, h, 0:K - 384]))
                    cases.append(dict(
                        R=R, K=K, adds=adds, mask=causal[:, 384:512] if t == 0 else d["A"][0:R, t - 1, 0:K],
                        qk=[(head(d["q"], h, P * t, P * t + R), head(d["k"], h, c0, c1), bank, 0)
                            for bank, c0, c1 in bank_parts(K)],
                        tiles=[(P * s, n, d["V"][0:n, s, 64 * h:64 * h + 64]) for s, n in KEYTILE[0:t + 1]],
                        out=d["O"][0:R, t, 64 * h:64 * h + 64]))
            return cases

        def dsa_turns(d):
            iw = [(d["iwT"][:, P * t:P * t + min(P, T1 - P * t)], 8 * t) for t in range(5)]
            return [(iw, [(P, (0, 32), d["iwt"][:, 0:4, :]), (16, (32, 40), d["iwt"][0:16, 4, :])])]

        def dsa_ys(d):
            return [dict(srcs=[d["O"][0:min(P, T1 - P * t), t, P * b:P * b + P] for b in range(4)], y0=0, c0=P * t)
                    for t in range(5)]

        def dsa_pe(pe):
            d = dsa_views()
            pe_first(pe, [(PLAN["a_v"], b) for b in range(4)], T1)
            for n in ("a_q", "a_k", "a_iq", "a_small"):
                pe_units(pe, PLAN[n], T1)
            wait_evacuated(pe, PLAN["a_small"])
            tables_flip(pe, 0, d["tables"])
            turn_pe(pe, dsa_turns(d))
            turn_pe(pe, v_jobs(d["vT"], d["V"], T1, 4))
            sig["tb_copied"].take(pe, "pe")
            for n, (t, h, R, K) in enumerate(index_cases()):
                if n >= 2:
                    sig["idx_relu"].take(pe, "pe")
                for bank, c0, c1 in bank_parts(K):
                    mm = pe.matmul(ps[0:R, 2 * (n % 2) + bank, 0:c1 - c0], head(d["iq"], h, P * t, P * t + R),
                                   d["ikk"][64 * (h % 2):64 * (h % 2) + 64, c0:c1], start=True, stop=True)
                sig["idx"].by(mm)
            sig["idx_relu"].take(pe, "pe", 2)
            turned_all(pe, "pe")
            attn_pe(pe, dsa_cases(d), d["L"], d["PT"])
            yturn_pe(pe, dsa_ys(d))
            pe_units(pe, PLAN["a_out"], T1, (YBLK[T1](Yh), YBLK[T1](Yl)), tuple(range(4)))

        def dsa_act(act):
            d = dsa_views()
            evac_units(act, None, PLAN["a_v"], T1, d["vT"])
            a = EXTRA["cap"][0]
            act.dma_start(d["cap"], extra[:, a:a + P]).then_inc(tables_landed.sem, 16)
            act.dma_start(d["far"], bass.AP(tensor=relb1.tensor, offset=31 * 8, ap=[[0, P], [1, 8]]))\
               .then_inc(tables_landed.sem, 16)
            evac_units(act, None, PLAN["a_q"], T1, d["q"], 64 ** -0.5)
            evac_units(act, None, PLAN["a_k"], T1, d["k"])
            evac_units(act, None, PLAN["a_iq"], T1, d["iq"])
            j, n = unit(PLAN["a_small"], 0)
            act.wait_ge(unit_done[j], n)
            act.activation(cols(d["ikk"], T1), acc(j, T1), ACT.Copy).then_inc(acc_free[j], 1)
            tables_copy(act, d["tables"])
            act.preload_act_table_set("natural_log_exp_and_others")
            turn_copy(act, "act", dsa_turns(d), 8 ** -0.5 * 64 ** -0.5)
            turn_copy(act, "act", v_jobs(d["vT"], d["V"], T1, 4))
            turned_all(act, "act")
            for n, (t, h, R, K) in enumerate(index_cases()):
                sig["idx"].take(act, "act")
                if n >= 2:
                    sig["idx_added"].take(act, "act")
                for bank, c0, c1 in bank_parts(K):
                    ins = act.activation(d["L"][0:R, n % 2, c0:c1], ps[0:R, 2 * (n % 2) + bank, 0:c1 - c0], ACT.Relu)
                sig["idx_relu"].by(ins)
            sig["idx_added"].take(act, "act", 2)
            attn_act(act, dsa_cases(d), d["L"], d["PT"], d["small"])
            yturn_act(act, dsa_ys(d), T1)

        def dsa_dve(v):
            d = dsa_views()
            evac_units(None, v, PLAN["a_v"], T1, d["vT"])
            evac_units(None, v, PLAN["a_q"], T1, d["q"], 64 ** -0.5)
            evac_units(None, v, PLAN["a_k"], T1, d["k"])
            evac_units(None, v, PLAN["a_iq"], T1, d["iq"])
            j, n = unit(PLAN["a_small"], 1)
            v.wait_ge(unit_done[j], n)
            v.tensor_copy(cols(d["iwT"], T1), ps[0:8, 2 * j:2 * j + 2, 0:264]).then_inc(acc_free[j], 1)
            sig["tb_copied"].take(v, "dve")
            turn_copy(v, "dve", dsa_turns(d))
            turn_copy(v, "dve", v_jobs(d["vT"], d["V"], T1, 4))
            turned_all(v, "dve")
            v.wait_ge(tables_landed.sem, 32)
            ROUNDS = (KEEP - META) // 8

            def mask_part(t, part, parts):
                if t > 4:
                    return
                R, K = min(P, T1 - P * t), min(T1, P * (t + 1))
                A = d["A"][0:R, t - 1, 0:K]
                rest = A[:, META:K]
                if part == 0:
                    diag = A[:, P * t:P * t + R]
                    dve.by(v.tensor_tensor(diag, diag, d["cap"][0:R, 0:R], ALU.min))
                    dve.last(v)
                for _ in range(ROUNDS * part // parts, ROUNDS * (part + 1) // parts):
                    dve.by(v.max(d["m8"][0:R], rest))
                    dve.last(v)
                    dve.by(v.match_replace(rest, d["m8"][0:R], rest, TAKEN))
                    dve.last(v)
                if part == parts - 1:
                    dve.by(v.tensor_scalar(rest, rest, TAKEN_LIMIT, NEG, ALU.is_gt, ALU.mult))
                    dve.by(v.memset(A[:, 0:META], 0.0))
                    dve.last(v)

            for t, h, R, K in index_cases():
                A, r = d["A"][0:R, t - 1, 0:K], d["L"][0:R, h % 2, 0:K]
                sig["idx_relu"].take(v, "dve")
                if h == 0:
                    ins = v.tensor_scalar(A, r, d["iwt"][0:R, t, 0:1], None, ALU.mult)
                else:
                    ins = v.scalar_tensor_tensor(out=A, in0=r, scalar=d["iwt"][0:R, t, h:h + 1], in1=A,
                                                 op0=ALU.mult, op1=ALU.add)
                sig["idx_added"].by(ins)
                sig["idx_added"].last(v)
            attn_dve(v, dsa_cases(d), d["L"], d["PT"], d["small"], lambda n: mask_part(n // 8 + 1, n % 8, 8))
            yturn_dve(v, dsa_ys(d), T1)
            residual_units(v, PLAN["a_out"], T1, 0)

        def ret_views():
            cut = Cut()
            q, k = cut(2 * T1, b=2), cut(2 * T1, b=2)
            at = cut.at
            AT = cut(2 * TRI, b=2)
            vT = Cut(at)(4 * T1, b=4)
            V, G = cut(5 * 512, t=5), cut(4 * T1, b=4)
            at = cut.at
            O = cut(5 * 512, t=5)
            rt = Cut(at)(2 * T1, a=2)
            decay, cos, sin, rot = cut(2 * T1, b=2), cut(T1), cut(T1), cut(P)
            tmp, st, mv, sd = cut(1024, a=2), cut(6), cut(20, a=10), cut(10)
            return dict(q=q, k=k, qk=(q, k), AT=AT, vT=vT, V=V, G=G, O=O, rt=rt, decay=decay, cos=cos, sin=sin,
                        rot=rot, tmp=tmp,
                        st=st, mv=mv, sd=sd)

        RET_PIECES = [(hh, *p) for hh in range(2) for p in PIECES]
        RET_OUTS = [(hh, t, min(P, T1 - P * t)) for hh in range(2) for t in range(5)]

        def ret_ys(d, g):
            return [dict(srcs=[d["O"][0:min(P, T1 - P * t), t, P * b:P * b + P] for b in range(4)], y0=4 * g, c0=P * t,
                         tmp=d["tmp"], mult=[(param("gn", 4 * g + b), d["G"][:, b, P * t:min(T1, P * t + P)])
                                             for b in range(4)]) for t in range(5)]

        def ret_pe(pe, g):
            d = ret_views()
            for n in ("b_q", "b_k"):
                pe_units(pe, PLAN[f"{n}{g}"], T1)
            pe.wait_ge(tables_landed.sem, 32 + 64 * (g + 1))
            for n in range(4):
                j, filled = unit(PLAN[f"b_q{g}"], n)
                pe.wait_ge(acc_free[j], filled)
                x = d["qk"[n // 2]][:, n % 2, :]
                for h, (c0, c1) in enumerate(halves(T1)):
                    mm = pe.matmul(ps[:, 2 * j + h, 0:c1 - c0], d["rot"], x[:, c0:c1], start=True, stop=True)
                sig["rot_made"].by(mm)
            for b in range(4):
                sig["rot_done"].take(pe, "pe")
                pe_units(pe, PLAN[f"b_v{g}"], T1, only=(b,))
            pe_units(pe, PLAN[f"b_g{g}"], T1)
            wait_evacuated(pe, PLAN[f"b_g{g}"])
            turn_pe(pe, v_jobs(d["vT"], d["V"], T1, 4))
            turned_all(pe, "pe")
            for n, (hh, s, c0, c1) in enumerate(RET_PIECES):
                if n >= 4:
                    sig["ret_a"].take(pe, "pe")
                R = KEYTILE[s][1]
                sig["ret_s"].by(pe.matmul(ps[0:R, n % 4, 0:c1 - c0], d["k"][:, hh, P * s:P * s + R],
                                          d["q"][:, hh, c0:c1], start=True, stop=True))
            sig["ret_a"].take(pe, "pe", 4)
            for n, (hh, t, R) in enumerate(RET_OUTS):
                if n >= 2:
                    sig["ret_copied"].take(pe, "pe")
                for s in range(t + 1):
                    a = TILE_AT[s] + P * (t - s)
                    mm = pe.matmul(ps[0:R, 4 + n % 2, 0:256], d["AT"][0:KEYTILE[s][1], hh, a:a + R],
                                   d["V"][0:KEYTILE[s][1], s, 256 * hh:256 * hh + 256], start=(s == 0), stop=(s == t))
                sig["ret_o"].by(mm)
            sig["ret_copied"].take(pe, "pe", 2)
            yturn_pe(pe, ret_ys(d, g), sig["ret_norm"])

        def ret_act(act, g):
            d = ret_views()
            evac_units(act, None, PLAN[f"b_q{g}"], T1, d["q"])
            for name, dst, c, n in (("cos", d["cos"], 0, T1), ("sin", d["sin"], 0, T1), ("rot", d["rot"], 0, P),
                                    ("decay", d["decay"].rearrange("p b t -> p (b t)"), 2 * T1 * g, 2 * T1)):
                a = EXTRA[name][0] + c
                act.dma_start(dst, extra[:, a:a + n]).then_inc(tables_landed.sem, 16)
            evac_units(act, None, PLAN[f"b_k{g}"], T1, d["k"])
            evac_units(act, None, PLAN[f"b_v{g}"], T1, d["vT"])
            evac_units(act, None, PLAN[f"b_g{g}"], T1, d["G"], func=ACT.Silu)
            turn_copy(act, "act", v_jobs(d["vT"], d["V"], T1, 4))
            for n, (hh, t, R) in enumerate(RET_OUTS):
                sig["ret_o"].take(act, "act")
                sig["ret_copied"].by(act.activation(d["O"][0:R, t, 256 * hh:256 * hh + 256],
                                                    ps[0:R, 4 + n % 2, 0:256], ACT.Copy))
            sig["ret_var"].take(act, "act")
            sig["ret_std"].by(act.activation(d["sd"], d["mv"][:, :, 1], ACT.Sqrt, bias=eps[:, 0:1]))
            yturn_act(act, ret_ys(d, g), T1)

        def ret_dve(v, g):
            d = ret_views()
            evac_units(None, v, PLAN[f"b_q{g}"], T1, d["q"])
            evac_units(None, v, PLAN[f"b_k{g}"], T1, d["k"])
            v.wait_ge(tables_landed.sem, 32 + 64 * (g + 1))
            for n in range(4):
                sig["rot_made"].take(v, "dve")
                if n:
                    sig["rot_done"].last(v)
                x = d["qk"[n // 2]][:, n % 2, :]
                dve.by(v.tensor_tensor(d["rt"][:, 0], x, d["cos"], ALU.mult))
                j, _ = unit(PLAN[f"b_q{g}"], n)
                dve.by(v.tensor_tensor(cols(d["rt"][:, 1], T1), acc(j, T1), cols(d["sin"], T1), ALU.mult))
                dve.last(v)
                sig["rot_done"].by(v.tensor_tensor(x, d["rt"][:, 0], d["rt"][:, 1], ALU.add))
            evac_units(None, v, PLAN[f"b_v{g}"], T1, d["vT"])
            turn_copy(v, "dve", v_jobs(d["vT"], d["V"], T1, 4))
            for n, (hh, s, c0, c1) in enumerate(RET_PIECES):
                sig["ret_s"].take(v, "dve")
                if n == 0:
                    turned_all(v, "dve")
                R, a = KEYTILE[s][1], TILE_AT[s] + c0 - P * s
                sig["ret_a"].by(v.tensor_tensor(d["AT"][0:R, hh, a:a + c1 - c0], ps[0:R, n % 4, 0:c1 - c0],
                                                d["decay"][0:R, hh, c0 - P * s:c1 - P * s], ALU.mult))
            dve.by(v.memset(d["mv"], 1.0))
            dve.last(v)
            for n, (hh, t, R) in enumerate(RET_OUTS):
                sig["ret_copied"].take(v, "dve")
                dve.by(v.bn_stats(d["st"][0:R], d["O"][0:R, t, 256 * hh:256 * hh + 256]))
                dve.last(v)
                dve.by(v.bn_aggr(d["mv"][0:R, n], d["st"][0:R]))
                dve.last(v)
            sig["ret_var"].by(v.memset(d["st"], 0.0))
            sig["ret_std"].take(v, "dve")
            dve.by(v.reciprocal(d["sd"], d["sd"]))
            dve.last(v)
            for t in range(5):
                for hh in range(2):
                    n, R = 5 * hh + t, min(P, T1 - P * t)
                    o = d["O"][0:R, t, 256 * hh:256 * hh + 256]
                    ins = v.tensor_scalar(o, o, d["mv"][0:R, n, 0:1], d["sd"][0:R, n:n + 1], ALU.subtract, ALU.mult)
                sig["ret_norm"].by(ins)
            yturn_dve(v, ret_ys(d, g), T1)

        def stick_views():
            cut = Cut()
            q, k = cut(4 * T1, b=4), cut(4 * T1, b=4)
            at = cut.at
            L1 = cut(2 * TRI, b=2)
            vT = Cut(at)(4 * T1, b=4)
            V, A, E = cut(5 * 512, t=5), cut(3 * 400, a=3), cut(4 * 400, a=4)
            oT = cut(T1)
            strictT, strictmul, ntri, nones = cut(P), cut(P), cut(P), cut(P)
            return dict(q=q, k=k, oT=oT, L1=L1, vT=vT, V=V, A=A, E=E, strictT=strictT, strictmul=strictmul, ntri=ntri,
                        nones=nones)

        STICK = [(hh, x, *p) for hh in range(8) for x, p in enumerate(PIECES)]
        NS = len(STICK)

        def has_diag(s, c0):
            return c0 == P * s

        def l_cols(d, hh, s, c0, c1):
            a = TILE_AT[s] - P * s
            return d["L1"][0:KEYTILE[s][1], hh % 2, a + c0:a + c1]

        def stick_pe(pe, g):
            d = stick_views()
            if g == 0:
                pe_first(pe, [(PLAN["c_v0"], b) for b in range(4)], T1)
            for n in ("c_v", "c_q", "c_k")[g == 0:]:
                pe_units(pe, PLAN[f"{n}{g}"], T1)
            wait_evacuated(pe, PLAN[f"c_k{g}"])
            pe.wait_ge(tables_landed.sem, 32 + 128 + 64 * (g + 1))
            turn_pe(pe, v_jobs(d["vT"], d["V"], T1, 4))
            turned_all(pe, "pe")
            for n in range(NS + 5):
                if n < NS:
                    hh, x, s, c0, c1 = STICK[n]
                    R = KEYTILE[s][1]
                    sig["z_made"].by(pe.matmul(ps[0:R, n % 6, 0:c1 - c0], head(d["k"], hh, P * s, P * s + R),
                                               head(d["q"], hh, c0, c1), start=True, stop=True))
                if 0 <= n - 3 < NS:
                    m = n - 3
                    hh, x, s, c0, c1 = STICK[m]
                    R = KEYTILE[s][1]
                    sig["l_made"].take(pe, "pe")
                    mm = pe.matmul(ps[0:R, m % 6, 0:c1 - c0], d["ntri"][0:R, 0:R], l_cols(d, hh, s, c0, c1),
                                   start=False, stop=True, skip_group_check=True)
                    for s2 in range(s + 1, 5):
                        lo = max(c0, P * s2)
                        if lo < c1:
                            mm = pe.matmul(ps[0:R, m % 6, lo - c0:c1 - c0], d["nones"][0:KEYTILE[s2][1], 0:R],
                                           l_cols(d, hh, s2, lo, c1), start=False, stop=True, skip_group_check=True)
                    sig["cum"].by(mm)
                if 0 <= n - 5:
                    m = n - 5
                    hh, x, s, c0, c1 = STICK[m]
                    R = KEYTILE[s][1]
                    sig["a_exp"].take(pe, "pe")
                    if x == 0 and hh % 2 == 0 and hh >= 2:
                        sig["oT_copied"].take(pe, "pe")
                    for h, (h0, h1) in enumerate(halves(T1)):
                        lo, hi = max(c0, h0), min(c1, h1)
                        if lo < hi:
                            mm = pe.matmul(ps[64 * (hh % 2):64 * (hh % 2) + 64, 6 + h, lo - h0:hi - h0],
                                           d["V"][0:R, s, 64 * hh:64 * hh + 64], d["A"][0:R, m % 3, lo - c0:hi - c0],
                                           start=(x == (2, 0)[h]), stop=(x == (5, 4)[h]), skip_group_check=True)
                    sig["o_used"].by(mm)
            sig["oT_copied"].take(pe, "pe")

        def stick_act(act, g):
            d = stick_views()
            evac_units(act, None, PLAN[f"c_v{g}"], T1, d["vT"])
            for name in ("strictT", "strictmul", "ntri", "nones"):
                a = EXTRA[name][0]
                act.dma_start(d[name], extra[:, a:a + P]).then_inc(tables_landed.sem, 16)
            evac_units(act, None, PLAN[f"c_q{g}"], T1, d["q"], 64 ** -0.5)
            evac_units(act, None, PLAN[f"c_k{g}"], T1, d["k"])
            turn_copy(act, "act", v_jobs(d["vT"], d["V"], T1, 4))
            act.preload_act_table_set("natural_log_exp_and_others")
            for n in range(NS + 6):
                if n < NS:
                    hh, x, s, c0, c1 = STICK[n]
                    R = KEYTILE[s][1]
                    e = d["E"][0:R, n % 4, 0:c1 - c0]
                    sig["z_made"].take(act, "act")
                    if n >= 4:
                        sig["l_made"].take(act, "act")
                    acts.by(act.activation(e, ps[0:R, n % 6, 0:c1 - c0], ACT.Abs))
                    acts.last(act)
                    sig["z_exp"].by(act.activation(e, e, ACT.Exp, scale=-1.0))
                if 0 <= n - 4 < NS:
                    m = n - 4
                    hh, x, s, c0, c1 = STICK[m]
                    R = KEYTILE[s][1]
                    sig["cum"].take(act, "act")
                    if m >= 3:
                        sig["o_used"].take(act, "act")
                    if has_diag(s, c0):
                        sig["a_diag"].take(act, "act")
                    sig["a_exp"].by(act.activation(d["A"][0:R, m % 3, 0:c1 - c0], ps[0:R, m % 6, 0:c1 - c0], ACT.Exp))
                if n < NS:
                    sig["z_exp"].take(act, "act")
                    sig["z_log"].by(act.activation(e, e, ACT.Ln, bias=1.0))
                if 0 <= n - 6 < NS:
                    hh, x = STICK[n - 6][0:2]
                    if x == 5 and hh % 2:
                        sig["oT_copied"].take(act, "act")
                        sig["oT_hi"].by(act.activation(YBLK[T1](Yh)[:, 4 * g + hh // 2, :], d["oT"], ACT.Copy))
            sig["o_used"].take(act, "act", 3)
            sig["l_made"].take(act, "act", 4)

        def stick_dve(v, g):
            d = stick_views()
            evac_units(None, v, PLAN[f"c_v{g}"], T1, d["vT"])
            evac_units(None, v, PLAN[f"c_q{g}"], T1, d["q"], 64 ** -0.5)
            evac_units(None, v, PLAN[f"c_k{g}"], T1, d["k"])
            turn_copy(v, "dve", v_jobs(d["vT"], d["V"], T1, 4))
            turned_all(v, "dve")
            v.wait_ge(tables_landed.sem, 32 + 128 + 64 * (g + 1))
            for n in range(NS + 6):
                if 0 <= n - 1 < NS:
                    m = n - 1
                    hh, x, s, c0, c1 = STICK[m]
                    R = KEYTILE[s][1]
                    if x == 0 and hh >= 2:
                        sig["cum"].take(v, "dve", 6)
                    sig["z_log"].take(v, "dve")
                    l1 = l_cols(d, hh, s, c0, c1)
                    ins = v.scalar_tensor_tensor(out=l1, in0=ps[0:R, m % 6, 0:c1 - c0], scalar=0.0,
                                                 in1=d["E"][0:R, m % 4, 0:c1 - c0], op0=ALU.max, op1=ALU.add)
                    if has_diag(s, c0):
                        dve.by(ins)
                        dve.last(v)
                        ins = v.tensor_tensor(l1[:, 0:R], l1[:, 0:R], d["strictmul"][0:R, 0:R], ALU.mult)
                    sig["l_made"].by(ins)
                if 0 <= n - 4 < NS:
                    m = n - 4
                    hh, x, s, c0, c1 = STICK[m]
                    R = KEYTILE[s][1]
                    if has_diag(s, c0):
                        v.wait_ge(sig["cum"].sem, NS * g + m + 1)
                        diag = ps[0:R, m % 6, 0:R]
                        sig["a_diag"].by(v.tensor_tensor(diag, diag, d["strictT"][0:R, 0:R], ALU.add))
                if 0 <= n - 5 < NS:
                    hh, x = STICK[n - 5][0:2]
                    if x == 5 and hh % 2:
                        if hh > 1:
                            sig["oT_lo"].last(v)
                        v.wait_ge(sig["o_used"].sem, NS * g + n - 4)
                        sig["oT_copied"].by(v.tensor_copy(cols(d["oT"], T1), acc(3, T1)))
                if 0 <= n - 6 < NS:
                    hh, x = STICK[n - 6][0:2]
                    if x == 5 and hh % 2:
                        sig["oT_hi"].take(v, "dve")
                        yh, yl = (YBLK[T1](y)[:, 4 * g + hh // 2, :] for y in (Yh, Yl))
                        sig["oT_lo"].by(v.tensor_tensor(yl, d["oT"], yh.bitcast(F32), ALU.subtract))
            sig["oT_lo"].last(v)
            sig["cum"].take(v, "dve", 12)
            sig["a_exp"].take(v, "dve", NS)

        def keep_views():
            cut = Cut(ARENA - 4096)
            sv, mo = cut(T2), cut(2 * T2, b=2)
            rows = [cut(T2, rows=4) for _ in range(5)]
            return dict(sv=sv, mo=mo, c=rows[0], B=rows[1], u=rows[2], M=rows[3], e=rows[4])

        def headnorm_act(act, items, sq, rs):
            N = len(items)
            act.preload_act_table_set("natural_log_exp_and_others")
            for n in range(N + 1):
                if n < N:
                    sig["hn_sq"].by(act.activation(sq[:, n % 2], items[n][0], ACT.Square))
                if n >= 1:
                    m = n - 1
                    sig["hn_sum"].take(act, "act")
                    if m >= 2:
                        sig["hn_done"].take(act, "act")
                    e = 64 if items[m][2] else 1
                    rsqrt(act, sig["hn_std"], rs[:, m % 2], ps[:, m % 2, :],
                          eps[:, 1:2] if items[m][2] else eps[:, 0:1], e / 64)
            sig["hn_done"].take(act, "act", 2)

        def headnorm_pe(pe, N, sq, blockones):
            for n in range(N):
                sig["hn_sq"].take(pe, "pe")
                if n >= 2:
                    sig["hn_std"].take(pe, "pe")
                sig["hn_sum"].by(pe.matmul(ps[:, n % 2, :], blockones, sq[:, n % 2], start=True, stop=True))
            sig["hn_std"].take(pe, "pe", 2)
            pe.wait_ge(sig["hn_done"].sem, headnorm_pe_total(N))

        hn_total = [0]

        def headnorm_pe_total(N):
            hn_total[0] += N
            return hn_total[0]

        def headnorm_dve(v, items, rs):
            for n, (x, gain, _) in enumerate(items):
                sig["hn_std"].take(v, "dve")
                sig["hn_done"].by(v.scalar_tensor_tensor(out=x, in0=x, scalar=gain, in1=rs[:, n % 2], op0=ALU.mult,
                                                         op1=ALU.mult))

        TB1 = 32 + 128 + 128

        def spread_act(act, dst):
            sig["bc_made"].take(act, "act")
            sig["bc_copied"].by(act.activation(dst, ps[:, 0:4, :], ACT.Copy))

        def spread_pe(pe, selneg, row):
            for h in range(4):
                mm = pe.matmul(ps[:, h, :], selneg[:, h, :], row, start=True, stop=True)
            sig["bc_made"].by(mm)
            sig["bc_copied"].take(pe, "pe")

        def fox_views():
            cut = Cut()
            vT, V = cut(2 * T2, b=2), cut(4 * 256, t=4)
            q, k = cut(2 * T2, b=2), cut(2 * T2, b=2)
            at = cut.at
            NC = cut(4 * T2, h=4)
            tmp = Cut(at)
            z1, l1, z2, l2 = (tmp(T2, rows=4) for _ in range(4))
            L = cut(3 * T2, a=3)
            at = cut.at
            PT = cut(2 * 512, a=2)
            one = Cut(at)(T2, rows=4)
            O, sq, rs = cut(4 * 256, t=4), cut(2 * T2, a=2), cut(2 * T2, a=2)
            blockones, selneg, small = cut(P), cut(4 * P, rows=4, h=4), cut(28)
            return dict(vT=vT, V=V, q=q, k=k, NC=NC, z=(z1, z2), l=(l1, l2), L=L, PT=PT, one=one, O=O, sq=sq, rs=rs,
                        blockones=blockones, selneg=selneg, small=small, **{"keep": keep_views()})

        def fox_norms(d):
            return [(d["q"][:, b], param("fq"), True) for b in range(2)] + \
                   [(d["k"][:, b], param("fk"), False) for b in range(2)]

        def fox_cases(d):
            return [dict(R=P, K=P * (t + 1), adds=[(0, 0, P * (t + 1), 0, d["NC"][:, h, 0:P * (t + 1)])],
                         mask=causal[:, 512 - P * (t + 1):512],
                         qk=[(head(d["q"], h, P * t, P * t + P), head(d["k"], h, 0, P * (t + 1)), 0, 0)],
                         tiles=[(P * s, P, d["V"][:, s, 64 * h:64 * h + 64]) for s in range(t + 1)],
                         out=d["O"][:, t, 64 * h:64 * h + 64]) for t in range(4) for h in range(4)]

        def token_ys(O, nb, y0, **more):
            return [dict(srcs=[O[:, t, P * b:P * b + P] for b in range(nb)], y0=y0, c0=P * t, **more)
                    for t in range(4)]

        def fox_pe(pe):
            d = fox_views()
            pe_first(pe, [(PLAN[n], b) for n in ("f_v", "f_q") for b in range(2)], T2)
            for n in ("f_k", "f_small", "m_o"):
                pe_units(pe, PLAN[n], T2)
            wait_evacuated(pe, PLAN["m_o"])
            pe.wait_ge(tables_landed.sem, TB1 + 32)
            turn_pe(pe, v_jobs(d["vT"], d["V"], T2, 2))
            headnorm_pe(pe, 4, d["sq"], d["blockones"])
            sig["row_scan"].take(pe, "pe")
            spread_pe(pe, d["selneg"], d["keep"]["c"])
            turned_all(pe, "pe")
            attn_pe(pe, fox_cases(d), d["L"], d["PT"])
            yturn_pe(pe, token_ys(d["O"], 2, 0))

        def fox_act(act):
            d = fox_views()
            kp = d["keep"]
            evac_units(act, None, PLAN["f_v"], T2, d["vT"])
            for name, dst, n in (("blockones", d["blockones"], P), ("selneg", d["selneg"].rearrange("p h c -> p (h c)"),
                                                                    4 * P)):
                a = EXTRA[name][0]
                act.dma_start(dst, extra[0:dst.shape[0], a:a + n]).then_inc(tables_landed.sem, 16)
            evac_units(act, None, PLAN["f_q"], T2, d["q"])
            evac_units(act, None, PLAN["f_k"], T2, d["k"])
            for b, (dst, bias) in enumerate(((d["z"][0], "fbias"), (d["z"][1], "mfbias"), (kp["u"], "ibias"))):
                j, n = unit(PLAN["f_small"], b)
                act.wait_ge(unit_done[j], n)
                act.activation(dst, ps[0:4, 2 * j, :], ACT.Identity, bias=param(bias, 0, 4)).then_inc(acc_free[j], 1)
            for b in range(2):
                j, n = unit(PLAN["f_small"], b)
                act.wait_ge(acc_free[j], n)
                acts.by(act.activation(d["l"][b], d["z"][b], ACT.Abs))
                acts.last(act)
                acts.by(act.activation(d["l"][b], d["l"][b], ACT.Exp, scale=-1.0))
                acts.last(act)
                sig["row_log"].by(act.activation(d["l"][b], d["l"][b], ACT.Ln, bias=1.0))
            for b in range(2):
                j, n = unit(PLAN["m_o"], b)
                act.wait_ge(unit_done[j], n)
                act.activation(kp["mo"][:, b], acc(j, T2), ACT.Sigmoid).then_inc(acc_free[j], 1)
            turn_copy(act, "act", v_jobs(d["vT"], d["V"], T2, 2))
            wait_evacuated(act, PLAN["f_k"])
            headnorm_act(act, fox_norms(d), d["sq"], d["rs"])
            sig["row_done"].take(act, "act")
            acts.by(act.activation(kp["e"], kp["e"], ACT.Exp, scale=-1.0))
            acts.last(act)
            spread_act(act, d["NC"])
            attn_act(act, fox_cases(d), d["L"], d["PT"], d["small"])
            yturn_act(act, token_ys(d["O"], 2, 0), T2)

        def fox_dve(v):
            d = fox_views()
            kp = d["keep"]
            evac_units(None, v, PLAN["f_v"], T2, d["vT"])
            evac_units(None, v, PLAN["f_q"], T2, d["q"])
            evac_units(None, v, PLAN["f_k"], T2, d["k"])
            dve.by(v.memset(d["one"], 1.0))
            for b, dst in enumerate((kp["c"], kp["B"])):
                sig["row_log"].take(v, "dve")
                dve.by(v.scalar_tensor_tensor(out=d["l"][b], in0=d["z"][b], scalar=0.0, in1=d["l"][b], op0=ALU.min,
                                              op1=ALU.subtract))
                dve.last(v)
                ins = v.tensor_tensor_scan(dst, d["one"], d["l"][b], 0.0, ALU.mult, ALU.add)
                (dve if b else sig["row_scan"]).by(ins)
            dve.last(v)
            j, n = unit(PLAN["f_small"], 2)
            v.wait_ge(acc_free[j], n)
            dve.by(v.tensor_tensor(kp["u"], kp["u"], kp["B"], ALU.subtract))
            dve.last(v)
            dve.by(v.tensor_tensor_scan(kp["M"], d["one"], kp["u"], 0.0, ALU.mult, ALU.max))
            dve.last(v)
            sig["row_done"].by(v.tensor_tensor(kp["e"], kp["B"], kp["M"], ALU.add))
            j, n = unit(PLAN["m_o"], 2)
            v.wait_ge(unit_done[j], n)
            v.tensor_copy(kp["sv"], acc(j, T2)).then_inc(acc_free[j], 1)
            turn_copy(v, "dve", v_jobs(d["vT"], d["V"], T2, 2))
            headnorm_dve(v, fox_norms(d), d["rs"])
            sig["bc_copied"].take(v, "dve")
            attn_dve(v, fox_cases(d), d["L"], d["PT"], d["small"])
            yturn_dve(v, token_ys(d["O"], 2, 0), T2)

        def conv_views():
            cut = Cut()
            return dict(u=cut(2 * T2, b=2), b=cut(2 * T2, b=2), c=cut(2 * T2, b=2), z=cut(2 * (T2 + 2), b=2),
                        y=cut(2 * T2, b=2))

        def conv_pe(pe):
            for n in ("v_u", "v_b", "v_c"):
                pe_units(pe, PLAN[n], T2)

        def conv_act(act):
            d = conv_views()
            for n in "ubc":
                evac_units(act, None, PLAN["v_" + n], T2, d[n])
            for b in range(2):
                sig["cv_tmp"].take(act, "act")
                sig["cv_hi"].by(act.activation(YBLK[T2](Yh)[:, 2 + b], d["y"][:, b], ACT.Copy))

        def conv_dve(v):
            d = conv_views()
            for n in "ubc":
                evac_units(None, v, PLAN["v_" + n], T2, d[n])
            wait_evacuated(v, PLAN["v_c"])
            dve.by(v.memset(d["z"][:, :, 0:2], 0.0))
            for b in range(2):
                w = [param("conv2", 3 * b + a) for a in range(3)]
                dve.by(v.tensor_tensor(d["z"][:, b, 2:], d["c"][:, b], d["u"][:, b], ALU.mult))
                dve.last(v)
                dve.by(v.tensor_scalar(d["y"][:, b], d["z"][:, b, 2:], w[2], None, ALU.mult))
                dve.last(v)
                for a in (1, 0):
                    dve.by(v.scalar_tensor_tensor(out=d["y"][:, b], in0=d["z"][:, b, a:a + T2], scalar=w[a],
                                                  in1=d["y"][:, b], op0=ALU.mult, op1=ALU.add))
                    dve.last(v)
                sig["cv_tmp"].by(v.tensor_tensor(d["y"][:, b], d["y"][:, b], d["b"][:, b], ALU.mult))
            for b in range(2):
                sig["cv_tmp"].last(v)
                sig["cv_hi"].take(v, "dve")
                sig["cv_lo"].by(v.tensor_tensor(YBLK[T2](Yl)[:, 2 + b], d["y"][:, b],
                                                YBLK[T2](Yh)[:, 2 + b].bitcast(F32), ALU.subtract))

        M_AT = [0, 512, 896, 1152]

        def mlstm_views():
            cut = Cut()
            at = cut.at
            sq = cut(4 * 256, t=4)
            vT = Cut(at)(2 * T2, b=2)
            V = cut(4 * 4 * 65, t=4, h=4)
            q, k, NM = cut(2 * T2, b=2), cut(2 * T2, b=2), cut(4 * T2, h=4)
            AT, W, D = cut(2 * 1280, a=2), cut(2 * T2, a=2), cut(2 * P, a=2)
            H, tmp = cut(4 * 256, t=4), cut(2 * 256, a=2)
            selneg, ue, dn, rc, ss = cut(4 * P, rows=4, h=4), cut(32), cut(2), cut(2), cut(16)
            return dict(sq=sq, vT=vT, V=V, q=q, k=k, NM=NM, AT=AT, W=W, D=D, H=H, tmp=tmp, selneg=selneg, ue=ue,
                        dn=dn, rc=rc, ss=ss, keep=keep_views())

        def mlstm_turns(d):
            kp, jobs = d["keep"], []
            parts = [(kp[r][:, P * t:P * t + P], 16 * a + 4 * t) for a, r in enumerate(("u", "e")) for t in range(4)]
            jobs.append((parts, [(P, (0, 32), d["ue"])]))
            for s in range(4):
                jobs.append(([(d["vT"][:, b, P * s:P * s + P], P * b) for b in range(2)],
                             [(P, (0, 256), d["V"][:, s, :, 0:64])]))
            return jobs

        MP = [(h, s) for h in range(4) for s in range(4)]

        def mlstm_ys(d):
            return [dict(srcs=[d["H"][:, t, P * b:P * b + P] for b in range(2)], y0=4, c0=P * t, tmp=d["tmp"],
                         mult=[(param("mh", b), d["keep"]["mo"][:, b, P * t:P * t + P]) for b in range(2)])
                    for t in range(4)]

        def mlstm_pe(pe):
            d = mlstm_views()
            for n in ("m_v", "m_q", "m_k"):
                pe_units(pe, PLAN[n], T2)
            wait_evacuated(pe, PLAN["m_k"])
            pe.wait_ge(tables_landed.sem, TB1 + 48)
            spread_pe(pe, d["selneg"], d["keep"]["M"])
            turn_pe(pe, mlstm_turns(d))
            turned_all(pe, "pe")
            for h in range(5):
                for s in range(4 if h < 4 else 0):
                    n = 4 * h + s
                    if n >= 4:
                        sig["m_a"].take(pe, "pe")
                    sig["m_s"].by(pe.matmul(ps[:, n % 4, 0:512 - P * s], head(d["k"], h, P * s, P * s + P),
                                            head(d["q"], h, P * s, T2), start=True, stop=True))
                if h == 4:
                    sig["m_a"].take(pe, "pe", 4)
                for t in range(4 if h else 0):
                    n = 4 * (h - 1) + t
                    if n >= 2:
                        sig["m_read"].take(pe, "pe")
                    for s in range(t + 1):
                        a = M_AT[s] + P * (t - s)
                        mm = pe.matmul(ps[:, 4 + n % 2, 0:65], d["AT"][:, (h - 1) % 2, a:a + P], d["V"][:, s, h - 1],
                                       start=(s == 0), stop=(s == t))
                    sig["m_o"].by(mm)
            sig["m_read"].take(pe, "pe", 2)
            sig["ret_norm"].take(pe, "pe")
            yturn_pe(pe, mlstm_ys(d))

        def mlstm_act(act):
            d = mlstm_views()
            evac_units(act, None, PLAN["m_v"], T2, d["vT"])
            a = EXTRA["selneg"][0]
            act.dma_start(d["selneg"].rearrange("p h c -> p (h c)"), extra[0:4, a:a + 4 * P])\
               .then_inc(tables_landed.sem, 16)
            evac_units(act, None, PLAN["m_q"], T2, d["q"], 64 ** -0.5)
            evac_units(act, None, PLAN["m_k"], T2, d["k"])
            spread_act(act, d["NM"])
            turn_copy(act, "act", mlstm_turns(d))
            turned_all(act, "act")
            for n, (h, s) in enumerate(MP):
                sig["m_wd"].take(act, "act")
                if n >= 2:
                    sig["m_a"].take(act, "act")
                u = d["ue"][:, 4 * s + h:4 * s + h + 1]
                ins = act.activation(d["W"][:, n % 2, 0:P], d["D"][:, n % 2], ACT.Exp, bias=u)
                if s < 3:
                    ins = act.activation(d["W"][:, n % 2, P:512 - P * s], d["NM"][:, h, P * s + P:512], ACT.Exp, bias=u)
                sig["m_w"].by(ins)
            sig["m_a"].take(act, "act", 2)
            sig["m_ss"].take(act, "act")
            sig["m_std"].by(act.activation(d["ss"], d["ss"], ACT.Sqrt, bias=eps[:, 0:1], scale=1 / 64))
            yturn_act(act, mlstm_ys(d), T2)

        def mlstm_dve(v):
            d = mlstm_views()
            evac_units(None, v, PLAN["m_v"], T2, d["vT"])
            evac_units(None, v, PLAN["m_q"], T2, d["q"], 64 ** -0.5)
            evac_units(None, v, PLAN["m_k"], T2, d["k"])
            dve.by(v.memset(d["V"][:, :, :, 64:65], 1.0))
            dve.last(v)
            sig["bc_copied"].take(v, "dve")
            turn_copy(v, "dve", mlstm_turns(d))
            turned_all(v, "dve")
            for h in range(5):
                for s in range(5 if h < 4 else 0):
                    if s < 4:
                        n = 4 * h + s
                        sig["m_wd"].by(v.tensor_tensor(d["D"][:, n % 2], d["NM"][:, h, P * s:P * s + P], causalT,
                                                       ALU.add))
                    if s >= 1:
                        n, s1 = 4 * h + s - 1, s - 1
                        sig["m_w"].take(v, "dve")
                        sig["m_s"].take(v, "dve")
                        w = 512 - P * s1
                        sig["m_a"].by(v.tensor_tensor(d["AT"][:, h % 2, M_AT[s1]:M_AT[s1] + w], ps[:, n % 4, 0:w],
                                                      d["W"][:, n % 2, 0:w], ALU.mult))
                for t in range(4 if h else 0):
                    n = 4 * (h - 1) + t
                    o = ps[:, 4 + n % 2, :]
                    sig["m_o"].take(v, "dve")
                    dn, rc = d["dn"][:, n % 2:n % 2 + 1], d["rc"][:, n % 2:n % 2 + 1]
                    e = d["ue"][:, 16 + 4 * t + h - 1:17 + 4 * t + h - 1]
                    dve.by(v.tensor_scalar(dn, o[:, 64:65], -1.0, e, ALU.mult, ALU.max))
                    dve.last(v)
                    dve.by(v.tensor_tensor(dn, dn, o[:, 64:65], ALU.max))
                    dve.last(v)
                    dve.by(v.reciprocal(rc, dn))
                    dve.last(v)
                    sig["m_read"].by(v.tensor_scalar(d["H"][:, t, 64 * (h - 1):64 * h], o[:, 0:64], rc, None,
                                                     ALU.mult))
            sig["m_read"].last(v)
            Hf = d["H"].rearrange("p t (h e) -> p (t h) e", h=4)
            sqf = d["sq"].rearrange("p t (h e) -> p (t h) e", h=4)
            dve.by(v.tensor_tensor(sqf, Hf, Hf, ALU.mult))
            dve.last(v)
            sig["m_ss"].by(v.tensor_reduce(d["ss"], sqf, AX_X, ALU.add))
            sig["m_std"].take(v, "dve")
            dve.by(v.reciprocal(d["ss"], d["ss"]))
            dve.last(v)
            sig["ret_norm"].by(v.tensor_tensor(Hf, Hf, d["ss"].to_broadcast([P, 16, 64]), ALU.mult))
            yturn_dve(v, mlstm_ys(d), T2)

        def swa_views():
            cut = Cut()
            q, k = cut(4 * T2, b=4), cut(2 * T2, b=2)
            V, TB = cut(4 * P, t=4), cut(2048)
            at = cut.at
            O = cut(4 * 512, t=4)
            hank = Cut(at)(2048)
            rel, sink = cut(8, rows=33), cut(8)
            L, PT, small = cut(3 * 256, a=3), cut(2 * 256, a=2), cut(28)
            sq, rs, blockones = cut(2 * T2, a=2), cut(2 * T2, a=2), cut(P)
            onehot, vec, flip = cut(384, rows=33), cut(384, rows=8), cut(P)
            return dict(q=q, k=k, V=V, TB=TB.rearrange("p (h c) -> p h c", h=8), O=O, sink=sink, L=L, PT=PT,
                        small=small, sq=sq, rs=rs, blockones=blockones, keep=keep_views(),
                        tables=(rel, onehot, vec, hank, flip, TB))

        def swa_norms(d):
            return [(d["q"][:, b], param("sq"), True) for b in range(4)] + \
                   [(d["k"][:, b], param("sk"), False) for b in range(2)]

        def swa_turns(d):
            return [([(d["keep"]["sv"][:, P * s:P * s + P], 0)], [(P, (0, P), d["V"][:, s, :])]) for s in range(4)]

        def swa_cases(d):
            cases = []
            for t in range(4):
                for h in range(8):
                    k0 = max(t - 1, 0) * P
                    K = P * (t + 1) - k0
                    po = 64 * (h % 2)
                    cases.append(dict(
                        R=P, K=K, adds=[(0, 0, K, 0, d["TB"][:, h, 256 - K:256])], mask=None,
                        sink=d["sink"][:, h:h + 1],
                        qk=[(head(d["q"], h, P * t, P * t + P), d["k"][po:po + 64, h // 4, k0:k0 + K], 0, 0)],
                        tiles=[(P * a, P, d["V"][:, k0 // P + a, 64 * (h // 4):64 * (h // 4) + 64])
                               for a in range(K // P)],
                        out=d["O"][:, t, 64 * h:64 * h + 64]))
            return cases

        def swa_pe(pe):
            d = swa_views()
            pe_units(pe, PLAN["s_q"], T2)
            tables_product(pe, 1, d["tables"])
            pe_units(pe, PLAN["s_k"], T2)
            wait_evacuated(pe, PLAN["s_k"])
            tables_flip(pe, 1, d["tables"])
            pe.wait_ge(tables_landed.sem, TB1 + 80)
            turn_pe(pe, swa_turns(d))
            sig["tb_copied"].take(pe, "pe")
            headnorm_pe(pe, 6, d["sq"], d["blockones"])
            turned_all(pe, "pe")
            attn_pe(pe, swa_cases(d), d["L"], d["PT"])
            yturn_pe(pe, token_ys(d["O"], 4, 6))

        def swa_act(act):
            d = swa_views()
            evac_units(act, None, PLAN["s_q"], T2, d["q"], only=(0,))
            tables_load(act, 1, d["tables"])
            evac_units(act, None, PLAN["s_q"], T2, d["q"], only=(1, 2, 3))
            tables_store(act, 1, d["tables"])
            a = EXTRA["blockones"][0]
            act.dma_start(d["blockones"], extra[:, a:a + P]).then_inc(tables_landed.sem, 16)
            act.dma_start(d["sink"], bass.AP(tensor=sinks.tensor, offset=0, ap=[[0, P], [1, 8]]))\
               .then_inc(tables_landed.sem, 16)
            evac_units(act, None, PLAN["s_k"], T2, d["k"])
            tables_reload(act, 1, d["tables"])
            tables_copy(act, d["tables"])
            turn_copy(act, "act", swa_turns(d))
            wait_evacuated(act, PLAN["s_k"])
            headnorm_act(act, swa_norms(d), d["sq"], d["rs"])
            act.wait_ge(tables_landed.sem, TB1 + 80)
            attn_act(act, swa_cases(d), d["L"], d["PT"], d["small"])
            yturn_act(act, token_ys(d["O"], 4, 6), T2)

        def swa_dve(v):
            d = swa_views()
            evac_units(None, v, PLAN["s_q"], T2, d["q"])
            tables_dve(v, d["tables"])
            evac_units(None, v, PLAN["s_k"], T2, d["k"])
            sig["tb_copied"].take(v, "dve")
            turn_copy(v, "dve", swa_turns(d))
            headnorm_dve(v, swa_norms(d), d["rs"])
            v.wait_ge(tables_landed.sem, TB1 + 80)
            attn_dve(v, swa_cases(d), d["L"], d["PT"], d["small"])
            yturn_dve(v, token_ys(d["O"], 4, 6), T2)

        def merge_views():
            cut = Cut()
            G, t, MG = cut(8 * T2, b=8), cut(3 * T2, a=3), cut(2 * T2, b=2)
            split = Cut(cut.at, arena_r)
            return G, MG, t, (split(8 * T2, b=8), split(8 * T2, b=8))

        def merge_groups(b):
            y, hsrc = (YBLK[T2](Yh), YBLK[T2](Yl)), (Hh, Hl)
            if b < 8:
                return [(0, hsrc, list(enumerate(range(KB))))]
            if b < 10:
                return [(0, y, [(0, 0), (1, 1)]), (1, y, [(2, 2), (3, 3)])]
            return [(0, y, [(0, 4), (1, 5)]), (1, y, [(2, 6), (3, 7), (4, 8), (5, 9)])]

        def merge_pe(pe):
            pe_units(pe, PLAN["merge"], T2, groups=merge_groups)
            y_ready.take(pe, "pe", 8)
            pe_units(pe, PLAN["merge_out"], T2, merge_views()[3])

        def merge_act(act):
            G, MG, _, (hi, lo) = merge_views()
            st = PLAN["merge"]
            with loop(act, st.trips, [(sig["mg_sum"].reader("act"), 2), (sig["mg_hi"].made, 2)]) as i:
                for b in range(8):
                    j, n = unit(st, b, i)
                    act.wait_ge(unit_done[j], n)
                    act.activation(G[:, b], acc(j, T2), ACT.Sigmoid).then_inc(acc_free[j], 1)
                for mm in range(2):
                    sig["mg_sum"].take(act, "act")
                    sig["mg_hi"].by(act.activation(hi[:, bass.ds(i * 2 + mm, 1), :].rearrange("p a n -> p (a n)"),
                                                   MG[:, mm], ACT.Copy))

        def merge_dve(v):
            G, MG, t, (hi, lo) = merge_views()
            st = PLAN["merge"]
            with loop(v, st.trips, [(dve.made, 8), (sig["mg_sum"].made, 2), (sig["mg_hi"].reader("dve"), 2),
                                     (y_ready.made, 2)]) as i:
                for mm in range(2):
                    for a, (b, bank) in enumerate(((8 + mm, 0), (8 + mm, 1), (10 + mm, 0), (10 + mm, 1))):
                        j, n = unit(st, b, i)
                        jg, ng = unit(st, 2 * a + mm, i)
                        v.wait_ge(acc_free[jg], ng)
                        v.wait_ge(unit_done[j], n)
                        ins = v.tensor_tensor(t[:, min(a, 1)], ps[:, 2 * j + bank, :], G[:, 2 * a + mm], ALU.mult)
                        if bank:
                            ins.then_inc(acc_free[j], 1)
                            v.wait_ge(acc_free[j], n)
                        else:
                            dve.by(ins)
                            dve.last(v)
                        if a:
                            ins = v.tensor_tensor(t[:, 0] if a < 3 else MG[:, mm], t[:, 0], t[:, 1], ALU.add)
                            if a < 3:
                                dve.by(ins)
                                dve.last(v)
                            else:
                                sig["mg_sum"].by(ins)
                                sig["mg_sum"].last(v)
                for mm in range(2):
                    sig["mg_hi"].take(v, "dve")
                    hi_, lo_ = (a[:, bass.ds(i * 2 + mm, 1), :].rearrange("p a n -> p (a n)") for a in (hi, lo))
                    y_ready.by(v.tensor_tensor(lo_, MG[:, mm], hi_.bitcast(F32), ALU.subtract))
                y_ready.last(v)
            residual_squares(v, PLAN["merge_out"], T2, META)

        @block.sync
        def _(sp):
            sp.dma_start(X[:, :, :], xT.rearrange("(b p) t -> p b t", p=P)).then_inc(start_landed, 16)
            sp.dma_start(par[:, :], params).then_inc(start_landed, 16)
            sp.dma_start(cst[:, :], consts).then_inc(start_landed, 16)

            def load(n, s):
                sp.dma_start(raw[:, s].rearrange("p k c -> p (k c)"),
                             w_all[bass.ds(n, 1)].rearrange("a p c -> (a p) c")).then_inc(raw_landed[s], 16)

            load(0, 0)
            load(1, 1)
            with sp.Fori(1, LOADS // 2) as i:
                for s in range(2):
                    sp.wait_ge(split_ready[2 * s + 1], i * 1)
                    load(i * 2 + s, s)
            last = PLAN["ffn2_down2"]
            blocks = out.rearrange("(b p) t -> p b t", p=P)
            for b in range(4):
                j, n = unit(last, b)
                sp.wait_ge(acc_free[j], n)
            sp.dma_start(blocks[:, 0:4], X[:, 0:4, META:META + T2]).then_inc(out_stored, 16)
            for b in range(4):
                j, n = unit(last, b, 1)
                sp.wait_ge(acc_free[j], n)
                sp.dma_start(blocks[:, 4 + b], X[:, 4 + b, META:META + T2]).then_inc(out_stored, 16)
            sp.wait_ge(out_stored, 5 * 16)

        @block.gpsimd
        def _(pool):
            pool.memset(zero[:, :], 0.0).then_inc(pool_zero, 1)
            pool.memset(eps[:, 0:1], EPS).then_inc(pool_zero, 1)
            pool.memset(eps[:, 1:2], 64 * EPS).then_inc(pool_zero, 1)
            pool.wait_ge(pool_zero, 3)

            def split(i, s):
                pool.wait_ge(raw_landed[s], i * 16 + 16)
                for e in range(2):
                    j = 2 * s + e
                    src = raw[:, s, :, P * e:P * e + P]
                    if not (isinstance(i, int) and i == 0):
                        pool.wait_ge(unit_done[j], i * 1)
                    pool.tensor_tensor(wh[:, j], src, zero[:, 0:1].to_broadcast([P, KB, P]), ALU.add)\
                        .then_inc(hi_split, 1)
                    pool.wait_ge(hi_split, i * 4 + (j + 1))
                    pool.tensor_tensor(wl[:, j], src, wh[:, j].bitcast(F32), ALU.subtract).then_inc(split_ready[j], 1)

            split(0, 0)
            split(0, 1)
            with pool.Fori(1, UNITS // 4) as i:
                split(i, 0)
                split(i, 1)

        @block.tensor
        def _(pe):
            tables_product(pe, 0, dsa_views()["tables"])
            pe.wait_ge(start_landed, START)
            sig["v_copied"].take(pe, "pe")
            squares_alone_pe(pe, T1)
            dsa_pe(pe)
            for g in range(2):
                ret_pe(pe, g)
            pe_units(pe, PLAN["b_out"], T1, (YBLK[T1](Yh), YBLK[T1](Yl)))
            norm_pe(pe, PLAN["b_out"], T1)
            ffn_pe(pe, 0, T1)
            norm_pe(pe, PLAN["ffn0_down2"], T1)
            for g in range(2):
                stick_pe(pe, g)
            sig["oT_lo"].take(pe, "pe", 8)
            pe_units(pe, PLAN["c_out"], T1, (YBLK[T1](Yh), YBLK[T1](Yl)))
            norm_pe(pe, PLAN["c_out"], T1)
            ffn_pe(pe, 1, T1)
            norm_pe(pe, PLAN["ffn1_down2"], T1)
            squares_alone_pe(pe, T2)
            fox_pe(pe)
            conv_pe(pe)
            mlstm_pe(pe)
            swa_pe(pe)
            sig["cv_lo"].take(pe, "pe", 2)
            merge_pe(pe)
            norm_pe(pe, PLAN["merge_out"], T2)
            ffn_pe(pe, 2, T2)

        @block.scalar
        def _(act):
            tables_load(act, 0, dsa_views()["tables"])
            act.wait_ge(pool_zero, 3)
            tables_store(act, 0, dsa_views()["tables"])
            act.wait_ge(start_landed, START)
            squares_alone_act(act, T1, 0)
            tables_reload(act, 0, dsa_views()["tables"])
            norm_act(act, T1, True, root=True, alone=True)
            dsa_act(act)
            for g in range(2):
                ret_act(act, g)
            squares_act(act, T1, 0, PLAN["b_out"])
            norm_act(act, T1, True, ACT.Silu)
            ffn_act(act, 0, T1)
            squares_act(act, T1, 0, PLAN["ffn0_down2"])
            norm_act(act, T1, True)
            for g in range(2):
                stick_act(act, g)
            squares_act(act, T1, 0, PLAN["c_out"])
            norm_act(act, T1, True, ACT.Silu)
            ffn_act(act, 1, T1)
            squares_act(act, T1, 0, PLAN["ffn1_down2"])
            norm_act(act, T1, False)
            squares_alone_act(act, T2, META)
            norm_act(act, T2, True, alone=True)
            fox_act(act)
            conv_act(act)
            mlstm_act(act)
            swa_act(act)
            merge_act(act)
            squares_act(act, T2, META, PLAN["merge_out"])
            norm_act(act, T2, True, ACT.Silu)
            ffn_act(act, 2, T2)

        @block.vector
        def _(v):
            tables_dve(v, dsa_views()["tables"])
            v.wait_ge(start_landed, START)
            norm_dve(v, T1, 0, "g_mix0", True, root=True)
            dsa_dve(v)
            for g in range(2):
                ret_dve(v, g)
            residual_squares(v, PLAN["b_out"], T1, 0)
            norm_dve(v, T1, 0, "g_ffn0", True)
            ffn_dve(v, 0, T1, 0)
            norm_dve(v, T1, 0, "g_mix1", True)
            for g in range(2):
                stick_dve(v, g)
            residual_squares(v, PLAN["c_out"], T1, 0)
            norm_dve(v, T1, 0, "g_ffn1", True)
            ffn_dve(v, 1, T1, 0)
            norm_dve(v, T1, 0, "g_final", False)
            sig["stage_dve"].last(v)
            norm_dve(v, T2, META, "g_attn", True)
            fox_dve(v)
            conv_dve(v)
            mlstm_dve(v)
            swa_dve(v)
            merge_dve(v)
            norm_dve(v, T2, META, "g_ffn2", True)
            ffn_dve(v, 2, T2, META)


def bucket(n):
    n = np.maximum(n, 0)
    large = 16 + (np.log(np.maximum(n, 1).astype(np.float32) / np.float32(16)) / np.float32(np.log(8.0))
                  * np.float32(16)).astype(np.int32)
    return np.where(n < 16, n, np.minimum(large, 31))


def const_arrays():
    c = np.zeros((P, NCONST), np.float32)
    e = np.zeros((P, NEXTRA), np.float32)
    p, f = np.arange(P)[:, None], np.arange(P)[None, :]

    def put(a, table, name, v):
        at = table[name][0]
        a[:v.shape[0], at:at + v.shape[1]] = v

    put(c, CONSTS, "ident", (p == f).astype(np.float32))
    put(c, CONSTS, "ones", np.ones((P, P), np.float32))
    put(c, CONSTS, "causal", np.concatenate([np.zeros((P, 384)), np.where(f > p, NEG, 0.0)], 1))
    put(c, CONSTS, "causalT", np.where(p > f, NEG, 0.0))
    put(e, EXTRA, "flip", (p + f == P - 1).astype(np.float32))
    put(e, EXTRA, "cap", np.where(f <= p, CAP, -CAP))
    put(e, EXTRA, "blockones", (p // 64 == f // 64).astype(np.float32))
    put(e, EXTRA, "strictT", np.where(p >= f, NEG, 0.0))
    put(e, EXTRA, "strictmul", (p < f).astype(np.float32))
    put(e, EXTRA, "ntri", np.where(p >= f, -1.0, 0.0))
    put(e, EXTRA, "nones", -np.ones((P, P)))
    put(e, EXTRA, "rot", np.where(p == f + 64, -1.0, 0.0) + np.where(p + 64 == f, 1.0, 0.0))
    half = 64
    inv = (1.0 / (np.float32(10000.0) ** (np.arange(half, dtype=np.float32) / half))).astype(np.float32)
    ang = (np.arange(T1, dtype=np.float32)[:, None] * inv[None, :]).astype(np.float64).T
    put(e, EXTRA, "cos", np.concatenate([np.cos(ang)] * 2, 0))
    put(e, EXTRA, "sin", np.concatenate([np.sin(ang)] * 2, 0))
    diff = np.arange(T1)[None, :] - p
    decay = [np.where(diff >= 0, np.exp(np.maximum(diff, 0) * np.log(1.0 - 2.0 ** (-5.0 - h))), 0.0) * P ** -0.5
             for h in range(4)]
    put(e, EXTRA, "decay", np.concatenate(decay, 1))
    put(e, EXTRA, "selneg", np.concatenate([np.where(np.arange(4)[:, None] == h, -1.0, 0.0) * np.ones((4, P))
                                            for h in range(4)], 1))
    dist = 255 - np.arange(384)
    b = np.arange(32)[:, None]
    hot = (bucket(dist)[None, :] == b) & (np.arange(384) < 383)[None, :]
    put(e, EXTRA, "onehot1", hot.astype(np.float32))
    valid = ((dist >= 0) & (dist < 128))[None, :]
    put(e, EXTRA, "onehot2", np.concatenate([hot & valid, ~valid], 0).astype(np.float32))
    return c, e


def lay_weights(a):
    wide = np.zeros((UNITS, P, KB, P), np.float32)
    at = [0]

    def put(cols_):
        k = -(-cols_.shape[0] // P)
        wide[at[0], :, 0:k, 0:cols_.shape[1]] = cols_.reshape(k, P, cols_.shape[1]).transpose(1, 0, 2)
        at[0] += 1

    def many(w, c0, n):
        for m in range(n):
            put(w[:, c0 + P * m:c0 + P * m + P])

    def ffn(up, gate, down):
        for m0, n in CHUNKS:
            for i in range(n // 2):
                c = P * (m0 + 2 * i)
                many(gate, c, 2)
                many(up, c, 2)
            many(down[P * m0:P * (m0 + n)], 0, 8)

    w = a["even_w_in"][0]
    many(w, 1024, 4), many(w, 0, 4), many(w, 512, 4), many(w, 1536, 4)
    put(np.concatenate([w[:, 2048:2112]] * 2, 1)), put(w[:, 2112:2120])
    many(a["even_w_out"][0][0:512], 0, 8)
    for g in range(2):
        many(w, 2120 + 256 * g, 2), many(w, 2632 + 256 * g, 2), many(w, 3144 + 512 * g, 4), many(w, 4168 + 512 * g, 4)
    many(a["even_w_out"][0][512:], 0, 8)
    ffn(a["ffn_w_up"][0], a["ffn_w_gate"][0], a["ffn_w_down"][0])
    w = a["odd_w_in"][0]
    for g in range(2):
        many(w, 2048 + 512 * g, 4), many(w, 512 * g, 4), many(w, 1024 + 512 * g, 4)
    many(a["odd_w_out"][0], 0, 8)
    ffn(a["ffn_w_up"][1], a["ffn_w_gate"][1], a["ffn_w_down"][1])
    w = a["w_in_2"][0]
    many(w, 512, 2), many(w, 0, 2), many(w, 256, 2)
    put(w[:, 768:772]), put(w[:, 2312:2316]), put(w[:, 2308:2312])
    many(w, 2316, 2), many(w, 3212, 1)
    many(w, 772, 2), many(w, 1028, 2), many(w, 1284, 2)
    many(w, 2052, 2), many(w, 1540, 2), many(w, 1796, 2)
    many(w, 2572, 4)
    for g in range(2):
        put(np.concatenate([w[:, 3084 + 64 * g:3148 + 64 * g]] * 2, 1))
    first = np.concatenate([a["w_fox_out_2"][0], a["w_conv_out_2"][0]], 0)
    second = np.concatenate([a["w_mlstm_out_2"][0], a["w_swa_out_2"][0]], 0)
    for i in range(4):
        for b in range(4):
            many(w, 3340 + 1024 * b + 256 * i, 2)
        many(first, 256 * i, 2), many(second, 256 * i, 2)
    many(a["w_merge_out_2"][0], 0, 8)
    ffn(a["w_up_2"][0], a["w_gate_2"][0], a["w_down_2"][0])
    assert at[0] == UNITS
    wide = wide.reshape(LOADS, 2, P, KB, P).transpose(0, 2, 3, 1, 4)
    return np.ascontiguousarray(wide).reshape(LOADS, P, KB * 2 * P)


def lay_small(a):
    par = np.zeros((P, NPARAM), np.float32)

    def put(name, v):
        at = PARAMS[name][0]
        par[:v.shape[0], at:at + v.shape[1]] = v

    blocks = lambda v: v.reshape(-1, P).T
    put("g_mix0", blocks(a["norm_mix"][0])), put("g_mix1", blocks(a["norm_mix"][1]))
    put("g_ffn0", blocks(a["norm_ffn"][0])), put("g_ffn1", blocks(a["norm_ffn"][1]))
    put("g_final", blocks(a["norm_final"])), put("g_attn", blocks(a["attn_norm_2"][0]))
    put("g_ffn2", blocks(a["ffn_norm_2"][0])), put("gn", blocks(a["even_gn_gain"][0]))
    for l in range(2):
        w = np.concatenate([a["ffn_conv_w"][l], a["ffn_conv_b"][l][None]], 0)
        put(f"conv{l}", w.reshape(4, FB, P).transpose(2, 1, 0).reshape(P, 4 * FB))
    put("conv2", a["conv_w_2"][0].reshape(3, 2, P).transpose(2, 1, 0).reshape(P, 6))
    for name, src in (("fq", "fox_q_gain_2"), ("fk", "fox_k_gain_2"), ("sq", "swa_q_gain_2"), ("sk", "swa_k_gain_2")):
        put(name, np.concatenate([a[src][0]] * 2)[:, None])
    put("mh", blocks(a["mlstm_h_gain_2"][0]))
    put("fbias", a["fox_f_bias_2"][0][:, None]), put("ibias", a["mlstm_i_bias_2"][0][:, None])
    put("mfbias", a["mlstm_f_bias_2"][0][:, None])
    return par


def kernel(**inputs):
    import concourse.bacc as bacc
    from concourse.bass_utils import run_bass_kernel_spmd as run

    a = {k: np.asarray(v) for k, v in inputs.items()}
    consts, extra = const_arrays()
    arrays = {
        "xT": np.ascontiguousarray(np.concatenate([a["meta_tokens"], a["x"][0]], 0).T),
        "w_all": lay_weights(a), "params": lay_small(a), "consts": consts, "extra": extra,
        "sinks": np.ascontiguousarray(a["swa_sinks_2"]), "relb1": np.ascontiguousarray(a["rel_bias"]),
        "relb2": np.ascontiguousarray(a["rel_bias_2"]),
    }
    nc = bacc.Bacc("TRN2", target_bir_lowering=False, num_devices=1)
    h = {k: nc.dram_tensor("in_" + k, v.shape, F32, kind="ExternalInput").ap() for k, v in arrays.items()}
    scratch = nc.dram_tensor("scratch", [2, 8, 384], F32, kind="Internal").ap()
    out = nc.dram_tensor("out", [D, T2], F32, kind="ExternalOutput").ap()
    program(nc, h["xT"], h["w_all"], h["params"], h["consts"], h["extra"], h["sinks"], h["relb1"], h["relb2"], scratch,
            out)
    r = run(nc, [{"in_" + k: v for k, v in arrays.items()}], core_ids=[0]).results[0]["out"]
    return np.ascontiguousarray(r.T)[None]
```
